# Optimizing a Trainium2 kernel written in Bass

```python
import jax
import jax.numpy as jnp
from jax import lax
import numpy as np
import jax, jax.numpy as jnp

D_MODEL = 1024
BATCH = 1
SEQ = 512
DEPTH = 2

GRID_W = 64
CTX_LEN = 256
N_MIXERS = 4
MIX_CONV = 0
MIX_POOL = 1
MIX_MLA = 2
MIX_CHUNK = 3
BRANCH = D_MODEL
EPS = 1e-6
CONV_WIDTH = 31
POOL_WINDOWS = (2, 4, 8, 16)
POOL_GROUP = BRANCH // len(POOL_WINDOWS)
MLA_HEADS = D_MODEL // 128
MLA_NOPE = 128
MLA_ROPE = 64
MLA_V = 128
MLA_Q_RANK = 3 * D_MODEL // 8
MLA_KV_RANK = D_MODEL // 4
MLA_KVC = MLA_KV_RANK + MLA_ROPE
MLA_SCALE = (MLA_NOPE + MLA_ROPE) ** -0.5
ROPE_THETA = 10000.0
Q_BLOCK = 128
CHUNK = 128
CHUNK_GROUPS = 8
CHUNK_GC = BRANCH // CHUNK_GROUPS


def _n_layers_of(kind):
    return len(range(kind, DEPTH, N_MIXERS))

def _rms(x, g):
    xf = x.astype(jnp.float32)
    y = xf * lax.rsqrt(jnp.mean(xf * xf, axis=-1, keepdims=True) + EPS)
    return (y * g.astype(jnp.float32)).astype(x.dtype)

def _layernorm(x, g, b):
    xf = x.astype(jnp.float32)
    mu = jnp.mean(xf, axis=-1, keepdims=True)
    var = jnp.mean(jnp.square(xf - mu), axis=-1, keepdims=True)
    y = (xf - mu) * lax.rsqrt(var + EPS)
    return (y * g.astype(jnp.float32) + b.astype(jnp.float32)).astype(x.dtype)

def _rope_tables(rows):
    row_id = jnp.repeat(jnp.arange(rows), GRID_W).astype(jnp.float32)
    col_id = jnp.tile(jnp.arange(GRID_W), rows).astype(jnp.float32)
    axis_dim = MLA_ROPE // 2
    freqs = ROPE_THETA ** (-jnp.arange(0, axis_dim, 2, dtype=jnp.float32) / axis_dim)
    ar = row_id[:, None] * freqs
    ac = col_id[:, None] * freqs
    return (jnp.cos(ar), jnp.sin(ar), jnp.cos(ac), jnp.sin(ac))

def _rope1d(x, cos, sin):
    x1, x2 = jnp.split(x, 2, axis=-1)
    return jnp.concatenate([x1 * cos - x2 * sin, x1 * sin + x2 * cos], axis=-1)

def _rope2d(x, tabs):
    cr, sr, cc, sc = [t.astype(x.dtype) for t in tabs]
    if x.ndim == 4:
        cr, sr, cc, sc = cr[:, None], sr[:, None], cc[:, None], sc[:, None]
    xr, xc = jnp.split(x, 2, axis=-1)
    return jnp.concatenate([_rope1d(xr, cr, sr), _rope1d(xc, cc, sc)], axis=-1)

def _conv_mixer(h, w_in, dw, db, ln_g, ln_b, w_out):
    a, b, g = jnp.split(h @ w_in, 3, axis=-1)
    y = a * jax.nn.sigmoid(b)
    y = lax.conv_general_dilated(
        y, dw[:, None, :].astype(y.dtype), window_strides=(1,),
        padding=[(CONV_WIDTH // 2, CONV_WIDTH // 2)],
        dimension_numbers=('NWC', 'WIO', 'NWC'),
        feature_group_count=BRANCH) + db
    y = jax.nn.silu(_layernorm(y, ln_g, ln_b)) * jax.nn.silu(g)
    return y @ w_out

def _window_mean(v, w):
    L = v.shape[1]
    cs = jnp.pad(jnp.cumsum(v.astype(jnp.float32), axis=1), ((0, 0), (1, 0), (0, 0)))
    t = jnp.arange(L)
    start = jnp.clip(t - w // 2, 0, L)
    end = jnp.clip(t + (w - w // 2), 0, L)
    total = jnp.take(cs, end, axis=1) - jnp.take(cs, start, axis=1)
    cnt = (end - start).astype(jnp.float32)
    return (total / cnt[None, :, None]).astype(v.dtype)

def _pool_mixer(h, w_in, w_grp, scale, w_out):
    v, g = jnp.split(h @ w_in, 2, axis=-1)
    B, L, _ = v.shape
    vg = v.reshape(B, L, len(POOL_WINDOWS), POOL_GROUP)
    pooled = jnp.stack([_window_mean(vg[:, :, k], w) for k, w in enumerate(POOL_WINDOWS)], axis=2) - vg
    y = jnp.einsum('blgc,gcd->blgd', pooled, w_grp).reshape(B, L, BRANCH) * scale
    return (y * jax.nn.silu(g)) @ w_out

def _mla_keys(pkv, kv_norm, w_ukv, k_nope_g, k_rope_g, tabs):
    ckv, kr = jnp.split(pkv, [MLA_KV_RANK], axis=-1)
    B, L, _ = ckv.shape
    kv = (_rms(ckv, kv_norm) @ w_ukv).reshape(B, L, MLA_HEADS, MLA_NOPE + MLA_V)
    kn, v = jnp.split(kv, [MLA_NOPE], axis=-1)
    kn = _rms(kn, k_nope_g)
    kr = _rms(kr, k_rope_g)
    if tabs is not None:
        kr = _rope2d(kr, tabs)
    return kn, kr, v

def _mla_queries(cq, q_norm, w_uq, q_nope_g, q_rope_g, tabs):
    B, L, _ = cq.shape
    q = (_rms(cq, q_norm) @ w_uq).reshape(B, L, MLA_HEADS, MLA_NOPE + MLA_ROPE)
    qn, qr = jnp.split(q, [MLA_NOPE], axis=-1)
    qn = _rms(qn, q_nope_g)
    qr = _rms(qr, q_rope_g)
    if tabs is not None:
        qr = _rope2d(qr, tabs)
    return qn, qr

def _attend(qn, qr, kn, kr, v):
    s = (jnp.einsum('bqhd,bkhd->bhqk', qn, kn)
         + jnp.einsum('bqhr,bkr->bhqk', qr, kr)).astype(jnp.float32) * MLA_SCALE
    p = jax.nn.softmax(s, axis=-1).astype(v.dtype)
    return jnp.einsum('bhqk,bkhd->bqhd', p, v)

def _attend_blocks(qn, qr, kn, kr, v):
    B, L, H, _ = qn.shape
    nb = L // Q_BLOCK

    def blk(t):
        return jnp.moveaxis(t.reshape((B, nb, Q_BLOCK) + t.shape[2:]), 1, 0)

    out = lax.map(lambda q: _attend(q[0], q[1], kn, kr, v), (blk(qn), blk(qr)))
    return jnp.moveaxis(out, 0, 1).reshape(B, L, H * MLA_V)

def _mla_mixer(h, hc, with_ctx_out, tabs, w_in, q_norm, kv_norm, w_uq, w_ukv, nope_g, rope_g, w_out):
    pkv, cq, g = jnp.split(h @ w_in, [MLA_KVC, MLA_KVC + MLA_Q_RANK], axis=-1)
    kn, kr, v = _mla_keys(pkv, kv_norm, w_ukv, nope_g[1], rope_g[1], tabs)
    qn, qr = _mla_queries(cq, q_norm, w_uq, nope_g[0], rope_g[0], tabs)
    pc = hc @ (w_in if with_ctx_out else w_in[:, :MLA_KVC])
    knc, krc, vc = _mla_keys(pc[..., :MLA_KVC], kv_norm, w_ukv, nope_g[1], rope_g[1], None)
    o = _attend_blocks(qn, qr,
                       jnp.concatenate([kn, knc], axis=1),
                       jnp.concatenate([kr, krc], axis=1),
                       jnp.concatenate([v, vc], axis=1))
    out = (o * jax.nn.silu(g)) @ w_out
    out_c = None
    if with_ctx_out:
        cqc, gc = jnp.split(pc[..., MLA_KVC:], [MLA_Q_RANK], axis=-1)
        qnc, qrc = _mla_queries(cqc, q_norm, w_uq, nope_g[0], rope_g[0], None)
        Bc, Lc = hc.shape[0], hc.shape[1]
        oc = _attend(qnc, qrc, knc, krc, vc).reshape(Bc, Lc, MLA_HEADS * MLA_V)
        out_c = (oc * jax.nn.silu(gc)) @ w_out
    return out, out_c

def _chunk_mixer(h, w_in, ln_g, ln_b, w_s, b_s, w_out):
    u, v, g = jnp.split(h @ w_in, 3, axis=-1)
    B, L, _ = v.shape
    v = _layernorm(v, ln_g, ln_b).reshape(B, L // CHUNK, CHUNK, CHUNK_GROUPS, CHUNK_GC)
    s = jnp.einsum('gpq,bnqgc->bnpgc', w_s, v) + b_s[:, :, None]
    y = u * s.reshape(B, L, BRANCH) * jax.nn.silu(g)
    return y @ w_out

def first_inputs(seed: int = 0) -> dict:
    key = jax.random.key(seed)
    ks = iter(jax.random.split(key, 40))

    def nrm(shape, s):
        return jax.random.normal(next(ks), shape, jnp.float32) * s

    nA, nB, nC, nD = (_n_layers_of(k) for k in range(N_MIXERS))
    D, E = D_MODEL, BRANCH
    HQK = MLA_HEADS * (MLA_NOPE + MLA_ROPE)
    HKV = MLA_HEADS * (MLA_NOPE + MLA_V)
    HV = MLA_HEADS * MLA_V
    return {
        'x': nrm((BATCH, SEQ, D), 1.0),
        'c': nrm((BATCH, D), 1.0),
        'ctx': nrm((BATCH, CTX_LEN, D), 1.0),
        'c_ctx': nrm((D,), 1.0),
        'norm_g': 1.0 + nrm((DEPTH, D), 0.05),
        'w_mod': nrm((DEPTH, D, 3 * D), 0.5 * D ** -0.5),
        'b_mod': nrm((DEPTH, 3 * D), 0.01),
        'cv_w_in': nrm((nA, D, 3 * E), D ** -0.5),
        'cv_dw': nrm((nA, CONV_WIDTH, E), CONV_WIDTH ** -0.5),
        'cv_db': nrm((nA, E), 0.01),
        'cv_ln_g': 1.0 + nrm((nA, E), 0.05),
        'cv_ln_b': nrm((nA, E), 0.01),
        'cv_w_out': nrm((nA, E, D), E ** -0.5),
        'pl_w_in': nrm((nB, D, 2 * E), D ** -0.5),
        'pl_w_grp': nrm((nB, len(POOL_WINDOWS), POOL_GROUP, POOL_GROUP), POOL_GROUP ** -0.5),
        'pl_scale': 1.0 + nrm((nB, E), 0.05),
        'pl_w_out': nrm((nB, E, D), E ** -0.5),
        'ml_w_in': nrm((nC, D, MLA_KVC + MLA_Q_RANK + HV), D ** -0.5),
        'ml_q_norm': 1.0 + nrm((nC, MLA_Q_RANK), 0.05),
        'ml_kv_norm': 1.0 + nrm((nC, MLA_KV_RANK), 0.05),
        'ml_w_uq': nrm((nC, MLA_Q_RANK, HQK), MLA_Q_RANK ** -0.5),
        'ml_w_ukv': nrm((nC, MLA_KV_RANK, HKV), MLA_KV_RANK ** -0.5),
        'ml_nope_norm': 1.0 + nrm((nC, 2, MLA_NOPE), 0.05),
        'ml_rope_norm': 1.0 + nrm((nC, 2, MLA_ROPE), 0.05),
        'ml_w_out': nrm((nC, HV, D), HV ** -0.5),
        'ch_w_in': nrm((nD, D, 3 * E), D ** -0.5),
        'ch_ln_g': 1.0 + nrm((nD, E), 0.05),
        'ch_ln_b': nrm((nD, E), 0.01),
        'ch_w_s': nrm((nD, CHUNK_GROUPS, CHUNK, CHUNK), CHUNK ** -0.5),
        'ch_b_s': 1.0 + nrm((nD, CHUNK, CHUNK_GROUPS), 0.05),
        'ch_w_out': nrm((nD, E, D), E ** -0.5),
    }

def first_block(x, c, ctx, c_ctx, norm_g, w_mod, b_mod,
              cv_w_in, cv_dw, cv_db, cv_ln_g, cv_ln_b, cv_w_out,
              pl_w_in, pl_w_grp, pl_scale, pl_w_out,
              ml_w_in, ml_q_norm, ml_kv_norm, ml_w_uq, ml_w_ukv, ml_nope_norm, ml_rope_norm, ml_w_out,
              ch_w_in, ch_ln_g, ch_ln_b, ch_w_s, ch_b_s, ch_w_out):
    L = x.shape[1]
    ROWS = L // GRID_W
    tabs = _rope_tables(ROWS)
    s_lat = jax.nn.silu(c)
    s_ctx = jax.nn.silu(c_ctx)
    cx = ctx
    for i in range(DEPTH):
        kind, j = i % N_MIXERS, i // N_MIXERS
        ctx_out = any(k % N_MIXERS == MIX_MLA for k in range(i + 1, DEPTH))
        ctx_in = ctx_out or kind == MIX_MLA
        sh, sc, gt = jnp.split((s_lat @ w_mod[i] + b_mod[i])[:, None, :], 3, axis=-1)
        h = _rms(x, norm_g[i]) * (1.0 + sc) + sh
        if ctx_in:
            shc, scc, gtc = jnp.split(s_ctx @ w_mod[i] + b_mod[i], 3, axis=-1)
            hc = _rms(cx, norm_g[i]) * (1.0 + scc) + shc
        if kind == MIX_CONV:
            args = (cv_w_in[j], cv_dw[j], cv_db[j], cv_ln_g[j], cv_ln_b[j], cv_w_out[j])
            o = _conv_mixer(h, *args)
            oc = _conv_mixer(hc, *args) if ctx_out else None
        elif kind == MIX_POOL:
            args = (pl_w_in[j], pl_w_grp[j], pl_scale[j], pl_w_out[j])
            o = _pool_mixer(h, *args)
            oc = _pool_mixer(hc, *args) if ctx_out else None
        elif kind == MIX_MLA:
            o, oc = _mla_mixer(h, hc, ctx_out, tabs, ml_w_in[j], ml_q_norm[j], ml_kv_norm[j],
                               ml_w_uq[j], ml_w_ukv[j], ml_nope_norm[j], ml_rope_norm[j], ml_w_out[j])
        else:
            args = (ch_w_in[j], ch_ln_g[j], ch_ln_b[j], ch_w_s[j], ch_b_s[j], ch_w_out[j])
            o = _chunk_mixer(h, *args)
            oc = _chunk_mixer(hc, *args) if ctx_out else None
        x = x + gt * o
        if ctx_out:
            cx = cx + gtc * oc
    return x


N_MIXERS_2 = 2
FOURIER_GROUPS = 4
FOURIER_GROUP_DIM = D_MODEL // FOURIER_GROUPS
RET_HEADS = 4
RET_QK_DIM = D_MODEL // RET_HEADS
RET_V_DIM = 2 * RET_QK_DIM
RET_CHUNK = 128
ROPE_BASE = 10000.0
D_FF = -(-8 * D_MODEL // (3 * 256)) * 256


def rmsnorm(x, g):
    xf = x.astype(jnp.float32)
    y = xf * lax.rsqrt(jnp.mean(xf * xf, axis=-1, keepdims=True) + EPS)
    return (y * g.astype(jnp.float32)).astype(x.dtype)

def modulate(h, shift, scale):
    return h * (1.0 + scale[:, None, :]) + shift[:, None, :]

def fourier_mixer(h, w_o):
    B, S, D = h.shape
    hg = h.astype(jnp.float32).reshape(B, S, FOURIER_GROUPS, FOURIER_GROUP_DIM)
    f = jnp.fft.fftn(hg, axes=(1, 3), norm="ortho").real.astype(h.dtype)
    return f.reshape(B, S, D) @ w_o

def rotary(x, pos):
    half = x.shape[-1] // 2
    inv_freq = ROPE_BASE ** (-jnp.arange(half, dtype=jnp.float32) / half)
    ang = pos[:, None] * inv_freq[None, :]
    cos, sin = jnp.cos(ang), jnp.sin(ang)
    x1, x2 = x[..., :half], x[..., half:]
    return jnp.concatenate([x1 * cos - x2 * sin, x1 * sin + x2 * cos], axis=-1)

def chunk_retention(q, k, v, log_gamma, inclusive):
    B, H, S, dk = q.shape
    dv = v.shape[-1]
    C = RET_CHUNK
    N = S // C
    to_chunks = lambda a: jnp.moveaxis(a.reshape(B, H, N, C, a.shape[-1]), 2, 0)
    qc, kc, vc = to_chunks(q), to_chunks(k), to_chunks(v)

    t = jnp.arange(C)
    diff = t[:, None] - t[None, :]
    mask = (diff >= 0) if inclusive else (diff > 0)
    lg = log_gamma.astype(jnp.float32)[:, None, None]
    dmask = jnp.where(mask, jnp.exp(jnp.where(mask, diff, 0).astype(jnp.float32) * lg), 0.0)
    tf = t.astype(jnp.float32)[None, :, None]
    q_decay = jnp.exp((tf + 1.0) * lg)
    k_decay = jnp.exp((C - 1.0 - tf) * lg)
    chunk_decay = jnp.exp(C * lg)

    def step(R, xs):
        qb, kb, vb = xs
        scores = jnp.einsum('bhtd,bhsd->bhts', qb, kb) * dmask
        inner = jnp.einsum('bhts,bhsv->bhtv', scores, vb)
        cross = jnp.einsum('bhtd,bhdv->bhtv', qb, R) * q_decay
        R = R * chunk_decay + jnp.einsum('bhsd,bhsv->bhdv', kb * k_decay, vb)
        return R, inner + cross

    R0 = jnp.zeros((B, H, dk, dv), jnp.float32)
    _, out = lax.scan(step, R0, (qc, kc, vc))
    return jnp.moveaxis(out, 0, 2).reshape(B, H, S, dv)

def retention_mixer(h, w_in, w_out, log_g_fwd, log_g_bwd):
    B, S, _ = h.shape
    H, dk, dv = RET_HEADS, RET_QK_DIM, RET_V_DIM
    proj = h @ w_in
    q, k, v, g = jnp.split(proj, [H * dk, 2 * H * dk, 2 * H * dk + H * dv], axis=-1)
    heads = lambda a, d: a.astype(jnp.float32).reshape(B, S, H, d).transpose(0, 2, 1, 3)
    pos = jnp.arange(S, dtype=jnp.float32)
    q = rotary(heads(q, dk), pos)
    k = rotary(heads(k, dk), pos) * (dk ** -0.5)
    v = heads(v, dv)
    y_fwd = chunk_retention(q, k, v, log_g_fwd, True)
    flip = lambda a: jnp.flip(a, axis=2)
    y_bwd = flip(chunk_retention(flip(q), flip(k), flip(v), log_g_bwd, False))
    y = y_fwd + y_bwd
    mu = jnp.mean(y, axis=-1, keepdims=True)
    var = jnp.mean(jnp.square(y - mu), axis=-1, keepdims=True)
    y = (y - mu) * lax.rsqrt(var + EPS)
    y = y.transpose(0, 2, 1, 3).reshape(B, S, H * dv).astype(h.dtype)
    return (jax.nn.silu(g) * y) @ w_out

def swiglu(h, w_in, w_out):
    gate, up = jnp.split(h @ w_in, 2, axis=-1)
    return (jax.nn.silu(gate) * up) @ w_out

def second_inputs(seed: int = 0) -> dict:
    key = jax.random.key(seed)
    ks = jax.random.split(key, 14)
    D, F = D_MODEL, D_FF
    n_four = len(range(0, DEPTH, N_MIXERS_2))
    n_ret = len(range(1, DEPTH, N_MIXERS_2))
    ret_in_w = 2 * RET_HEADS * RET_QK_DIM + 2 * RET_HEADS * RET_V_DIM
    ret_v_w = RET_HEADS * RET_V_DIM
    nrm = lambda k, shape, s: jax.random.normal(k, shape, jnp.float32) * s
    return {
        "x": nrm(ks[0], (BATCH, SEQ, D), 1.0),
        "c": nrm(ks[1], (BATCH, D), 1.0),
        "w_ada": nrm(ks[2], (DEPTH, D, 6 * D), 0.5 * D ** -0.5),
        "b_ada": nrm(ks[3], (DEPTH, 6 * D), 0.01),
        "norm_mix_g": 1.0 + nrm(ks[4], (DEPTH, D), 0.02),
        "norm_ffn_g": 1.0 + nrm(ks[5], (DEPTH, D), 0.02),
        "w_fourier_out": nrm(ks[6], (n_four, D, D), D ** -0.5),
        "w_ret_in": nrm(ks[7], (n_ret, D, ret_in_w), D ** -0.5),
        "w_ret_out": nrm(ks[8], (n_ret, ret_v_w, D), ret_v_w ** -0.5),
        "w_ffn_in": nrm(ks[9], (DEPTH, D, 2 * F), D ** -0.5),
        "w_ffn_out": nrm(ks[10], (DEPTH, F, D), F ** -0.5),
        "final_norm_g": 1.0 + nrm(ks[11], (D,), 0.02),
        "w_ada_final": nrm(ks[12], (D, 2 * D), 0.5 * D ** -0.5),
        "b_ada_final": nrm(ks[13], (2 * D,), 0.01),
    }

def second_block(x, c, w_ada, b_ada, norm_mix_g, norm_ffn_g, w_fourier_out, w_ret_in, w_ret_out,
              w_ffn_in, w_ffn_out, final_norm_g, w_ada_final, b_ada_final):
    hidx = jnp.arange(RET_HEADS, dtype=jnp.float32)
    log_g_fwd = jnp.log1p(-jnp.exp2(-5.0 - hidx))
    log_g_bwd = jnp.flip(log_g_fwd)
    c_act = jax.nn.silu(c)
    for i in range(DEPTH):
        mod = c_act @ w_ada[i] + b_ada[i]
        sh1, sc1, g1, sh2, sc2, g2 = jnp.split(mod, 6, axis=-1)
        h = modulate(rmsnorm(x, norm_mix_g[i]), sh1, sc1)
        j = i // N_MIXERS_2
        if i % N_MIXERS_2 == 0:
            m = fourier_mixer(h, w_fourier_out[j])
        else:
            m = retention_mixer(h, w_ret_in[j], w_ret_out[j], log_g_fwd, log_g_bwd)
        x = x + g1[:, None, :] * m
        h = modulate(rmsnorm(x, norm_ffn_g[i]), sh2, sc2)
        x = x + g2[:, None, :] * swiglu(h, w_ffn_in[i], w_ffn_out[i])
    shf, scf = jnp.split(c_act @ w_ada_final + b_ada_final, 2, axis=-1)
    return modulate(rmsnorm(x, final_norm_g), shf, scf)


def setup_inputs(seed=0):
    out = dict(first_inputs(seed))
    for name, value in second_inputs(seed + 1).items():
        if name != "x":
            out[name + "_2"] = value
    return out


def reference(
    x, c, ctx, c_ctx, norm_g, w_mod, b_mod, cv_w_in, cv_dw, cv_db, cv_ln_g, cv_ln_b, cv_w_out,
    pl_w_in, pl_w_grp, pl_scale, pl_w_out, ml_w_in, ml_q_norm, ml_kv_norm, ml_w_uq, ml_w_ukv,
    ml_nope_norm, ml_rope_norm, ml_w_out, ch_w_in, ch_ln_g, ch_ln_b, ch_w_s, ch_b_s, ch_w_out,
    c_2, w_ada_2, b_ada_2, norm_mix_g_2, norm_ffn_g_2, w_fourier_out_2, w_ret_in_2, w_ret_out_2,
    w_ffn_in_2, w_ffn_out_2, final_norm_g_2, w_ada_final_2, b_ada_final_2,
):
    x = first_block(
        x, c, ctx, c_ctx, norm_g, w_mod, b_mod, cv_w_in, cv_dw, cv_db, cv_ln_g, cv_ln_b,
        cv_w_out, pl_w_in, pl_w_grp, pl_scale, pl_w_out, ml_w_in, ml_q_norm, ml_kv_norm,
        ml_w_uq, ml_w_ukv, ml_nope_norm, ml_rope_norm, ml_w_out, ch_w_in, ch_ln_g, ch_ln_b,
        ch_w_s, ch_b_s, ch_w_out,
    )
    return second_block(
        x, c_2, w_ada_2, b_ada_2, norm_mix_g_2, norm_ffn_g_2, w_fourier_out_2, w_ret_in_2,
        w_ret_out_2, w_ffn_in_2, w_ffn_out_2, final_norm_g_2, w_ada_final_2, b_ada_final_2,
    )


_drawn_inputs = setup_inputs


def setup_inputs(seed=0):
    import zlib

    import numpy as np

    out = dict(_drawn_inputs(seed))
    spreads = {}
    factors = {'norm_g': 3.66,
     'b_mod': 6.531,
     'cv_db': 8.0,
     'cv_ln_g': 8.0,
     'cv_ln_b': 24.666,
     'pl_scale': 6.11,
     'b_ada_2': 3.622,
     'norm_mix_g_2': 56.96,
     'norm_ffn_g_2': 7.585,
     'final_norm_g_2': 7.746,
     'b_ada_final_2': 4.284}
    for name, (base, spread) in spreads.items():
        noise = np.random.default_rng([zlib.crc32(name.encode()), seed]).standard_normal(out[name].shape)
        drawn = base * np.exp(spread * noise) if base else spread * noise
        out[name] = jnp.asarray(drawn.astype(out[name].dtype))
    for name, factor in factors.items():
        out[name] = (out[name] * factor).astype(out[name].dtype)
    return out
```

```python
from contextlib import ExitStack

import numpy as np

import concourse.bass as bass
from concourse import mybir

F32 = mybir.dt.float32
F32R = mybir.dt.float32r
ALU = mybir.AluOpType
ACT = mybir.ActivationFunctionType

P = 128
T = 512
D = 1024
DC = D // P
EPS = 1e-6
TAPS = 31
HALO = TAPS // 2
ROW = T + 2 * HALO
WINDOWS = (2, 4, 8, 16)
PAD = WINDOWS[-1] // 2
GROUPS = 4
GD = D // GROUPS
HEADS = 4
DK = D // HEADS
DV = 2 * DK
FF = -(-8 * D // (3 * 256)) * 256
FC = FF // P
PARTS = (8, 8, FC - 16)
SLOTS = 4
UNIT = 1024

MOD_COLS = 20 * DC
MOD_GROUPS = MOD_COLS // 4
MOD_1 = 12
V_C = 0
V_BIAS = V_C + 2 * DC
V_GAIN = V_BIAS + MOD_COLS
V_DW = V_GAIN + 7 * DC
V_DB = V_DW + TAPS * DC
V_LNG = V_DB + DC
V_LNB = V_LNG + DC
V_POOL = V_LNB + DC
V_COLS = V_POOL + DC

SHIFT = [3 * DC * n for n in range(7)]

G_START, G_AB, G_GATE, G_WAIT = 4, 4, 2, 8
W_FIRST = G_START + G_AB + G_GATE


IN_WEIGHT_RING = [g for g in (*range(G_START), *range(W_FIRST, W_FIRST + G_WAIT)) if g % 2]


def ring_count(g):
    odd = g in IN_WEIGHT_RING
    return sum((n in IN_WEIGHT_RING) == odd for n in range(g))


def ring_before(g):
    odd = g in IN_WEIGHT_RING
    return max((n + 1 for n in range(g) if (n in IN_WEIGHT_RING) == odd), default=None)


def starts(parts):
    at, found = 0, {}
    for name, n in parts:
        found[name] = at
        at += n
    return found, at


def head_order(of):
    out = []
    for h in range(HEADS):
        out += [of("qk", h), of("v", h), of("sc", h)]
        if h:
            out.append(of("ro", h - 1))
        out += [of("g", h), of("av", h)]
    return out + [of("ro", HEADS - 1)]


def both_ffn(layer, n_in, n_out):
    return [x for p, n in enumerate(PARTS)
            for x in ((f"in{layer}{p}", n_in(n)), (f"out{layer}{p}", n_out))]


U0, N_UNITS = starts(
    [("cv_ab", 16), ("cv_g", 8), ("cv_out", 8), ("pl_v", 8), ("pl_g", 8), ("pl_grp", 4), ("pl_out", 8),
     ("fr_2", 4), ("fr_out", 8)] + both_ffn(0, lambda n: 2 * n, 8)
    + head_order(lambda kind, h: (f"{kind}{h}", 0 if kind in ("sc", "av") else 4))
    + both_ffn(1, lambda n: 2 * n, 8))
R0, _ = starts(
    [("cv_ab", 16), ("cv_g", 8), ("cv_out", 8), ("pl_v", 8), ("pl_g", 8), ("pl_grp", 8), ("pl_out", 8),
     ("fr_1", 8), ("fr_2", 12), ("fr_out", 8)] + both_ffn(0, lambda n: 2 * n, 8)
    + head_order(lambda kind, h: (f"{kind}{h}", 8 if kind == "ro" else 4))
    + both_ffn(1, lambda n: 2 * n, 8))
assert all(v % SLOTS == 0 for v in (*U0.values(), *R0.values()))
UH, RH = U0["qk2"] - U0["qk1"], R0["qk2"] - R0["qk1"]

ffn_z = lambda layer: [(f"f{layer}{p}", n) for p, n in enumerate(PARTS)]
Z0, _ = starts(
    [("cv", 8), ("pv", 8), ("pg", 8), ("fr", 8)] + ffn_z(0) + [("qk0", 4), ("p0", 4)]
    + [x for h in range(1, HEADS) for x in ((f"q{h}", 2), (f"k{h}", 2), (f"y{h - 1}", 4), (f"p{h}", 4))]
    + [(f"y{HEADS - 1}", 4)] + ffn_z(1))
ZH = Z0["q2"] - Z0["q1"]
ZR0, _ = starts(
    [("cv", 8), ("pv", 8), ("fr", 4), ("qk0", 4)]
    + [x for h in range(1, HEADS) for x in ((f"q{h}", 2), (f"k{h}", 2), (f"y{h - 1}", 4))]
    + [(f"y{HEADS - 1}", 4)])
ZRH = ZR0["q2"] - ZR0["q1"]

STATS = ["n0", "cv", "n1", "n2", "n3", "n4"] + [f"h{h}" for h in range(HEADS)] + ["n5", "n6"]
ST = {name: i for i, name in enumerate(STATS)}
SS0, _ = starts([x for s in STATS for x in (
    [(s + "m", DC), (s, DC)] if s == "cv" else [(s + "m", 3), (s, 4)] if s[0] == "h" else [(s, DC)])])
SQ0, _ = starts([(s, 4 if s[0] == "h" else DC) for s in STATS])


def build_program(nc, t):
    with ExitStack() as ctx:
        sem = lambda name: ctx.enter_context(nc.semaphore(name))
        sb = lambda name, shape, dt=F32: ctx.enter_context(nc.sbuf_tensor(name, shape, dt))

        w_raw = sb("w_raw", [P, SLOTS, UNIT])
        w_hi = sb("w_hi", [P, SLOTS, UNIT], F32R)
        w_lo = sb("w_lo", [P, SLOTS, UNIT], F32R)
        x = sb("x", [P, DC, T])
        h_hi = sb("h_hi", [P, DC, T], F32R)
        h_lo = sb("h_lo", [P, DC, T], F32R)
        f_hi = sb("f_hi", [P, 8, T], F32R)
        f_lo = sb("f_lo", [P, 8, T], F32R)
        sq = sb("sq", [P, T])
        ssum = sb("ssum", [P, T])
        diag = sb("diag", [P, T])
        mrow = sb("mrow", [P, T])
        ident = sb("ident", [P, P])
        ones = sb("ones", [P, P])
        vec = sb("vec", [P, V_COLS])
        c_pad = sb("c_pad", [P, 2 * DC, 32])
        mraw = sb("mraw", [P, MOD_COLS])
        mod = sb("mod", [P, MOD_COLS])
        aff = sb("aff", [P, DC])
        stdev = sb("stdev", [P, 4])
        rstd = sb("rstd", [P, 4])
        eps = sb("eps", [P, 1])
        spare = sb("spare", [P, 1])
        sign = sb("sign", [P, 2])

        def phase(*parts):
            with ExitStack() as s:
                return [s.enter_context(nc.sbuf_tensor(n, shape, dt)) for n, shape, dt in parts]

        mods_ring, = phase(("mods_ring", [P, SLOTS, UNIT], F32))
        _, cv_y, cv_acc, cv_g = phase(
            ("under_cv", [P, SLOTS * UNIT], F32), ("cv_y", [P, DC * ROW], F32),
            ("cv_acc", [P, DC, T], F32), ("cv_g", [P, DC, T], F32))
        _, m_buf, z_buf, s_buf, pl_v, pl_s, pl_cnt, pl_g = phase(
            ("under_pl", [P, SLOTS * UNIT], F32),
            ("m_buf", [P, 2, T], F32), ("z_buf", [P, 2, T], F32), ("s_buf", [P, 2, T], F32),
            ("pl_v", [P, 2, T + 2 * PAD], F32), ("pl_s", [P, 2, T + 2 * PAD], F32),
            ("pl_cnt", [P, len(WINDOWS), T], F32), ("pl_g", [P, DC, T], F32))
        fr_raw = s_buf[:, 1, :].rearrange("p (k n) -> p k n", k=2)
        _, _, fr_hi, fr_lo, ab_hi, ab_lo = phase(
            ("under_fr", [P, SLOTS * UNIT], F32), ("beside_fr", [P, 6 * T], F32),
            ("fr_hi", [P, 2, GD], F32R), ("fr_lo", [P, 2, GD], F32R),
            ("ab_hi", [P, 4, D], F32R), ("ab_lo", [P, 4, D], F32R))
        yh, sg, _, rot, mask, qk_hi, qk_lo, v_hi, v_lo = phase(
            ("yh", [P, 4, T], F32), ("sg", [P, 4, T], F32), ("beside_ret", [P, 4 * T], F32),
            ("rot", [P, 2, T], F32), ("mask", [P, T + 3 * P], F32),
            ("qk_hi", [P, 4, T], F32R), ("qk_lo", [P, 4, T], F32R),
            ("v_hi", [P, 4, DV], F32R), ("v_lo", [P, 4, DV], F32R))

        ps = lambda name: ctx.enter_context(nc.psum_tensor(name, [P, T], F32))
        bank = [ps(f"bank{b}") for b in range(SLOTS)]
        ps_stat, ps_bc, ps_mcol, ps_mrow = ps("ps_stat"), ps("ps_bc"), ps("ps_mcol"), ps("ps_mrow")

        raw_in = [sem(f"raw_in{s}") for s in range(SLOTS)]
        mods_in = [[sem(f"mods_in{s}") for s in range(SLOTS)], [sem(f"mods_in_w{s}") for s in range(SLOTS)]]
        vec_in, x_in, cnt_in, fr_in, rot_in, mask_in, y_out = (
            sem(n) for n in ("vec_in", "x_in", "cnt_in", "fr_in", "rot_in", "mask_in", "y_out"))
        hi_done = sem("hi_done")
        lo_done = sem("lo_done")
        unit_used = sem("unit_used")
        tile_done = sem("tile_done")
        left = [sem(f"left_bank{b}") for b in range(SLOTS)]
        zeroed, const_ready, c_ready = sem("zeroed"), sem("const_ready"), sem("c_ready")
        mrow_done, mrow_copied = sem("mrow_done"), sem("mrow_copied")
        mcol_done, mcol_copied = sem("mcol_done"), sem("mcol_copied")
        mod_step = sem("mod_step")
        sq_ready, sum_step = sem("sq_ready"), sem("sum_step")
        stat_done, std_ready, rstd_ready, diag_ready, bc_done, mean_done, centered, scaled = (
            sem(n) for n in ("stat_done", "std_ready", "rstd_ready", "diag_ready", "bc_done", "mean_done",
                             "centered", "scaled"))
        m_ready, hh_ready, hl_ready = sem("m_ready"), sem("hh_ready"), sem("hl_ready")
        z_ready, zh_ready, zl_ready = sem("z_ready"), sem("zh_ready"), sem("zl_ready")
        halo_ready, y_ready, tap_done, ln_silu = sem("halo_ready"), sem("y_ready"), sem("tap_done"), sem("ln_silu")
        win_step, fr_const, fr_const_lo, ab_ready, vh_ready, rot_step = (
            sem(n) for n in ("win_step", "fr_const", "fr_const_lo", "ab_ready", "vh_ready", "rot_step"))
        out_ready = sem("out_ready")

        def wait_unit(eng, name, n, i=0, per=SLOTS):
            eng.wait_ge(unit_used, per * i + (U0[name] + n + 1))

        def wait_left(eng, name, n, i=0, per=SLOTS):
            eng.wait_ge(left[n % SLOTS], (per // SLOTS) * i + ((R0[name] + n) // SLOTS + 1))

        def at(buf, i):
            return buf[:, i, :] if isinstance(i, int) else buf[:, bass.ds(i, 1), :].rearrange("p a n -> p (a n)")

        block = ctx.enter_context(nc.Block())

        @block.sync
        def _(sp):
            def four(name, a, first, width=UNIT, i=0, per_u=SLOTS, per_a=SLOTS, fresh=False):
                for s in range(SLOTS):
                    if not fresh:
                        sp.wait_ge(lo_done, per_u * i + (U0[name] + s + 1 - SLOTS))
                    src = a[bass.ds(per_a * i + (first + s), 1)].rearrange("a p n -> p (a n)")
                    sp.dma_start(w_raw[:, s, 0:width], src).then_inc(raw_in[s], 16)

            def later(name, n):
                U0[f"{name}+{n}"] = U0[name] + SLOTS * n
                return f"{name}+{n}"

            def mods(g, i=0, per=1):
                odd = g in IN_WEIGHT_RING
                before = ring_before(g)
                if before:
                    sp.wait_ge(mrow_done, per * i + before)
                for s in range(SLOTS):
                    src = t["w_mods"][bass.ds(SLOTS * per * i + (SLOTS * g + s), 1)].rearrange("a p n -> p (a n)")
                    sp.dma_start((w_raw if odd else mods_ring)[:, s, :], src).then_inc(mods_in[odd][s], 16)

            sp.dma_start(vec[:], t["vectors"]).then_inc(vec_in, 16)
            mods(0)
            sp.dma_start(x[:], t["x_t"]).then_inc(x_in, 16)
            for g in range(1, G_START):
                mods(g)
            g = G_START
            sp.wait_ge(mrow_done, G_START)
            four("cv_ab", t["cv_ab"], 0, fresh=True)
            mods(g)
            with sp.Fori(1, 4) as i:
                four("cv_ab", t["cv_ab"], 0, i=i)
                mods(g + 1, i - 1)
            g += G_AB
            for b in range(2):
                four(later("cv_g", b), t["cv_g"], SLOTS * b)
                mods(g + b)
            g += G_GATE
            mods(g)
            sp.wait_ge(lo_done, U0["cv_out"])
            mods(g + 1)
            with sp.Fori(0, G_WAIT // 2 - 1) as i:
                mods(g + 2, i, 2)
                mods(g + 3, i, 2)
            g += G_WAIT
            sp.wait_ge(mrow_done, g)
            for b in range(2):
                four(later("cv_out", b), t["cv_out"], SLOTS * b, fresh=b == 0)
                mods(g + b)
            g += 2
            for name in ("pl_v", "pl_g"):
                for b in range(2):
                    four(later(name, b), t[name], SLOTS * b)
                    if (name, b) == ("pl_v", 0):
                        sp.wait_ge(zl_ready, Z0["cv"] + DC)
                        sp.dma_start(pl_cnt[:], t["pl_cnt"]).then_inc(cnt_in, 16)
                        sp.dma_start(fr_raw, t["dft_feature"]).then_inc(fr_in, 16)
                    mods(g + b)
                g += 2
            four("pl_grp", t["pl_grp"], 0, width=2 * GD)
            for b in range(2):
                four(later("pl_out", b), t["pl_out"], SLOTS * b)
                mods(g + b)
            g += 2
            four("fr_2", t["dft_token"], 0)
            mods(g)
            g += 1
            for b in range(2):
                four(later("fr_out", b), t["fr_out"], SLOTS * b)
                mods(g + b)
            g += 2

            def ffn(layer, g):
                first_in = 0
                for p, n in enumerate(PARTS):
                    with sp.Fori(0, n // 2) as i:
                        four(f"in{layer}{p}", t[f"ff_in{layer}"], first_in, i=i)
                        if layer == 0:
                            mods(g, i)
                    if layer == 0:
                        g += n // 2
                    first_in += 2 * n
                    src, first_out = (t[f"ff_out{layer}"], 8 * p) if n == 8 else (t[f"ff_tail{layer}"], 0)
                    with sp.Fori(0, 2) as i:
                        four(f"out{layer}{p}", src, first_out, width=n * P, i=i)
                return g

            g = ffn(0, g)
            assert g == MOD_GROUPS, g

            def mask_load(h):
                sp.dma_start(mask[:], t["decay"][bass.ds(h, 1)].rearrange("a p n -> p (a n)")).then_inc(mask_in, 16)

            sp.wait_ge(zl_ready, Z0["f02"] + PARTS[2])
            sp.dma_start(rot[:], t["rotary"]).then_inc(rot_in, 16)
            mask_load(0)
            four("qk0", t["ret"], 0)
            four("v0", t["ret"], 4)
            four("g0", t["ret"], 8)
            with sp.Fori(0, HEADS - 1) as h:
                four("qk1", t["ret"], 16, i=h, per_u=UH, per_a=16)
                sp.wait_ge(zl_ready, ZH * h + (Z0["p0"] + 4))
                mask_load(h + 1)
                four("v1", t["ret"], 20, i=h, per_u=UH, per_a=16)
                four("ro0", t["ret"], 12, i=h, per_u=UH, per_a=16)
                four("g1", t["ret"], 24, i=h, per_u=UH, per_a=16)
            four(f"ro{HEADS - 1}", t["ret"], 16 * (HEADS - 1) + 12)
            ffn(1, g)
            for c in range(DC):
                sp.wait_ge(out_ready, c + 1)
                sp.dma_start(t["y_t"][:, c, :], x[:, c, :]).then_inc(y_out, 16)
            sp.wait_ge(y_out, 16 * DC)

        @block.gpsimd
        def _(pool):
            pool.memset(ident[:], 0.0)
            pool.memset(ones[:], 1.0)
            pool.memset(eps[:], EPS)
            pool.memset(sign[:, 0:1], -1.0)
            pool.memset(sign[:, 1:2], 1.0)
            pool.memset(c_pad[:], 0.0).then_inc(zeroed, 1)
            pool.wait_ge(zeroed, 1)
            pool.memset(sign[0:1, :], 0.0)
            pool.affine_select(out=ident[:], in_=ident[:], compare_op=ALU.not_equal, fill=1.0, base=0,
                               pattern=[[-1, P]], channel_multiplier=1).then_inc(const_ready, 1)

            def lo_part(u, s):
                pool.wait_ge(hi_done, u + 1)
                pool.tensor_tensor(w_lo[:, s, :], w_raw[:, s, :], w_hi[:, s, :].bitcast(F32),
                                   ALU.subtract).then_inc(lo_done, 1)

            for u in range(SLOTS):
                lo_part(u, u)
            pool.wait_ge(hl_ready, DC)
            rows = cv_y[:].rearrange("p (c n) -> p c n", c=DC)
            pool.memset(rows[:, :, 0:HALO], 0.0)
            pool.memset(rows[:, :, HALO + T:ROW], 0.0).then_inc(halo_ready, 1)
            with pool.Fori(0, 4) as i:
                for q in range(2):
                    if q:
                        lo_part(SLOTS * i + 5, 1)
                    lo_part(SLOTS * i + (4 + 2 * q), 2 * q)
                    wait_left(pool, "cv_ab", 2 * q, i)
                    wait_left(pool, "cv_ab", 2 * q + 1, i)
                    pool.tensor_tensor(cv_y[:, bass.ds((2 * i + q) * ROW + HALO, T)], cv_g[:, 2 * q, :],
                                       cv_g[:, 2 * q + 1, :], ALU.mult).then_inc(y_ready, 1)
                lo_part(SLOTS * i + 7, 3)
            first = U0["cv_g"] + SLOTS
            with pool.Fori(0, (N_UNITS - first) // SLOTS) as i:
                for s in range(SLOTS):
                    lo_part(SLOTS * i + (first + s), s)

        @block.scalar
        def _(act):
            def refill(name, s, i=0, per=SLOTS):
                u = U0[name] + s + SLOTS
                if u >= N_UNITS:
                    return
                act.wait_ge(raw_in[u % SLOTS], 16 * (per // SLOTS) * i + 16 * (u // SLOTS + 1))
                act.wait_ge(unit_used, per * i + (u + 1 - SLOTS))
                act.activation(w_hi[:, u % SLOTS, :], w_raw[:, u % SLOTS, :], ACT.Copy).then_inc(hi_done, 1)

            def mods(g):
                mcol(g - 1)
                act.wait_ge(mrow_done, g + 1)
                act.activation(mrow[:], ps_mrow[:], ACT.Copy).then_inc(mrow_copied, 1)

            def mcol(g):
                act.wait_ge(mcol_done, g + 1)
                if isinstance(g, int):
                    dst = mraw[:, 4 * g:4 * g + 4]
                else:
                    act.wait_ge(const_ready, 1)
                    dst = mraw[:, bass.ds(4 * g, 4)]
                act.activation(dst, ps_mcol[:, 0:4], ACT.Copy).then_inc(mcol_copied, 1)

            def square(stat, c, src, i=0, per=0):
                if SS0[stat] + c:
                    act.wait_ge(sum_step, per * i + (SS0[stat] + c))
                act.activation(sq[:], src, ACT.Square).then_inc(sq_ready, 1)

            def std(stat, n):
                act.wait_ge(stat_done, stat + 1)
                act.wait_ge(const_ready, 1)
                act.activation(stdev[:], ps_stat[:, 0:4], ACT.Sqrt, bias=eps[:], scale=1.0 / n).then_inc(std_ready, 1)

            def norm(n):
                for c in range(DC):
                    act.wait_ge(m_ready, DC * n + c + 1)
                    act.activation(h_hi[:, c, :], m_buf[:, c % 2, :], ACT.Identity,
                                   bias=mod[:, SHIFT[n] + c:SHIFT[n] + c + 1]).then_inc(hh_ready, 1)

            def hi(dst, q):
                act.activation(dst, z_buf[:, q, :], ACT.Copy).then_inc(zh_ready, 1)

            def out(name, stat, g=None, last_mcol=None):
                for j in range(DC):
                    if stat is not None:
                        if j == 0:
                            act.activation(spare[:], eps[:], ACT.Sqrt)
                        wait_left(act, name, j)
                        square(stat, j, x[:, j, :])
                    refill(name, j)
                    if last_mcol is not None and j == SLOTS - 1:
                        mcol(last_mcol)
                    if g is not None and j % SLOTS == SLOTS - 1:
                        mods(g)
                        g += 1
                return g

            act.wait_ge(const_ready, 1)
            act.wait_ge(vec_in, 16)
            act.activation(c_pad[:, :, 0], vec[:, V_C:V_C + 2 * DC], ACT.Silu).then_inc(c_ready, 1)
            act.wait_ge(x_in, 16)
            for c in range(DC):
                square("n0", c, x[:, c, :])
            act.wait_ge(mrow_done, 1)
            act.activation(mrow[:], ps_mrow[:], ACT.Copy).then_inc(mrow_copied, 1)
            for g in range(1, G_START):
                mods(g)
            mcol(G_START - 1)
            std(0, D)
            for u in range(SLOTS):
                act.wait_ge(raw_in[u], 16)
                act.activation(w_hi[:, u, :], w_raw[:, u, :], ACT.Copy).then_inc(hi_done, 1)
            norm(0)

            def ab(i):
                for q in range(2):
                    wait_unit(act, "cv_ab", 2 * q, i)
                    if not isinstance(i, int):
                        act.wait_ge(y_ready, 2 * i + (q - 1))
                    act.activation(cv_g[:, 2 * q, :], bank[2 * q][:], ACT.Copy).then_inc(left[2 * q], 1)
                    refill("cv_ab", 2 * q, i)
                    wait_unit(act, "cv_ab", 2 * q + 1, i)
                    act.activation(cv_g[:, 2 * q + 1, :], bank[2 * q + 1][:], ACT.Sigmoid).then_inc(left[2 * q + 1], 1)
                    refill("cv_ab", 2 * q + 1, i)

            g = G_START
            ab(0)
            act.wait_ge(mrow_done, g + 1)
            act.activation(mrow[:], ps_mrow[:], ACT.Copy).then_inc(mrow_copied, 1)
            with act.Fori(1, 4) as i:
                ab(i)
                mods(i + g)
            g += G_AB
            act.wait_ge(y_ready, DC)
            for j in range(DC):
                wait_unit(act, "cv_g", j)
                act.activation(cv_g[:, j, :], bank[j % SLOTS][:], ACT.Silu).then_inc(left[j % SLOTS], 1)
                if j < SLOTS:
                    refill("cv_g", j)
                if j % SLOTS == SLOTS - 1:
                    mods(g)
                    g += 1
            with act.Fori(g, g + G_WAIT) as i:
                mods(i)
            g += G_WAIT
            for j in range(SLOTS, DC):
                refill("cv_g", j)
            for c in range(DC):
                act.wait_ge(centered, c + 1)
                square("cv", c, cv_acc[:, c, :])
            std(ST["cv"], D)
            for c in range(DC + 1):
                if c < DC:
                    act.wait_ge(scaled, c + 1)
                    act.activation(cv_acc[:, c, :], cv_acc[:, c, :], ACT.Silu, bias=vec[:, V_LNB + c:V_LNB + c + 1],
                                   scale=vec[:, V_LNG + c:V_LNG + c + 1]).then_inc(ln_silu, 1)
                if c:
                    act.wait_ge(z_ready, ZR0["cv"] + c)
                    hi(f_hi[:, c - 1, :], (c - 1) % 2)
            g = out("cv_out", "n1", g)
            std(ST["n1"], D)
            norm(1)

            for j in range(DC):
                wait_unit(act, "pl_v", j)
                if j < 2:
                    act.wait_ge(win_step, 1)
                else:
                    act.wait_ge(z_ready, ZR0["pv"] + j - 1)
                act.activation(pl_v[:, j % 2, PAD:PAD + T], bank[j % SLOTS][:], ACT.Copy).then_inc(left[j % SLOTS], 1)
                refill("pl_v", j)
                act.wait_ge(z_ready, ZR0["pv"] + j + 1)
                hi(f_hi[:, j, :], j % 2)
                if j % SLOTS == SLOTS - 1:
                    mods(g)
                    g += 1
            for j in range(DC):
                wait_unit(act, "pl_g", j)
                act.activation(pl_g[:, j, :], bank[j % SLOTS][:], ACT.Silu).then_inc(left[j % SLOTS], 1)
                refill("pl_g", j)
                if j % SLOTS == SLOTS - 1:
                    mods(g)
                    g += 1
            for j in range(DC):
                wait_left(act, "pl_grp", j)
                hi(h_hi[:, j, :], j % 2)
                if j % 2:
                    refill("pl_grp", j // 2)
            g = out("pl_out", "n2", g)
            act.wait_ge(fr_in, 16)
            act.activation(fr_hi[:], fr_raw, ACT.Copy).then_inc(fr_const, 1)
            std(ST["n2"], D)
            norm(2)

            for n in range(8):
                act.wait_ge(tile_done, n + 1)
                act.activation(ab_hi[:, n // 2, (n % 2) * T:(n % 2 + 1) * T], bank[n % SLOTS][:],
                               ACT.Copy).then_inc(ab_ready, 1)
            mods(g)
            g += 1
            for k in range(GROUPS):
                act.wait_ge(tile_done, 8 + 3 * k + 1)
                if k:
                    wait_left(act, "fr_2", 3 * k - 2)
                else:
                    act.wait_ge(fr_const_lo, 1)
                act.activation(s_buf[:, 0, :], bank[3 * k % SLOTS][:], ACT.Copy).then_inc(left[3 * k % SLOTS], 1)
                act.wait_ge(z_ready, ZR0["fr"] + k + 1)
                hi(f_hi[:, 2 * k, :], 0)
                wait_left(act, "fr_2", 3 * k + 2)
                hi(f_hi[:, 2 * k + 1, :], 1)
            for s in range(SLOTS):
                refill("fr_2", s)
            g = out("fr_out", "n3", g)
            std(ST["n3"], D)
            norm(3)

            def ffn(layer, g, stat):
                for p, n in enumerate(PARTS):
                    name = f"in{layer}{p}"
                    with_mods = layer == 0
                    with act.Fori(0, n // 2) as i:
                        for q in range(2):
                            wait_unit(act, name, 2 * q, i)
                            act.wait_ge(left[2 * q + 1], i + R0[name] // SLOTS)
                            act.activation(s_buf[:, q, :], bank[2 * q][:], ACT.Silu).then_inc(left[2 * q], 1)
                            refill(name, 2 * q, i)
                            wait_left(act, name, 2 * q + 1, i)
                            act.wait_ge(const_ready, 1)
                            hi(at(f_hi, 2 * i + q), q)
                            refill(name, 2 * q + 1, i)
                        if with_mods:
                            mods(i + g)
                    if with_mods:
                        g += n // 2
                    out(f"out{layer}{p}", stat if p == len(PARTS) - 1 else None,
                        last_mcol=MOD_GROUPS - 1 if layer == 0 and p == 2 else None)
                return g

            ffn(0, g, "n4")
            std(ST["n4"], D)
            norm(4)

            def head_rest(h, n, first):
                for s in range(0 if first else 2, 3):
                    refill(f"v{n}", s, h, UH)
                wait_unit(act, f"v{n}", 3, h, UH)
                for j in range(4):
                    act.activation(v_hi[:, j, :], bank[j][:], ACT.Copy).then_inc(vh_ready, 1)
                refill(f"v{n}", 3, h, UH)
                for j in range(4):
                    wait_left(act, f"sc{n}", j, h, RH)
                    hi(f_hi[:, 4 + j, :], j % 2)
                if not first:
                    for s in range(SLOTS):
                        refill(f"ro{n - 1}", s, h, UH)
                for s in range(SLOTS):
                    wait_unit(act, f"g{n}", s, h, UH)
                    act.activation(sg[:, s, :], bank[s][:], ACT.Silu).then_inc(left[s], 1)
                    refill(f"g{n}", s, h, UH)
                for j in range(4):
                    act.wait_ge(tile_done, 8 * h + (TD_HEAD + 8 * n + 4 + j + 1))
                    act.activation(yh[:, j, :], bank[j][:], ACT.Copy).then_inc(left[j], 1)

            def head_squares(h):
                for j in range(4):
                    act.wait_ge(centered, 4 * h + (DC + j + 1))
                    square("h0", j, yh[:, j, :], h, SS0["h1"] - SS0["h0"])

            for s in range(SLOTS):
                refill("qk0", s)
            for j in range(4):
                act.wait_ge(z_ready, ZR0["qk0"] + j + 1)
                hi(qk_hi[:, j, :], j % 2)
            head_rest(0, 0, True)
            with act.Fori(0, HEADS - 1) as h:
                for half in range(2):
                    for s in (2 * half, 2 * half + 1):
                        refill("qk1", s, h, UH)
                    for j in range(2):
                        act.wait_ge(z_ready, ZRH * h + (ZR0["qk"[half] + "1"] + j + 1))
                        hi(qk_hi[:, 2 * half + j, :], j)
                    if half == 0:
                        head_squares(h)
                std(h + ST["h0"], DV)
                refill("v1", 0, h, UH)
                refill("v1", 1, h, UH)
                for j in range(4):
                    act.wait_ge(z_ready, ZRH * h + (ZR0["y0"] + j + 1))
                    hi(f_hi[:, j, :], j % 2)
                head_rest(h, 1, False)
            head_squares(HEADS - 1)
            std(ST[f"h{HEADS - 1}"], DV)
            last = f"y{HEADS - 1}"
            for j in range(4):
                act.wait_ge(z_ready, ZR0[last] + j + 1)
                hi(f_hi[:, j, :], j % 2)
            name = f"ro{HEADS - 1}"
            for j in range(DC):
                wait_left(act, name, j)
                square("n5", j, x[:, j, :])
                if j % 2:
                    refill(name, j // 2)
            std(ST["n5"], D)
            norm(5)
            ffn(1, None, "n6")
            std(ST["n6"], D)
            for c in range(DC):
                act.wait_ge(m_ready, DC * 6 + c + 1)
                act.activation(x[:, c, :], m_buf[:, c % 2, :], ACT.Identity,
                               bias=mod[:, SHIFT[6] + c:SHIFT[6] + c + 1]).then_inc(out_ready, 1)

        @block.vector
        def _(vec_e):
            v = vec_e
            steps = {"mod": 0}

            def add_bias(a, n):
                v.wait_ge(mcol_copied, -(-(a + n) // 4))
                v.tensor_tensor(mod[:, a:a + n], mraw[:, a:a + n], vec[:, V_BIAS + a:V_BIAS + a + n],
                                ALU.add).then_inc(mod_step, 1)
                steps["mod"] += 1

            def prepare(n):
                add_bias(SHIFT[n], 2 * DC)
                v.wait_ge(mod_step, steps["mod"])
                v.scalar_tensor_tensor(aff[:], mod[:, SHIFT[n] + DC:SHIFT[n] + 2 * DC], 1.0,
                                       vec[:, V_GAIN + n * DC:V_GAIN + (n + 1) * DC], ALU.add,
                                       ALU.mult).then_inc(mod_step, 1)
                steps["mod"] += 1

            def gate(n, j):
                c = SHIFT[n] + 2 * DC + j
                return mod[:, c:c + 1]

            def add_square(stat, c, i=0, per=0, per_sq=0):
                v.wait_ge(sq_ready, per_sq * i + (SQ0[stat] + c + 1))
                if SS0[stat] + c:
                    v.wait_ge(sum_step, per * i + (SS0[stat] + c))
                if c == 0:
                    v.tensor_copy(ssum[:], sq[:]).then_inc(sum_step, 1)
                else:
                    v.tensor_tensor(ssum[:], ssum[:], sq[:], ALU.add).then_inc(sum_step, 1)

            def spread(stat):
                v.wait_ge(std_ready, stat + 1)
                v.reciprocal(rstd[:], stdev[:]).then_inc(rstd_ready, 1)
                v.wait_ge(rstd_ready, stat + 1)
                for j in range(4):
                    v.tensor_scalar(diag[:, j * P:(j + 1) * P], ident[:], rstd[:, j:j + 1], None,
                                    ALU.mult).then_inc(diag_ready, 1)

            def norm(n, stat, lo=True):
                prepare(n)
                spread(stat)
                v.wait_ge(mod_step, steps["mod"])
                v.wait_ge(bc_done, stat + 1)
                for c in range(DC + 1):
                    if c < DC:
                        if c >= 2:
                            v.wait_ge(hl_ready if lo else out_ready, (DC * n if lo else 0) + c - 1)
                        v.scalar_tensor_tensor(m_buf[:, c % 2, :], x[:, c, :], aff[:, c:c + 1], ps_bc[:],
                                               ALU.mult, ALU.mult).then_inc(m_ready, 1)
                    if c and lo:
                        v.wait_ge(hh_ready, DC * n + c)
                        v.scalar_tensor_tensor(h_lo[:, c - 1, :], m_buf[:, (c - 1) % 2, :],
                                               mod[:, SHIFT[n] + c - 1:SHIFT[n] + c],
                                               h_hi[:, c - 1, :].bitcast(F32), ALU.add,
                                               ALU.subtract).then_inc(hl_ready, 1)

            def z_free(z, i=0, per=0):
                if not isinstance(i, int) or per * i + z >= 2:
                    v.wait_ge(zl_ready, per * i + (z - 1))

            def lo(dst, hi, z, q, i=0, per=0):
                v.wait_ge(zh_ready, per * i + (z + 1))
                v.tensor_tensor(dst, z_buf[:, q, :], hi, ALU.subtract).then_inc(zl_ready, 1)

            def out(name, n, stat, per_unit=1):
                for j in range(DC):
                    wait_unit(v, name, j // per_unit)
                    v.scalar_tensor_tensor(x[:, j, :], bank[j % SLOTS][:], gate(n, j), x[:, j, :],
                                           ALU.mult, ALU.add).then_inc(left[j % SLOTS], 1)
                    if stat is not None:
                        add_square(stat, j)

            for c in range(DC):
                add_square("n0", c)
            norm(0, 0)
            for c in range(0, DC, 2):
                v.wait_ge(y_ready, c + 2)
                done = TAPS * c
                for q in range(2):
                    v.tensor_scalar(cv_acc[:, c + q, :], cv_y[:, (c + q) * ROW:(c + q) * ROW + T],
                                    vec[:, V_DW + c + q:V_DW + c + q + 1], vec[:, V_DB + c + q:V_DB + c + q + 1],
                                    ALU.mult, ALU.add).then_inc(tap_done, 1)
                with v.Fori(1, TAPS) as k:
                    for q in range(2):
                        v.wait_ge(tap_done, 2 * k + (done + q - 1))
                        v.scalar_tensor_tensor(cv_acc[:, c + q, :], cv_y[:, bass.ds(k + (c + q) * ROW, T)],
                                               vec[:, bass.ds(DC * k + (V_DW + c + q), 1)], cv_acc[:, c + q, :],
                                               ALU.mult, ALU.add).then_inc(tap_done, 1)
                for q in range(2):
                    n = c + q
                    v.wait_ge(tap_done, done + 2 * TAPS + q - 1)
                    v.wait_ge(sum_step, SS0["cvm"] + n)
                    if n == 0:
                        v.tensor_copy(ssum[:], cv_acc[:, n, :]).then_inc(sum_step, 1)
                    else:
                        v.tensor_tensor(ssum[:], ssum[:], cv_acc[:, n, :], ALU.add).then_inc(sum_step, 1)
            add_bias(SHIFT[0] + 2 * DC, DC)
            v.wait_ge(mean_done, 1)
            for c in range(DC + 1):
                if c < DC:
                    v.scalar_tensor_tensor(cv_acc[:, c, :], ps_bc[:], -1.0 / D, cv_acc[:, c, :],
                                           ALU.mult, ALU.add).then_inc(centered, 1)
                if c:
                    add_square("cv", c - 1)
            spread(ST["cv"])
            v.wait_ge(bc_done, ST["cv"] + 1)
            for c in range(DC + 2):
                if c < DC:
                    v.tensor_tensor(cv_acc[:, c, :], cv_acc[:, c, :], ps_bc[:], ALU.mult).then_inc(scaled, 1)
                if 1 <= c <= DC:
                    n = c - 1
                    v.wait_ge(ln_silu, n + 1)
                    z_free(Z0["cv"] + n)
                    v.tensor_tensor(z_buf[:, n % 2, :], cv_acc[:, n, :], cv_g[:, n, :], ALU.mult).then_inc(z_ready, 1)
                if c >= 2:
                    n = c - 2
                    lo(f_lo[:, n, :], f_hi[:, n, :].bitcast(F32), Z0["cv"] + n, n % 2)
            v.wait_ge(mod_step, steps["mod"])
            out("cv_out", 0, "n1")
            norm(1, ST["n1"])

            v.memset(pl_v[:], 0.0).then_inc(win_step, 1)
            ws = 1
            add_bias(SHIFT[1] + 2 * DC, DC)
            v.wait_ge(cnt_in, 16)
            for j in range(DC):
                w = WINDOWS[j // 2]
                wait_left(v, "pl_v", j)
                src, span, length = pl_v[:, j % 2, :], 1, T + 2 * PAD
                while span < w:
                    length -= span
                    dst = pl_s[:, span.bit_length() % 2, :]
                    v.tensor_tensor(dst[:, 0:length], src[:, 0:length], src[:, span:span + length],
                                    ALU.add).then_inc(win_step, 1)
                    ws += 1
                    v.wait_ge(win_step, ws)
                    src, span = dst, 2 * span
                first = PAD - w // 2
                z_free(Z0["pv"] + j)
                v.tensor_tensor(z_buf[:, j % 2, :], src[:, first:first + T], pl_cnt[:, j // 2, :],
                                ALU.mult).then_inc(win_step, 1)
                ws += 1
                v.wait_ge(win_step, ws)
                v.tensor_tensor(z_buf[:, j % 2, :], z_buf[:, j % 2, :], pl_v[:, j % 2, PAD:PAD + T],
                                ALU.subtract).then_inc(z_ready, 1)
                lo(f_lo[:, j, :], f_hi[:, j, :].bitcast(F32), Z0["pv"] + j, j % 2)
            for j in range(DC):
                wait_unit(v, "pl_grp", j // 2)
                wait_left(v, "pl_g", j)
                z_free(Z0["pg"] + j)
                v.scalar_tensor_tensor(z_buf[:, j % 2, :], bank[j % SLOTS][:], vec[:, V_POOL + j:V_POOL + j + 1],
                                       pl_g[:, j, :], ALU.mult, ALU.mult).then_inc(left[j % SLOTS], 1)
                lo(h_lo[:, j, :], h_hi[:, j, :].bitcast(F32), Z0["pg"] + j, j % 2)
            v.wait_ge(mod_step, steps["mod"])
            out("pl_out", 1, "n2")
            v.wait_ge(fr_const, 1)
            v.tensor_tensor(fr_lo[:], fr_raw, fr_hi[:].bitcast(F32), ALU.subtract).then_inc(fr_const_lo, 1)
            norm(2, ST["n2"])

            add_bias(SHIFT[2] + 2 * DC, DC)
            for n in range(8):
                part = slice((n % 2) * T, (n % 2 + 1) * T)
                v.wait_ge(ab_ready, n + 1)
                v.tensor_tensor(ab_lo[:, n // 2, part], bank[n % SLOTS][:], ab_hi[:, n // 2, part].bitcast(F32),
                                ALU.subtract).then_inc(left[n % SLOTS], 1)
            for k in range(GROUPS):
                v.wait_ge(tile_done, 8 + 3 * k + 2)
                wait_left(v, "fr_2", 3 * k)
                bv, bn = (3 * k + 1) % SLOTS, (3 * k + 2) % SLOTS
                z_free(Z0["fr"] + 2 * k)
                v.scalar_tensor_tensor(z_buf[:, 0, :], bank[bv][:], sign[:, 0:1], s_buf[:, 0, :], ALU.mult,
                                       ALU.add).then_inc(z_ready, 1)
                z_free(Z0["fr"] + 2 * k + 1)
                v.scalar_tensor_tensor(z_buf[:, 1, :], bank[bv][:], sign[:, 1:2], s_buf[:, 0, :], ALU.mult,
                                       ALU.add).then_inc(left[bv], 1)
                wait_left(v, "fr_2", 3 * k + 1)
                if k < GROUPS - 1:
                    v.wait_ge(tile_done, 8 + 3 * k + 3)
                else:
                    wait_unit(v, "fr_2", 3)
                v.tensor_copy(z_buf[0:1, 1, :], bank[bn][0:1, :]).then_inc(left[bn], 1)
                for q in range(2):
                    lo(f_lo[:, 2 * k + q, :], f_hi[:, 2 * k + q, :].bitcast(F32), Z0["fr"] + 2 * k + q, q)
            v.wait_ge(mod_step, steps["mod"])
            out("fr_out", 2, "n3")
            norm(3, ST["n3"])

            def ffn(layer, n, stat):
                for p, chunks in enumerate(PARTS):
                    name, z0 = f"in{layer}{p}", Z0[f"f{layer}{p}"]
                    with v.Fori(0, chunks // 2) as i:
                        for q in range(2):
                            wait_unit(v, name, 2 * q + 1, i)
                            wait_left(v, name, 2 * q, i)
                            z_free(z0 + q, i, 2)
                            v.tensor_tensor(z_buf[:, q, :], bank[2 * q + 1][:], s_buf[:, q, :],
                                            ALU.mult).then_inc(left[2 * q + 1], 1)
                            lo(at(f_lo, 2 * i + q), at(f_hi, 2 * i + q).bitcast(F32), z0 + q, q, i, 2)
                    if p == 0:
                        add_bias(SHIFT[n] + 2 * DC, DC)
                        v.wait_ge(mod_step, steps["mod"])
                    out(f"out{layer}{p}", n, stat if p == len(PARTS) - 1 else None)

            ffn(0, 3, "n4")
            norm(4, ST["n4"])
            add_bias(SHIFT[4] + 2 * DC, DC)

            SSH = SS0["h1"] - SS0["h0"]
            rot_count = {"n": 0}

            def rotary(half, h, n):
                b0, b1 = bank[2 * half], bank[2 * half + 1]
                z0 = Z0["qk0"] + 2 * half if n == 0 else Z0["qk"[half] + "1"]
                zr = ZR0["qk0"] + 2 * half if n == 0 else ZR0["qk"[half] + "1"]
                steps0 = 2 * half + 4 * n
                wait_unit(v, f"qk{n}", 2 * half + 1, h, UH)
                wait_left_own = lambda b: v.wait_ge(left[b], (RH // SLOTS) * h + (R0[f"qk{n}"] // SLOTS + 1))
                if not (n == 0 and half == 0):
                    v.wait_ge(z_ready, ZRH * h + zr_before(n, half))
                v.tensor_tensor(m_buf[:, 0, :], b0[:], rot[:, 0, :], ALU.mult).then_inc(rot_step, 1)
                v.tensor_tensor(m_buf[:, 1, :], b1[:], rot[:, 1, :], ALU.mult).then_inc(rot_step, 1)
                v.wait_ge(rot_step, 4 * h + (steps0 + 2))
                z_free(z0, h, ZH)
                v.tensor_tensor(z_buf[:, 0, :], m_buf[:, 0, :], m_buf[:, 1, :], ALU.subtract).then_inc(z_ready, 1)
                v.wait_ge(z_ready, ZRH * h + (zr + 1))
                v.tensor_tensor(m_buf[:, 0, :], b0[:], rot[:, 1, :], ALU.mult).then_inc(left[2 * half], 1)
                v.tensor_tensor(m_buf[:, 1, :], b1[:], rot[:, 0, :], ALU.mult).then_inc(left[2 * half + 1], 1)
                wait_left_own(2 * half)
                wait_left_own(2 * half + 1)
                z_free(z0 + 1, h, ZH)
                v.tensor_tensor(z_buf[:, 1, :], m_buf[:, 0, :], m_buf[:, 1, :], ALU.add).then_inc(z_ready, 1)
                for q in range(2):
                    lo(qk_lo[:, 2 * half + q, :], qk_hi[:, 2 * half + q, :].bitcast(F32), z0 + q, q, h, ZH)

            def zr_before(n, half):
                if n == 0:
                    return ZR0["qk0"] + 2
                return ZR0["q1"] if half == 0 else ZR0["k1"]

            def head_rest(h, n):
                for j in range(4):
                    v.wait_ge(vh_ready, 4 * h + (4 * n + j + 1))
                    v.tensor_tensor(v_lo[:, j, :], bank[j][:], v_hi[:, j, :].bitcast(F32),
                                    ALU.subtract).then_inc(left[j], 1)
                v.wait_ge(mask_in, 16 * h + 16 * (n + 1))
                for j in range(4):
                    v.wait_ge(tile_done, 8 * h + (TD_HEAD + 8 * n + j + 1))
                    z_free(Z0[f"p{n}"] + j, h, ZH)
                    v.tensor_tensor(z_buf[:, j % 2, :], bank[j][:], mask[:, (3 - j) * P:(3 - j) * P + T],
                                    ALU.mult).then_inc(left[j], 1)
                    lo(f_lo[:, 4 + j, :], f_hi[:, 4 + j, :].bitcast(F32), Z0[f"p{n}"] + j, j % 2, h, ZH)
                if n:
                    for j in range(DC):
                        wait_unit(v, f"ro{n - 1}", j // 2, h, UH)
                        v.scalar_tensor_tensor(x[:, j, :], bank[j % SLOTS][:], gate(4, j), x[:, j, :],
                                               ALU.mult, ALU.add).then_inc(left[j % SLOTS], 1)

            def head_sum(h):
                ss = SS0["h0m"]
                for j in range(4):
                    wait_left(v, "av0", j, h, RH)
                v.wait_ge(sum_step, SSH * h + ss)
                v.tensor_tensor(ssum[:], yh[:, 0, :], yh[:, 1, :], ALU.add).then_inc(sum_step, 1)
                for j in (2, 3):
                    v.wait_ge(sum_step, SSH * h + (ss + j - 1))
                    v.tensor_tensor(ssum[:], ssum[:], yh[:, j, :], ALU.add).then_inc(sum_step, 1)

            def head_center(h):
                v.wait_ge(mean_done, h + 2)
                for j in range(4):
                    v.scalar_tensor_tensor(yh[:, j, :], ps_bc[:], -1.0 / DV, yh[:, j, :],
                                           ALU.mult, ALU.add).then_inc(centered, 1)
                for j in range(4):
                    add_square("h0", j, h, SSH, 4)

            def head_result(h, i, z0):
                v.wait_ge(bc_done, h + (ST["h0"] + 1))
                for j in range(4):
                    v.tensor_tensor(yh[:, j, :], yh[:, j, :], ps_bc[:], ALU.mult).then_inc(scaled, 1)
                for j in range(4):
                    v.wait_ge(scaled, 4 * h + (DC + j + 1))
                    z_free(z0 + j, i, ZH)
                    v.tensor_tensor(z_buf[:, j % 2, :], yh[:, j, :], sg[:, j, :], ALU.mult).then_inc(z_ready, 1)
                    lo(f_lo[:, j, :], f_hi[:, j, :].bitcast(F32), z0 + j, j % 2, i, ZH)

            v.wait_ge(rot_in, 16)
            rotary(0, 0, 0)
            rotary(1, 0, 0)
            v.wait_ge(mod_step, steps["mod"])
            head_rest(0, 0)
            with v.Fori(0, HEADS - 1) as h:
                head_sum(h)
                rotary(0, h, 1)
                head_center(h)
                rotary(1, h, 1)
                spread(h + ST["h0"])
                head_result(h, h, Z0["y0"])
                head_rest(h, 1)
            h = HEADS - 1
            head_sum(h)
            head_center(h)
            spread(h + ST["h0"])
            head_result(h, 0, Z0[f"y{h}"])
            out(f"ro{h}", 4, "n5", per_unit=2)
            norm(5, ST["n5"])
            ffn(1, 5, "n6")
            norm(6, ST["n6"], lo=False)

        @block.tensor
        def _(pe):
            def three(out, w_h, w_l, m_h, m_l, start, stop):
                pe.matmul(out, w_h, m_h, start=start, stop=False)
                pe.matmul(out, w_h, m_l, start=False, stop=False)
                return pe.matmul(out, w_l, m_h, start=False, stop=stop)

            def bank_ready(name, n, i=0, per=SLOTS):
                before = (R0[name] + n) // SLOTS
                if not isinstance(i, int) or before:
                    pe.wait_ge(left[n % SLOTS], (per // SLOTS) * i + before)

            def unit_ready(name, n, i=0, per=SLOTS):
                pe.wait_ge(lo_done, per * i + (U0[name] + n + 1))

            def tile(s, k, a_hi, a_lo, chunks, offset=0):
                w = slice((offset + k) * P, (offset + k + 1) * P)
                return three(bank[s][:], w_hi[:, s, w], w_lo[:, s, w], a_hi[:, k, :], a_lo[:, k, :],
                             k == 0, k == chunks - 1)

            def four_tiles(name, first, a_hi, a_lo, chunks=DC, i=0, ready=None, together=SLOTS):
                done = chunks // 2 if ready else 0
                for s0 in range(0, SLOTS, together):
                    for k in range(done):
                        ready(k)
                        for s in range(s0, s0 + together):
                            if k == 0:
                                unit_ready(name, first + s, i)
                                bank_ready(name, first + s, i)
                            tile(s, k, a_hi, a_lo, chunks)
                for s in range(SLOTS):
                    if not ready:
                        unit_ready(name, first + s, i)
                        bank_ready(name, first + s, i)
                    for k in range(done, chunks):
                        if ready and s == 0:
                            ready(k)
                        last = tile(s, k, a_hi, a_lo, chunks)
                    last.then_inc(unit_used, 1)

            def h_part(n):
                return lambda k: pe.wait_ge(hl_ready, DC * n + k + 1)

            def z_part(name):
                return lambda k: pe.wait_ge(zl_ready, Z0[name] + k + 1)

            def mrow_sums(g, i=0, per=1):
                odd, c0 = g in IN_WEIGHT_RING, DC if g >= MOD_1 else 0
                for s in range(SLOTS):
                    pe.wait_ge(mods_in[odd][s], 16 * i + (16 * ring_count(g) + 16))
                if g:
                    pe.wait_ge(mrow_copied, per * i + g)
                for r in range(2):
                    for q in range(4):
                        k = 4 * r + q
                        last = pe.matmul(ps_mrow[32 * q:32 * q + 32, :], c_pad[:, c0 + k, :],
                                         (w_raw if odd else mods_ring)[:, k // 2, (k % 2) * T:(k % 2 + 1) * T],
                                         start=r == 0, stop=r == 1, tile_position=(0, 32 * q))
                last.then_inc(mrow_done, 1)

            def mcol(g, i=0, per=1):
                pe.wait_ge(mrow_copied, per * i + (g + 1))
                if g:
                    pe.wait_ge(mcol_copied, per * i + g)
                for j in range(4):
                    last = pe.matmul(ps_mcol[:, j:j + 1], mrow[:, j * P:(j + 1) * P], ones[:, 0:1],
                                     start=True, stop=True)
                last.then_inc(mcol_done, 1)

            def mods(g, i=0, per=1):
                mcol(g - 1, i, per)
                mrow_sums(g, i, per)

            def stat(name, n, s=None):
                pe.wait_ge(sum_step, n)
                for j in range(4):
                    last = pe.matmul(ps_stat[:, j:j + 1], ssum[:, j * P:(j + 1) * P], ones[:, 0:1],
                                     start=True, stop=True)
                last.then_inc(stat_done, 1)

            def spread(s):
                for j in range(4):
                    pe.wait_ge(diag_ready, 4 * s + (j + 1))
                    last = pe.matmul(ps_bc[:, j * P:(j + 1) * P], ones[:], diag[:, j * P:(j + 1) * P],
                                     start=True, stop=True)
                last.then_inc(bc_done, 1)

            def mean(n):
                pe.wait_ge(sum_step, n)
                pe.matmul(ps_bc[:], ones[:], ssum[:], start=True, stop=True).then_inc(mean_done, 1)

            def out(name, a_hi, a_lo, ready, chunks=DC, g=None):
                four_tiles(name, 0, a_hi, a_lo, chunks, ready=ready)
                if g is not None:
                    mods(g)
                four_tiles(name, SLOTS, a_hi, a_lo, chunks)
                if g is not None:
                    mods(g + 1)

            pe.wait_ge(c_ready, 1)
            pe.wait_ge(const_ready, 1)
            mrow_sums(0)
            for g in range(1, G_START):
                mods(g)
            mcol(G_START - 1)
            stat("n0", SS0["n0"] + DC)
            spread(0)

            g = G_START
            four_tiles("cv_ab", 0, h_hi, h_lo, ready=h_part(0))
            mrow_sums(g)
            with pe.Fori(1, 4) as i:
                four_tiles("cv_ab", 0, h_hi, h_lo, i=i)
                mods(g + 1, i - 1)
            g += G_AB
            for b in range(2):
                four_tiles("cv_g", SLOTS * b, h_hi, h_lo)
                mods(g)
                g += 1
            assert g + 2 == MOD_1
            mods(g)
            mods(g + 1)
            with pe.Fori(0, G_WAIT // 2 - 1) as i:
                mods(g + 2, i, 2)
                mods(g + 3, i, 2)
            g += G_WAIT
            mean(SS0["cvm"] + DC)
            stat("cv", SS0["cv"] + DC)
            spread(ST["cv"])
            out("cv_out", f_hi, f_lo, z_part("cv"), g=g)
            g += 2
            stat("n1", SS0["n1"] + DC)
            spread(ST["n1"])

            for name in ("pl_v", "pl_g"):
                for b in range(2):
                    four_tiles(name, SLOTS * b, h_hi, h_lo, ready=h_part(1) if (name, b) == ("pl_v", 0) else None)
                    mods(g)
                    g += 1
            for k in range(GROUPS):
                unit_ready("pl_grp", k)
                for d in range(2):
                    bank_ready("pl_grp", 2 * k + d)
                    for c in range(2):
                        w = slice(c * GD + d * P, c * GD + (d + 1) * P)
                        pe.wait_ge(zl_ready, Z0["pv"] + 2 * k + c + 1)
                        last = three(bank[(2 * k + d) % SLOTS][:], w_hi[:, k, w], w_lo[:, k, w],
                                     f_hi[:, 2 * k + c, :], f_lo[:, 2 * k + c, :], c == 0, c == 1)
                last.then_inc(unit_used, 1)
            out("pl_out", h_hi, h_lo, z_part("pg"), g=g)
            g += 2
            stat("n2", SS0["n2"] + DC)
            spread(ST["n2"])

            pe.wait_ge(fr_const_lo, 1)
            for n in range(8):
                tok = slice((n // 2) * P, (n // 2 + 1) * P)
                bank_ready("fr_1", n)
                for gg in range(2):
                    for c in range(2):
                        k = 4 * (n % 2) + 2 * gg + c
                        if n < 2:
                            pe.wait_ge(hl_ready, DC * 2 + k + 1)
                        last = three(bank[n % SLOTS][:, gg * GD:(gg + 1) * GD], h_hi[:, k, tok], h_lo[:, k, tok],
                                     fr_hi[:, c, :], fr_lo[:, c, :], c == 0, c == 1)
                last.then_inc(tile_done, 1)
            mods(g)
            g += 1
            for s in range(SLOTS):
                unit_ready("fr_2", s)
            for b in range(SLOTS):
                wait_left(pe, "fr_1", SLOTS + b)
            for k in range(GROUPS):
                for part in range(3):
                    n = 3 * k + part
                    bank_ready("fr_2", n)
                    rows = bank[n % SLOTS][0:1, :] if part == 2 else bank[n % SLOTS][:]
                    cols = slice(k * GD + P, k * GD + P + 1) if part == 2 else slice(k * GD + part * P, k * GD + (part + 1) * P)
                    for s in range(4):
                        slot, at_ = (2 if part == 1 else 0) + s // 2, slice((s % 2) * T, (s % 2 + 1) * T)
                        last = three(rows, ab_hi[:, s, cols], ab_lo[:, s, cols], w_hi[:, slot, at_],
                                     w_lo[:, slot, at_], s == 0, s == 3)
                    if n == 3 * GROUPS - 1:
                        last.then_inc(unit_used, SLOTS)
                    else:
                        last.then_inc(tile_done, 1)
            out("fr_out", f_hi, f_lo, z_part("fr"), g=g)
            g += 2
            stat("n3", SS0["n3"] + DC)
            spread(ST["n3"])

            def ffn(layer, n, g):
                for p, chunks in enumerate(PARTS):
                    name = f"in{layer}{p}"
                    with_mods = layer == 0
                    if p == 0:
                        four_tiles(name, 0, h_hi, h_lo, ready=h_part(n))
                        if with_mods:
                            mods(g)
                    with pe.Fori(1 if p == 0 else 0, chunks // 2) as i:
                        four_tiles(name, 0, h_hi, h_lo, i=i)
                        if with_mods:
                            mods(g, i)
                    if with_mods:
                        g += chunks // 2
                    four_tiles(f"out{layer}{p}", 0, f_hi, f_lo, chunks, ready=z_part(f"f{layer}{p}"),
                               together=2)
                    if layer == 0 and p == 2:
                        mcol(MOD_GROUPS - 1)
                    four_tiles(f"out{layer}{p}", SLOTS, f_hi, f_lo, chunks)
                return g

            ffn(0, 3, g)
            stat("n4", SS0["n4"] + DC)
            spread(ST["n4"])

            SSH = SS0["h1"] - SS0["h0"]

            def two_of_qk(h, half):
                for s in (2 * half, 2 * half + 1):
                    unit_ready("qk1", s, h, UH)
                    bank_ready("qk1", s, h, RH)
                    for k in range(DC):
                        last = tile(s, k, h_hi, h_lo, DC)
                    last.then_inc(unit_used, 1)

            def v_units(h, n, units):
                for u in units:
                    unit_ready(f"v{n}", u, h, UH)
                    for tok in range(4):
                        if u == 0:
                            bank_ready(f"v{n}", tok, h, RH)
                        for kk in range(2):
                            k, cols = 2 * u + kk, slice(tok * P, (tok + 1) * P)
                            last = three(bank[tok][:], h_hi[:, k, cols], h_lo[:, k, cols],
                                         w_hi[:, u, kk * DV:(kk + 1) * DV], w_lo[:, u, kk * DV:(kk + 1) * DV],
                                         k == 0, k == DC - 1)
                    last.then_inc(unit_used, 1)

            def scores(h, n):
                z = Z0["qk0"] + 4 if n == 0 else Z0["k1"] + 2
                pe.wait_ge(zl_ready, ZH * h + z)
                for j in range(4):
                    bank_ready(f"sc{n}", j, h, RH)
                    cols = slice(j * P, (j + 1) * P)
                    for c in range(2):
                        last = three(bank[j][:], qk_hi[:, 2 + c, cols], qk_lo[:, 2 + c, cols],
                                     qk_hi[:, c, :], qk_lo[:, c, :], c == 0, c == 1)
                    last.then_inc(tile_done, 1)

            def project(h, n):
                for u in range(SLOTS):
                    unit_ready(f"ro{n}", u, h, UH)
                    for d in range(2):
                        r = 2 * u + d
                        bank_ready(f"ro{n}", r, h, RH)
                        for k in range(4):
                            w = slice((4 * d + k) * P, (4 * d + k + 1) * P)
                            last = three(bank[r % SLOTS][:], w_hi[:, u, w], w_lo[:, u, w], f_hi[:, k, :],
                                         f_lo[:, k, :], k == 0, k == 3)
                    last.then_inc(unit_used, 1)

            def gate_and_result(h, n):
                for s in range(SLOTS):
                    unit_ready(f"g{n}", s, h, UH)
                    bank_ready(f"g{n}", s, h, RH)
                    for k in range(DC):
                        last = tile(s, k, h_hi, h_lo, DC)
                    last.then_inc(unit_used, 1)
                pe.wait_ge(zl_ready, ZH * h + (Z0[f"p{n}"] + 4))
                for j in range(4):
                    bank_ready(f"av{n}", j, h, RH)
                    cols = slice(j * P, (j + 1) * P)
                    for s in range(4):
                        last = three(bank[j][:], v_hi[:, s, cols], v_lo[:, s, cols], f_hi[:, 4 + s, :],
                                     f_lo[:, 4 + s, :], s == 0, s == 3)
                    last.then_inc(tile_done, 1)

            four_tiles("qk0", 0, h_hi, h_lo, ready=h_part(4))
            v_units(0, 0, range(4))
            scores(0, 0)
            gate_and_result(0, 0)
            with pe.Fori(0, HEADS - 1) as h:
                two_of_qk(h, 0)
                mean(SSH * h + (SS0["h0m"] + 3))
                two_of_qk(h, 1)
                stat("h", SSH * h + (SS0["h0"] + 4))
                v_units(h, 1, range(0, 2))
                spread(h + ST["h0"])
                v_units(h, 1, range(2, 4))
                scores(h, 1)
                pe.wait_ge(zl_ready, ZH * h + (Z0["y0"] + 4))
                project(h, 0)
                gate_and_result(h, 1)
            h = HEADS - 1
            mean(SS0[f"h{h}m"] + 3)
            stat("h", SS0[f"h{h}"] + 4)
            spread(ST[f"h{h}"])
            pe.wait_ge(zl_ready, Z0[f"y{h}"] + 4)
            project(0, h)
            stat("n5", SS0["n5"] + DC)
            spread(ST["n5"])
            ffn(1, 5, None)
            stat("n6", SS0["n6"] + DC)
            spread(ST["n6"])


TD_HEAD = 8 + 3 * GROUPS - 1


def tiles_of(w):
    k, n = w.shape
    return w.reshape(k // P, P, n // P, P).transpose(2, 1, 0, 3).reshape(n // P, P, k)


def columns(v):
    return v.reshape(-1, P).T


def layout(a):
    out = {}
    out["x_t"] = a["x"][0].T.reshape(DC, P, T).transpose(1, 0, 2)
    gains = [a["norm_g"][0], a["norm_g"][1], a["norm_mix_g_2"][0], a["norm_ffn_g_2"][0],
             a["norm_mix_g_2"][1], a["norm_ffn_g_2"][1], a["final_norm_g_2"]]
    biases = [a["b_mod"].reshape(-1), a["b_ada_2"].reshape(-1), a["b_ada_final_2"]]
    out["vectors"] = np.concatenate(
        [columns(v) for v in [a["c"][0], a["c_2"][0], *biases, *gains, a["cv_dw"][0].reshape(-1), a["cv_db"][0],
                              a["cv_ln_g"][0], a["cv_ln_b"][0], a["pl_scale"][0]]], axis=1)
    mods = [w for w in (*a["w_mod"], *a["w_ada_2"], a["w_ada_final_2"])]
    out["w_mods"] = np.concatenate(
        [w.reshape(4, 2, P, -1, T).transpose(3, 0, 2, 1, 4).reshape(-1, P, 2 * T) for w in mods])
    cv = tiles_of(a["cv_w_in"][0])
    out["cv_ab"] = cv[:2 * DC].reshape(2, DC, P, D).transpose(1, 0, 2, 3).reshape(2 * DC, P, D)
    out["cv_g"] = cv[2 * DC:]
    out["cv_out"] = tiles_of(a["cv_w_out"][0])
    pl = tiles_of(a["pl_w_in"][0])
    out["pl_v"], out["pl_g"] = pl[:DC], pl[DC:]
    out["pl_grp"] = a["pl_w_grp"][0].reshape(GROUPS, 2, P, GD).transpose(0, 2, 1, 3).reshape(GROUPS, P, 2 * GD)
    out["pl_out"] = tiles_of(a["pl_w_out"][0])
    order = np.concatenate([np.r_[g * GD:g * GD + P, g * GD + P, g * GD + GD - 1:g * GD + P:-1]
                            for g in range(GROUPS)])
    out["fr_out"] = tiles_of(a["w_fourier_out_2"][0][order])
    for layer in range(2):
        gate_up = tiles_of(a["w_ffn_in_2"][layer])
        out[f"ff_in{layer}"] = gate_up.reshape(2, FC, P, D).transpose(1, 0, 2, 3).reshape(2 * FC, P, D)
        w = a["w_ffn_out_2"][layer]
        out[f"ff_out{layer}"] = np.concatenate([tiles_of(w[:8 * P]), tiles_of(w[8 * P:16 * P])])
        out[f"ff_tail{layer}"] = tiles_of(w[16 * P:])
    w_in, w_out = a["w_ret_in_2"][0], a["w_ret_out_2"][0]
    ret = []
    for h in range(HEADS):
        q, k = (tiles_of(w_in[:, o + h * DK:o + (h + 1) * DK]) for o in (0, HEADS * DK))
        v = w_in[:, 2 * HEADS * DK + h * DV:2 * HEADS * DK + (h + 1) * DV]
        v = v.reshape(4, 2, P, DV).transpose(0, 2, 1, 3).reshape(4, P, 2 * DV)
        g0 = 2 * HEADS * DK + HEADS * DV + h * DV
        o = tiles_of(w_out[h * DV:(h + 1) * DV])
        ret += [q, k, v, tiles_of(w_in[:, g0:g0 + DV]),
                o.reshape(4, 2, P, DV).transpose(0, 2, 1, 3).reshape(4, P, 2 * DV)]
    out["ret"] = np.concatenate(ret)
    return out


def tables():
    out = {}
    j, k = np.arange(GD)[:, None], np.arange(P)[None, :]
    angle = lambda a, b, n: 2 * np.pi * ((a * b) % n) / n
    ortho = 1.0 / np.sqrt(T * GD)
    feature = np.concatenate([np.cos(angle(j, k, GD)), np.cos(angle(j, P, GD)), np.sin(angle(j, k[:, 1:], GD))], 1)
    out["dft_feature"] = (feature * ortho).reshape(2, P, GD).transpose(1, 0, 2)
    s, tt = np.arange(T)[:, None], np.arange(T)[None, :]
    both = np.concatenate([np.cos(angle(s, tt, T)), np.sin(angle(s, tt, T))])
    out["dft_token"] = both.reshape(4, 2, P, T).transpose(0, 2, 1, 3).reshape(4, P, 2 * T)
    pos = np.arange(T)
    out["pl_cnt"] = np.broadcast_to(
        np.stack([1.0 / (np.clip(pos + w - w // 2, 0, T) - np.clip(pos - w // 2, 0, T)) for w in WINDOWS]),
        (P, len(WINDOWS), T))
    half = DK // 2
    inv_freq = np.float32(10000.0) ** (-np.arange(half, dtype=np.float32) / np.float32(half))
    ang = (pos.astype(np.float32)[None, :] * inv_freq[:, None]).astype(np.float64)
    out["rotary"] = np.stack([np.cos(ang), np.sin(ang)], 1)
    log_f = np.log1p(-np.exp2(-5.0 - np.arange(HEADS)))
    d = np.arange(T + 3 * P)[None, :] - 3 * P - np.arange(P)[:, None]
    out["decay"] = np.stack([np.where(d >= 0, np.exp(np.maximum(d, 0) * log_f[h]),
                                      np.exp(np.maximum(-d, 0) * log_f[HEADS - 1 - h])) for h in range(HEADS)]) * DK ** -0.5
    return {n: np.ascontiguousarray(v, dtype=np.float32) for n, v in out.items()}


def kernel(**inputs):
    import concourse.bacc as bacc
    from concourse.bass_utils import run_bass_kernel_spmd

    arrays = {n: np.ascontiguousarray(v) for n, v in layout({k: np.asarray(v) for k, v in inputs.items()}).items()}
    arrays.update(tables())
    nc = bacc.Bacc("TRN2", target_bir_lowering=False, num_devices=1)
    t = {n: nc.dram_tensor(n + "_in", v.shape, F32, kind="ExternalInput").ap() for n, v in arrays.items()}
    t["y_t"] = nc.dram_tensor("y_t", (P, DC, T), F32, kind="ExternalOutput").ap()
    build_program(nc, t)
    y = run_bass_kernel_spmd(nc, [{n + "_in": v for n, v in arrays.items()}], core_ids=[0]).results[0]["y_t"]
    return np.ascontiguousarray(y.transpose(1, 0, 2).reshape(D, T).T[None])
```

```python
from contextlib import ExitStack

import numpy as np

import concourse.bass as bass
from concourse import mybir

F32 = mybir.dt.float32
F32R = mybir.dt.float32r
ALU = mybir.AluOpType
ACT = mybir.ActivationFunctionType

P = 128
T = 512
D = 1024
DC = D // P
EPS = 1e-6
TAPS = 31
HALO = TAPS // 2
ROW = T + 2 * HALO
WINDOWS = (2, 4, 8, 16)
PAD = WINDOWS[-1] // 2
GROUPS = 4
GD = D // GROUPS
HEADS = 4
DK = D // HEADS
DV = 2 * DK
FF = -(-8 * D // (3 * 256)) * 256
FC = FF // P
PARTS = (8, 8, FC - 16)
SLOTS = 4
UNIT = 1024

MOD_COLS = 20 * DC
MOD_GROUPS = MOD_COLS // 4
MOD_1 = 12
V_C = 0
V_BIAS = V_C + 2 * DC
V_GAIN = V_BIAS + MOD_COLS
V_DW = V_GAIN + 7 * DC
V_DB = V_DW + TAPS * DC
V_LNG = V_DB + DC
V_LNB = V_LNG + DC
V_POOL = V_LNB + DC
V_COLS = V_POOL + DC

DVE_CHUNKS = ((0,), (2, 3), (4, 5), (6, 7))
ACT_TAPS = 13

SHIFT = [3 * DC * n for n in range(7)]

G_START, G_AB, G_GATE, G_WAIT = 4, 4, 2, 2
W_FIRST = G_START + G_AB + G_GATE
G_SUMS = W_FIRST + G_WAIT


SECOND = [g for g in range(G_START) if g % 2] + [W_FIRST]


def place_count(g):
    return sum((n in SECOND) == (g in SECOND) for n in range(g))


def place_before(g):
    return max((n + 1 for n in range(g) if (n in SECOND) == (g in SECOND)), default=None)


def starts(parts):
    at, found = 0, {}
    for name, n in parts:
        found[name] = at
        at += n
    return found, at


def head_order(of):
    out = []
    for h in range(HEADS):
        out += [of("qk", h), of("v", h), of("sc", h)]
        if h:
            out.append(of("ro", h - 1))
        out += [of("g", h), of("av", h)]
    return out + [of("ro", HEADS - 1)]


def both_ffn(layer, n_in, n_out):
    return [x for p, n in enumerate(PARTS)
            for x in ((f"in{layer}{p}", n_in(n)), (f"out{layer}{p}", n_out))]


U0, N_UNITS = starts(
    [("cv_ab", 16), ("cv_g", 8), ("cv_out", 8), ("pl_v", 8), ("pl_g", 8), ("pl_grp", 4), ("pl_out", 8),
     ("fr_2", 4), ("fr_out", 8)] + both_ffn(0, lambda n: 2 * n, 8)
    + head_order(lambda kind, h: (f"{kind}{h}", 0 if kind in ("sc", "av") else 4))
    + both_ffn(1, lambda n: 2 * n, 8))
R0, _ = starts(
    [("cv_ab", 16), ("cv_g", 8), ("cv_out", 8), ("pl_v", 8), ("pl_g", 8), ("pl_grp", 8), ("pl_out", 8),
     ("fr_1", 8), ("fr_2", 12), ("fr_out", 8)] + both_ffn(0, lambda n: 2 * n, 8)
    + head_order(lambda kind, h: (f"{kind}{h}", 8 if kind == "ro" else 4))
    + both_ffn(1, lambda n: 2 * n, 8))
assert all(v % SLOTS == 0 for v in (*U0.values(), *R0.values()))
UH, RH = U0["qk2"] - U0["qk1"], R0["qk2"] - R0["qk1"]

ffn_z = lambda layer: [(f"f{layer}{p}", n) for p, n in enumerate(PARTS)]
Z0, _ = starts(
    [("cv", 8), ("pv", 8), ("pg", 8), ("fr", 8)] + ffn_z(0) + [("qk0", 4), ("p0", 4)]
    + [x for h in range(1, HEADS) for x in ((f"q{h}", 2), (f"k{h}", 2), (f"y{h - 1}", 4), (f"p{h}", 4))]
    + [(f"y{HEADS - 1}", 4)] + ffn_z(1))
ZH = Z0["q2"] - Z0["q1"]
ZR0, _ = starts(
    [("cv", 8), ("pv", 8), ("fr", 4), ("qk0", 4)]
    + [x for h in range(1, HEADS) for x in ((f"q{h}", 2), (f"k{h}", 2), (f"y{h - 1}", 4))]
    + [(f"y{HEADS - 1}", 4)])
ZRH = ZR0["q2"] - ZR0["q1"]

STATS = ["n0", "cv", "n1", "n2", "n3", "n4"] + [f"h{h}" for h in range(HEADS)] + ["n5", "n6"]
ST = {name: i for i, name in enumerate(STATS)}
SS0, _ = starts([x for s in STATS if s != "cv" for x in (
    [(s + "m", 3), (s, 3)] if s[0] == "h" else [(s, DC - 1)])])
SQ0, _ = starts([(s, 4 if s[0] == "h" else DC) for s in STATS])


def build_program(nc, t):
    with ExitStack() as ctx:
        sem = lambda name: ctx.enter_context(nc.semaphore(name))
        sb = lambda name, shape, dt=F32: ctx.enter_context(nc.sbuf_tensor(name, shape, dt))

        w_raw = sb("w_raw", [P, SLOTS, UNIT])
        w_hi = sb("w_hi", [P, SLOTS, UNIT], F32R)
        w_lo = sb("w_lo", [P, SLOTS, UNIT], F32R)
        x = sb("x", [P, DC, T])
        h_hi = sb("h_hi", [P, DC, T], F32R)
        h_lo = sb("h_lo", [P, DC, T], F32R)
        f_hi = sb("f_hi", [P, 8, T], F32R)
        f_lo = sb("f_lo", [P, 8, T], F32R)
        sq = sb("sq", [P, T])
        ssum = sb("ssum", [P, T])
        diag = sb("diag", [P, T])
        mrow = sb("mrow", [P, T])
        ident = sb("ident", [P, P])
        ones = sb("ones", [P, P])
        vec = sb("vec", [P, V_COLS])
        c_pad = sb("c_pad", [P, DC, 32])
        c_2 = sb("c_2", [P, DC])
        mraw = sb("mraw", [P, MOD_COLS])
        mod = sb("mod", [P, MOD_COLS])
        aff = sb("aff", [P, DC])
        stdev = sb("stdev", [P, 4])
        rstd = sb("rstd", [P, 4])
        eps = sb("eps", [P, 1])
        spare = sb("spare", [P, 1])
        sign = sb("sign", [P, 2])

        def phase(*parts):
            with ExitStack() as s:
                return [s.enter_context(nc.sbuf_tensor(n, shape, dt)) for n, shape, dt in parts]

        mods_ring, = phase(("mods_ring", [P, SLOTS, UNIT], F32))
        _, cv_y, cv_acc, cv_g = phase(
            ("under_cv", [P, SLOTS * UNIT], F32), ("cv_y", [P, DC * ROW], F32),
            ("cv_acc", [P, DC, T], F32), ("cv_g", [P, DC, T], F32))
        _, m_buf, z_buf, s_buf, pl_v, pl_s, pl_cnt, pl_g = phase(
            ("under_pl", [P, SLOTS * UNIT], F32),
            ("m_buf", [P, 2, T], F32), ("z_buf", [P, 2, T], F32), ("s_buf", [P, 2, T], F32),
            ("pl_v", [P, 2, T + 2 * PAD], F32), ("pl_s", [P, 2, T + 2 * PAD], F32),
            ("pl_cnt", [P, len(WINDOWS), T], F32), ("pl_g", [P, DC, T], F32))
        mods_place = lambda g: (mods_ring if g not in SECOND else w_raw if g >= G_START else
                                cv_acc[:].rearrange("p (s c) n -> p s (c n)", s=SLOTS))
        fr_raw = s_buf[:, 1, :].rearrange("p (k n) -> p k n", k=2)
        _, _, fr_hi, fr_lo, ab_hi, ab_lo = phase(
            ("under_fr", [P, SLOTS * UNIT], F32), ("beside_fr", [P, 6 * T], F32),
            ("fr_hi", [P, 2, GD], F32R), ("fr_lo", [P, 2, GD], F32R),
            ("ab_hi", [P, 4, D], F32R), ("ab_lo", [P, 4, D], F32R))
        yh, sg, _, rot, mask, qk_hi, qk_lo, v_hi, v_lo = phase(
            ("yh", [P, 4, T], F32), ("sg", [P, 4, T], F32), ("beside_ret", [P, 4 * T], F32),
            ("rot", [P, 2, T], F32), ("mask", [P, T + 3 * P], F32),
            ("qk_hi", [P, 4, T], F32R), ("qk_lo", [P, 4, T], F32R),
            ("v_hi", [P, 4, DV], F32R), ("v_lo", [P, 4, DV], F32R))

        ps = lambda name: ctx.enter_context(nc.psum_tensor(name, [P, T], F32))
        bank = [ps(f"bank{b}") for b in range(SLOTS)]
        ps_stat, ps_bc, ps_mcol, ps_mrow = ps("ps_stat"), ps("ps_bc"), ps("ps_mcol"), ps("ps_mrow")

        raw_in = [sem(f"raw_in{s}") for s in range(SLOTS)]
        mods_in = [[sem(f"mods_in{s}") for s in range(SLOTS)], [sem(f"mods_odd_in{s}") for s in range(SLOTS)]]
        vec_in, x_in, cnt_in, fr_in, rot_in, mask_in, y_out = (
            sem(n) for n in ("vec_in", "x_in", "cnt_in", "fr_in", "rot_in", "mask_in", "y_out"))
        hi_done = sem("hi_done")
        lo_done = sem("lo_done")
        unit_used = sem("unit_used")
        tile_done = sem("tile_done")
        left = [sem(f"left_bank{b}") for b in range(SLOTS)]
        zeroed, const_ready, c_ready = sem("zeroed"), sem("const_ready"), sem("c_ready")
        mrow_done, mrow_copied = sem("mrow_done"), sem("mrow_copied")
        mcol_done, mcol_copied = sem("mcol_done"), sem("mcol_copied")
        msum_step = sem("msum_step")
        mod_step = sem("mod_step")
        sq_ready, sum_step, sq_used = sem("sq_ready"), sem("sum_step"), sem("sq_used")
        pair_sum = sem("pair_sum")
        cv_sum = sem("cv_sum")
        pool_tap = sem("pool_tap")
        product_ready = sem("product_ready")
        v_done = sem("v_done")
        stat_done, std_ready, rstd_ready, diag_ready, bc_done, mean_done, centered, scaled = (
            sem(n) for n in ("stat_done", "std_ready", "rstd_ready", "diag_ready", "bc_done", "mean_done",
                             "centered", "scaled"))
        m_ready, hh_ready, hl_ready = sem("m_ready"), sem("hh_ready"), sem("hl_ready")
        z_ready, zh_ready, zl_ready = sem("z_ready"), sem("zh_ready"), sem("zl_ready")
        halo_ready, y_ready, tap_done, ln_silu = sem("halo_ready"), sem("y_ready"), sem("tap_done"), sem("ln_silu")
        win_step, fr_const, fr_const_lo, ab_ready, vh_ready, rot_step = (
            sem(n) for n in ("win_step", "fr_const", "fr_const_lo", "ab_ready", "vh_ready", "rot_step"))
        out_ready = sem("out_ready")

        def wait_unit(eng, name, n, i=0, per=SLOTS):
            eng.wait_ge(unit_used, per * i + (U0[name] + n + 1))

        def wait_left(eng, name, n, i=0, per=SLOTS):
            eng.wait_ge(left[n % SLOTS], (per // SLOTS) * i + ((R0[name] + n) // SLOTS + 1))

        def at(buf, i):
            return buf[:, i, :] if isinstance(i, int) else buf[:, bass.ds(i, 1), :].rearrange("p a n -> p (a n)")

        block = ctx.enter_context(nc.Block())

        @block.sync
        def _(sp):
            def four(name, a, first, width=UNIT, i=0, per_u=SLOTS, per_a=SLOTS, fresh=False):
                for s in range(SLOTS):
                    if not fresh:
                        sp.wait_ge(lo_done, per_u * i + (U0[name] + s + 1 - SLOTS))
                    src = a[bass.ds(per_a * i + (first + s), 1)].rearrange("a p n -> p (a n)")
                    sp.dma_start(w_raw[:, s, 0:width], src).then_inc(raw_in[s], 16)

            def later(name, n):
                U0[f"{name}+{n}"] = U0[name] + SLOTS * n
                return f"{name}+{n}"

            def mods(g, i=0, per=1):
                if g > G_SUMS:
                    sp.wait_ge(msum_step, DC * per * i + DC * (g - G_SUMS))
                elif place_before(g):
                    sp.wait_ge(mrow_done, per * i + place_before(g))
                for s in range(SLOTS):
                    src = t["w_mods"][bass.ds(SLOTS * per * i + (SLOTS * g + s), 1)].rearrange("a p n -> p (a n)")
                    sp.dma_start(mods_place(g)[:, s, :], src).then_inc(mods_in[g in SECOND][s], 16)

            sp.dma_start(vec[:], t["vectors"]).then_inc(vec_in, 16)
            mods(0)
            mods(1)
            sp.dma_start(x[:], t["x_t"]).then_inc(x_in, 16)
            for g in range(2, G_START):
                mods(g)
            g = G_START
            four("cv_ab", t["cv_ab"], 0, fresh=True)
            mods(g)
            with sp.Fori(1, 4) as i:
                four("cv_ab", t["cv_ab"], 0, i=i)
                mods(g + 1, i - 1)
            g += G_AB
            for b in range(2):
                four(later("cv_g", b), t["cv_g"], SLOTS * b)
                mods(g + b)
            g += G_GATE
            sp.wait_ge(lo_done, U0["cv_out"])
            mods(g)
            mods(g + 1)
            sp.wait_ge(mrow_done, W_FIRST + 1)
            g += G_WAIT
            for b in range(2):
                four(later("cv_out", b), t["cv_out"], SLOTS * b, fresh=b == 0)
                mods(g + b)
            g += 2
            for name in ("pl_v", "pl_g"):
                for b in range(2):
                    four(later(name, b), t[name], SLOTS * b)
                    if (name, b) == ("pl_v", 0):
                        sp.wait_ge(zl_ready, Z0["cv"] + DC)
                        sp.dma_start(pl_cnt[:], t["pl_cnt"]).then_inc(cnt_in, 16)
                        sp.dma_start(fr_raw, t["dft_feature"]).then_inc(fr_in, 16)
                    mods(g + b)
                g += 2
            four("pl_grp", t["pl_grp"], 0, width=2 * GD)
            for b in range(2):
                four(later("pl_out", b), t["pl_out"], SLOTS * b)
                mods(g + b)
            g += 2
            four("fr_2", t["dft_token"], 0)
            mods(g)
            g += 1
            for b in range(2):
                four(later("fr_out", b), t["fr_out"], SLOTS * b)
                mods(g + b)
            g += 2

            def ffn(layer, g):
                first_in = 0
                for p, n in enumerate(PARTS):
                    with sp.Fori(0, n // 2) as i:
                        four(f"in{layer}{p}", t[f"ff_in{layer}"], first_in, i=i)
                        if layer == 0:
                            mods(g, i)
                    if layer == 0:
                        g += n // 2
                    first_in += 2 * n
                    src, first_out = (t[f"ff_out{layer}"], 8 * p) if n == 8 else (t[f"ff_tail{layer}"], 0)
                    with sp.Fori(0, 2) as i:
                        four(f"out{layer}{p}", src, first_out, width=n * P, i=i)
                        if layer == 0:
                            mods(g, i)
                    if layer == 0:
                        g += 2
                return g

            g = ffn(0, g)
            assert g == MOD_GROUPS, g

            def mask_load(h):
                sp.dma_start(mask[:], t["decay"][bass.ds(h, 1)].rearrange("a p n -> p (a n)")).then_inc(mask_in, 16)

            sp.wait_ge(zl_ready, Z0["f02"] + PARTS[2])
            sp.dma_start(rot[:], t["rotary"]).then_inc(rot_in, 16)
            mask_load(0)
            four("qk0", t["ret"], 0)
            four("v0", t["ret"], 4)
            four("g0", t["ret"], 8)
            with sp.Fori(0, HEADS - 1) as h:
                four("qk1", t["ret"], 16, i=h, per_u=UH, per_a=16)
                sp.wait_ge(zl_ready, ZH * h + (Z0["p0"] + 4))
                mask_load(h + 1)
                four("v1", t["ret"], 20, i=h, per_u=UH, per_a=16)
                four("ro0", t["ret"], 12, i=h, per_u=UH, per_a=16)
                four("g1", t["ret"], 24, i=h, per_u=UH, per_a=16)
            four(f"ro{HEADS - 1}", t["ret"], 16 * (HEADS - 1) + 12)
            ffn(1, g)
            for c in range(DC):
                sp.wait_ge(out_ready, c + 1)
                sp.dma_start(t["y_t"][:, c, :], x[:, c, :]).then_inc(y_out, 16)
            sp.wait_ge(y_out, 16 * DC)

        @block.gpsimd
        def _(pool):
            pool.memset(ident[:], 0.0)
            pool.memset(ones[:], 1.0)
            pool.memset(eps[:], EPS)
            pool.memset(sign[:, 0:1], -1.0)
            pool.memset(sign[:, 1:2], 1.0)
            pool.memset(c_pad[:], 0.0).then_inc(zeroed, 1)
            pool.wait_ge(zeroed, 1)
            pool.memset(sign[0:1, :], 0.0)
            pool.affine_select(out=ident[:], in_=ident[:], compare_op=ALU.not_equal, fill=1.0, base=0,
                               pattern=[[-1, P]], channel_multiplier=1).then_inc(const_ready, 1)

            def lo_part(u, s):
                pool.wait_ge(hi_done, u + 1)
                pool.tensor_tensor(w_lo[:, s, :], w_raw[:, s, :], w_hi[:, s, :].bitcast(F32),
                                   ALU.subtract).then_inc(lo_done, 1)

            for u in range(SLOTS):
                lo_part(u, u)
            pool.wait_ge(hl_ready, DC)
            rows = cv_y[:].rearrange("p (c n) -> p c n", c=DC)
            pool.memset(rows[:, :, 0:HALO], 0.0)
            pool.memset(rows[:, :, HALO + T:ROW], 0.0).then_inc(halo_ready, 1)

            def y_and_lo_parts(i, k):
                for q in range(2):
                    if q:
                        lo_part(SLOTS * i + 5, 1)
                    lo_part(SLOTS * i + (4 + 2 * q), 2 * q)
                    wait_left(pool, "cv_ab", 2 * q, i)
                    wait_left(pool, "cv_ab", 2 * q + 1, i)
                    at_y = (2 * i + q) * ROW + HALO
                    pool.tensor_tensor(cv_y[:, at_y:at_y + T], cv_g[:, 2 * q, :], cv_g[:, 2 * q + 1, :],
                                       ALU.mult).then_inc(y_ready, 1)
                    if i:
                        for m in range(2):
                            tap(k + 2 * q + m)
                lo_part(SLOTS * i + 7, 3)

            def tap(k):
                product = (sq, diag)[k % 2]
                if k < ACT_TAPS:
                    pool.wait_ge(pool_tap, k)
                    pool.tensor_scalar(product[:], cv_y[:, ROW + k:ROW + k + T],
                                       vec[:, V_DW + DC * k + 1:V_DW + DC * k + 2], None,
                                       ALU.mult).then_inc(product_ready, 1)
                pool.wait_ge(product_ready, k)
                if k >= ACT_TAPS:
                    pool.wait_ge(pool_tap, k)
                pool.tensor_tensor(cv_acc[:, 1, :], cv_acc[:, 1, :], product[:], ALU.add).then_inc(pool_tap, 1)

            y_and_lo_parts(0, 0)
            pool.wait_ge(y_ready, 2)
            pool.tensor_scalar(cv_acc[:, 1, :], cv_y[:, ROW:ROW + T], vec[:, V_DW + 1:V_DW + 2],
                               vec[:, V_DB + 1:V_DB + 2], ALU.mult, ALU.add).then_inc(pool_tap, 1)
            for i in range(1, 4):
                y_and_lo_parts(i, 4 * i - 3)
            first = U0["cv_g"]
            for q in range(2):
                lo_part(first + SLOTS + 2 * q, 2 * q)
                lo_part(first + SLOTS + 2 * q + 1, 2 * q + 1)
                for m in range(4):
                    tap(ACT_TAPS + 4 * q + m)
            for k in range(ACT_TAPS + 8, TAPS):
                tap(k)
            pool.wait_ge(pool_tap, TAPS)
            pool.wait_ge(tap_done, 2 * TAPS)
            pool.tensor_tensor(ssum[:], cv_acc[:, 0, :], cv_acc[:, 1, :], ALU.add).then_inc(cv_sum, 1)
            pool.wait_ge(tap_done, 4 * TAPS)
            for n in (2, 3):
                pool.wait_ge(cv_sum, n - 1)
                pool.tensor_tensor(ssum[:], ssum[:], cv_acc[:, n, :], ALU.add).then_inc(cv_sum, 1)
            first = U0["cv_out"]
            with pool.Fori(0, (N_UNITS - first) // SLOTS) as i:
                for s in range(SLOTS):
                    lo_part(SLOTS * i + (first + s), s)

        @block.scalar
        def _(act):
            def refill(name, s, i=0, per=SLOTS):
                u = U0[name] + s + SLOTS
                if u >= N_UNITS:
                    return
                act.wait_ge(raw_in[u % SLOTS], 16 * (per // SLOTS) * i + 16 * (u // SLOTS + 1))
                act.wait_ge(unit_used, per * i + (u + 1 - SLOTS))
                act.activation(w_hi[:, u % SLOTS, :], w_raw[:, u % SLOTS, :], ACT.Copy).then_inc(hi_done, 1)

            def mods(g):
                mcol(g - 1)
                act.wait_ge(mrow_done, g + 1)
                act.activation(mrow[:], ps_mrow[:], ACT.Copy).then_inc(mrow_copied, 1)

            def mcol(g):
                act.wait_ge(mcol_done, g + 1)
                if isinstance(g, int):
                    dst = mraw[:, 4 * g:4 * g + 4]
                else:
                    act.wait_ge(const_ready, 1)
                    dst = mraw[:, bass.ds(4 * g, 4)]
                act.activation(dst, ps_mcol[:, 0:4], ACT.Copy).then_inc(mcol_copied, 1)

            def square(stat, c, src, i=0, per=0):
                if SS0[stat] + c:
                    act.wait_ge(sum_step, per * i + (SS0[stat] + c))
                if c == 0 and ST[stat]:
                    act.wait_ge(stat_done, i + ST[stat])
                act.activation(sq[:], src, ACT.Square).then_inc(sq_ready, 1)

            def std(stat, n):
                act.wait_ge(stat_done, stat + 1)
                act.wait_ge(const_ready, 1)
                act.activation(stdev[:], ps_stat[:, 0:4], ACT.Sqrt, bias=eps[:], scale=1.0 / n).then_inc(std_ready, 1)

            def norm(n):
                for c in range(DC):
                    act.wait_ge(m_ready, DC * n + c + 1)
                    act.activation(h_hi[:, c, :], m_buf[:, c % 2, :], ACT.Identity,
                                   bias=mod[:, SHIFT[n] + c:SHIFT[n] + c + 1]).then_inc(hh_ready, 1)

            def hi(dst, q):
                act.activation(dst, z_buf[:, q, :], ACT.Copy).then_inc(zh_ready, 1)

            def out(name, stat, g=None):
                for j in range(DC):
                    if stat is not None:
                        if j == 0:
                            act.activation(spare[:], eps[:], ACT.Sqrt)
                        wait_left(act, name, j)
                        square(stat, j, x[:, j, :])
                    refill(name, j)
                    if g is not None and j % SLOTS == SLOTS - 1:
                        mcol(g)
                        g += 1
                return g

            act.wait_ge(const_ready, 1)
            act.wait_ge(vec_in, 16)
            act.activation(c_2[:], vec[:, V_C + DC:V_C + 2 * DC], ACT.Silu)
            act.activation(c_pad[:, :, 0], vec[:, V_C:V_C + DC], ACT.Silu).then_inc(c_ready, 1)
            act.wait_ge(mrow_done, 1)
            act.activation(mrow[:], ps_mrow[:], ACT.Copy).then_inc(mrow_copied, 1)
            mods(1)
            act.wait_ge(x_in, 16)
            for c in range(DC):
                square("n0", c, x[:, c, :])
            for g in range(2, G_START):
                mods(g)
            mcol(G_START - 1)
            std(0, D)
            for u in range(SLOTS):
                act.wait_ge(raw_in[u], 16)
                act.activation(w_hi[:, u, :], w_raw[:, u, :], ACT.Copy).then_inc(hi_done, 1)
            norm(0)

            def ab(i):
                for q in range(2):
                    wait_unit(act, "cv_ab", 2 * q, i)
                    if not isinstance(i, int):
                        act.wait_ge(y_ready, 2 * i + (q - 1))
                    act.activation(cv_g[:, 2 * q, :], bank[2 * q][:], ACT.Copy).then_inc(left[2 * q], 1)
                    refill("cv_ab", 2 * q, i)
                    wait_unit(act, "cv_ab", 2 * q + 1, i)
                    act.activation(cv_g[:, 2 * q + 1, :], bank[2 * q + 1][:], ACT.Sigmoid).then_inc(left[2 * q + 1], 1)
                    refill("cv_ab", 2 * q + 1, i)

            g = G_START
            ab(0)
            act.wait_ge(mrow_done, g + 1)
            act.activation(mrow[:], ps_mrow[:], ACT.Copy).then_inc(mrow_copied, 1)
            with act.Fori(1, 4) as i:
                ab(i)
                mods(i + g)
            g += G_AB
            act.wait_ge(y_ready, DC)

            def products(k, n):
                for m in range(k, k + n):
                    act.wait_ge(pool_tap, m - 1)
                    if m == ACT_TAPS:
                        act.wait_ge(product_ready, ACT_TAPS - 1)
                    act.activation((sq, diag)[m % 2][:], cv_y[:, ROW + m:ROW + m + T], ACT.Copy,
                                   scale=vec[:, V_DW + DC * m + 1:V_DW + DC * m + 2]).then_inc(product_ready, 1)

            for j in range(DC):
                wait_unit(act, "cv_g", j)
                act.activation(cv_g[:, j, :], bank[j % SLOTS][:], ACT.Silu).then_inc(left[j % SLOTS], 1)
                if j < SLOTS:
                    refill("cv_g", j)
                else:
                    products(ACT_TAPS + 2 * j, 2)
                if j == 1:
                    products(ACT_TAPS, 4)
                if j == 3:
                    products(ACT_TAPS + 4, 4)
                if j % SLOTS == SLOTS - 1:
                    mods(g)
                    g += 1
            products(TAPS - 2, 2)
            mods(g)
            mods(g + 1)
            g += G_WAIT
            mcol(g - 1)
            for j in range(SLOTS, DC):
                refill("cv_g", j)
            act.wait_ge(mean_done, 1)
            for c in range(DC):
                act.wait_ge(centered, c + 1)
                if c >= 2:
                    act.wait_ge(pair_sum, c // 2)
                act.activation((sq, ssum)[c % 2][:], cv_acc[:, c, :], ACT.Square).then_inc(sq_ready, 1)
            std(ST["cv"], D)
            for c in range(DC + 1):
                if c < DC:
                    act.wait_ge(scaled, c + 1)
                    act.activation(cv_acc[:, c, :], cv_acc[:, c, :], ACT.Silu, bias=vec[:, V_LNB + c:V_LNB + c + 1],
                                   scale=vec[:, V_LNG + c:V_LNG + c + 1]).then_inc(ln_silu, 1)
                if c:
                    act.wait_ge(z_ready, ZR0["cv"] + c)
                    hi(f_hi[:, c - 1, :], (c - 1) % 2)
            g = out("cv_out", "n1", g)
            std(ST["n1"], D)
            norm(1)

            for j in range(DC):
                wait_unit(act, "pl_v", j)
                if j < 2:
                    act.wait_ge(win_step, 1)
                else:
                    act.wait_ge(z_ready, ZR0["pv"] + j - 1)
                act.activation(pl_v[:, j % 2, PAD:PAD + T], bank[j % SLOTS][:], ACT.Copy).then_inc(left[j % SLOTS], 1)
                refill("pl_v", j)
                act.wait_ge(z_ready, ZR0["pv"] + j + 1)
                hi(f_hi[:, j, :], j % 2)
                if j % SLOTS == SLOTS - 1:
                    mcol(g)
                    g += 1
            for j in range(DC):
                wait_unit(act, "pl_g", j)
                act.activation(pl_g[:, j, :], bank[j % SLOTS][:], ACT.Silu).then_inc(left[j % SLOTS], 1)
                refill("pl_g", j)
                if j % SLOTS == SLOTS - 1:
                    mcol(g)
                    g += 1
            for j in range(DC):
                wait_left(act, "pl_grp", j)
                hi(h_hi[:, j, :], j % 2)
                if j % 2:
                    refill("pl_grp", j // 2)
            g = out("pl_out", "n2", g)
            act.wait_ge(fr_in, 16)
            act.activation(fr_hi[:], fr_raw, ACT.Copy).then_inc(fr_const, 1)
            std(ST["n2"], D)
            norm(2)

            for n in range(8):
                act.wait_ge(tile_done, n + 1)
                act.activation(ab_hi[:, n // 2, (n % 2) * T:(n % 2 + 1) * T], bank[n % SLOTS][:],
                               ACT.Copy).then_inc(ab_ready, 1)
            mcol(g)
            g += 1
            for k in range(GROUPS):
                act.wait_ge(tile_done, 8 + 3 * k + 1)
                if k:
                    wait_left(act, "fr_2", 3 * k - 2)
                else:
                    act.wait_ge(fr_const_lo, 1)
                act.activation(s_buf[:, 0, :], bank[3 * k % SLOTS][:], ACT.Copy).then_inc(left[3 * k % SLOTS], 1)
                act.wait_ge(z_ready, ZR0["fr"] + k + 1)
                hi(f_hi[:, 2 * k, :], 0)
                wait_left(act, "fr_2", 3 * k + 2)
                hi(f_hi[:, 2 * k + 1, :], 1)
            for s in range(SLOTS):
                refill("fr_2", s)
            g = out("fr_out", "n3", g)
            std(ST["n3"], D)
            norm(3)

            def ffn(layer, g, stat):
                for p, n in enumerate(PARTS):
                    name = f"in{layer}{p}"
                    with_mods = layer == 0
                    with act.Fori(0, n // 2) as i:
                        for q in range(2):
                            wait_unit(act, name, 2 * q, i)
                            act.wait_ge(left[2 * q + 1], i + R0[name] // SLOTS)
                            act.activation(s_buf[:, q, :], bank[2 * q][:], ACT.Silu).then_inc(left[2 * q], 1)
                            refill(name, 2 * q, i)
                            wait_left(act, name, 2 * q + 1, i)
                            act.wait_ge(const_ready, 1)
                            hi(at(f_hi, 2 * i + q), q)
                            refill(name, 2 * q + 1, i)
                        if with_mods:
                            mcol(i + g)
                    if with_mods:
                        g += n // 2
                    g = out(f"out{layer}{p}", stat if p == len(PARTS) - 1 else None, g if with_mods else None)
                return g

            ffn(0, g, "n4")
            std(ST["n4"], D)
            norm(4)

            def head_rest(h, n, first):
                for s in range(0 if first else 2, 3):
                    refill(f"v{n}", s, h, UH)
                for j in range(4):
                    if j < 3:
                        act.wait_ge(v_done, 3 * h + (3 * n + j + 1))
                    else:
                        wait_unit(act, f"v{n}", 3, h, UH)
                    act.activation(v_hi[:, j, :], bank[j][:], ACT.Copy).then_inc(vh_ready, 1)
                refill(f"v{n}", 3, h, UH)
                for j in range(4):
                    wait_left(act, f"sc{n}", j, h, RH)
                    hi(f_hi[:, 4 + j, :], j % 2)
                if not first:
                    for s in range(SLOTS):
                        refill(f"ro{n - 1}", s, h, UH)
                for s in range(SLOTS):
                    wait_unit(act, f"g{n}", s, h, UH)
                    act.activation(sg[:, s, :], bank[s][:], ACT.Silu).then_inc(left[s], 1)
                    refill(f"g{n}", s, h, UH)
                for j in range(4):
                    act.wait_ge(tile_done, 8 * h + (TD_HEAD + 8 * n + 4 + j + 1))
                    act.activation(yh[:, j, :], bank[j][:], ACT.Copy).then_inc(left[j], 1)

            def head_squares(h):
                for j in range(4):
                    act.wait_ge(centered, 4 * h + (DC + j + 1))
                    square("h0", j, yh[:, j, :], h, SS0["h1"] - SS0["h0"])

            for s in range(SLOTS):
                refill("qk0", s)
            for j in range(4):
                act.wait_ge(z_ready, ZR0["qk0"] + j + 1)
                hi(qk_hi[:, j, :], j % 2)
            head_rest(0, 0, True)
            with act.Fori(0, HEADS - 1) as h:
                for half in range(2):
                    for s in (2 * half, 2 * half + 1):
                        refill("qk1", s, h, UH)
                    for j in range(2):
                        act.wait_ge(z_ready, ZRH * h + (ZR0["qk"[half] + "1"] + j + 1))
                        hi(qk_hi[:, 2 * half + j, :], j)
                    if half == 0:
                        head_squares(h)
                std(h + ST["h0"], DV)
                refill("v1", 0, h, UH)
                refill("v1", 1, h, UH)
                for j in range(4):
                    act.wait_ge(z_ready, ZRH * h + (ZR0["y0"] + j + 1))
                    hi(f_hi[:, j, :], j % 2)
                head_rest(h, 1, False)
            head_squares(HEADS - 1)
            std(ST[f"h{HEADS - 1}"], DV)
            last = f"y{HEADS - 1}"
            for j in range(4):
                act.wait_ge(z_ready, ZR0[last] + j + 1)
                hi(f_hi[:, j, :], j % 2)
            name = f"ro{HEADS - 1}"
            for j in range(DC):
                wait_left(act, name, j)
                square("n5", j, x[:, j, :])
                if j % 2:
                    refill(name, j // 2)
            std(ST["n5"], D)
            norm(5)
            ffn(1, None, "n6")
            std(ST["n6"], D)
            for c in range(DC):
                act.wait_ge(m_ready, DC * 6 + c + 1)
                act.activation(x[:, c, :], m_buf[:, c % 2, :], ACT.Identity,
                               bias=mod[:, SHIFT[6] + c:SHIFT[6] + c + 1]).then_inc(out_ready, 1)

        @block.vector
        def _(vec_e):
            v = vec_e
            steps = {"mod": 0}

            def add_bias(a, n):
                v.wait_ge(mcol_copied, -(-(a + n) // 4))
                v.tensor_tensor(mod[:, a:a + n], mraw[:, a:a + n], vec[:, V_BIAS + a:V_BIAS + a + n],
                                ALU.add).then_inc(mod_step, 1)
                steps["mod"] += 1

            def prepare(n):
                add_bias(SHIFT[n], 2 * DC)
                v.wait_ge(mod_step, steps["mod"])
                v.scalar_tensor_tensor(aff[:], mod[:, SHIFT[n] + DC:SHIFT[n] + 2 * DC], 1.0,
                                       vec[:, V_GAIN + n * DC:V_GAIN + (n + 1) * DC], ALU.add,
                                       ALU.mult).then_inc(mod_step, 1)
                steps["mod"] += 1

            def gate(n, j):
                c = SHIFT[n] + 2 * DC + j
                return mod[:, c:c + 1]

            def add_square(stat, c, i=0, per=0, per_sq=0):
                v.wait_ge(sq_ready, per_sq * i + (SQ0[stat] + c + 1))
                if SS0[stat] + c:
                    v.wait_ge(sum_step, per * i + (SS0[stat] + c))
                if c == 0:
                    v.tensor_copy(ssum[:], sq[:]).then_inc(sum_step, 1)
                else:
                    v.tensor_tensor(ssum[:], ssum[:], sq[:], ALU.add).then_inc(sum_step, 1)

            def spread(stat):
                v.wait_ge(std_ready, stat + 1)
                v.reciprocal(rstd[:], stdev[:]).then_inc(rstd_ready, 1)
                v.wait_ge(rstd_ready, stat + 1)
                for j in range(4):
                    v.tensor_scalar(diag[:, j * P:(j + 1) * P], ident[:], rstd[:, j:j + 1], None,
                                    ALU.mult).then_inc(diag_ready, 1)

            def norm(n, stat, lo=True):
                prepare(n)
                spread(stat)
                v.wait_ge(mod_step, steps["mod"])
                v.wait_ge(bc_done, stat + 1)
                for c in range(DC + 1):
                    if c < DC:
                        if c >= 2:
                            v.wait_ge(hl_ready if lo else out_ready, (DC * n if lo else 0) + c - 1)
                        v.scalar_tensor_tensor(m_buf[:, c % 2, :], x[:, c, :], aff[:, c:c + 1], ps_bc[:],
                                               ALU.mult, ALU.mult).then_inc(m_ready, 1)
                    if c and lo:
                        v.wait_ge(hh_ready, DC * n + c)
                        v.scalar_tensor_tensor(h_lo[:, c - 1, :], m_buf[:, (c - 1) % 2, :],
                                               mod[:, SHIFT[n] + c - 1:SHIFT[n] + c],
                                               h_hi[:, c - 1, :].bitcast(F32), ALU.add,
                                               ALU.subtract).then_inc(hl_ready, 1)

            def sum_mods(g, i=0):
                steps0 = DC * (g - G_SUMS)
                v.wait_ge(mcol_done, i + g)
                for k in range(DC):
                    part = mods_ring[:, k // 2, (k % 2) * T:(k % 2 + 1) * T]
                    if k % 2 == 0:
                        v.wait_ge(mods_in[0][k // 2], 16 * i + (16 * place_count(g) + 16))
                    if k == 0:
                        v.tensor_scalar(mrow[:], part, c_2[:, 0:1], None, ALU.mult).then_inc(msum_step, 1)
                    else:
                        v.wait_ge(msum_step, DC * i + (steps0 + k))
                        v.scalar_tensor_tensor(mrow[:], part, c_2[:, k:k + 1], mrow[:], ALU.mult,
                                               ALU.add).then_inc(msum_step, 1)

            def z_free(z, i=0, per=0):
                if not isinstance(i, int) or per * i + z >= 2:
                    v.wait_ge(zl_ready, per * i + (z - 1))

            def lo(dst, hi, z, q, i=0, per=0):
                v.wait_ge(zh_ready, per * i + (z + 1))
                v.tensor_tensor(dst, z_buf[:, q, :], hi, ALU.subtract).then_inc(zl_ready, 1)

            def out(name, n, stat, per_unit=1, g=None):
                for j in range(DC):
                    if g is not None and j % SLOTS == 0:
                        sum_mods(g + j // SLOTS)
                    wait_unit(v, name, j // per_unit)
                    v.scalar_tensor_tensor(x[:, j, :], bank[j % SLOTS][:], gate(n, j), x[:, j, :],
                                           ALU.mult, ALU.add).then_inc(left[j % SLOTS], 1)
                    if stat is not None and j < DC - 1:
                        add_square(stat, j)

            for c in range(DC - 1):
                add_square("n0", c)
            norm(0, 0)
            done = 0
            for chunks in DVE_CHUNKS:
                pieces = [(c, 0, T) for c in chunks] if len(chunks) > 1 else [(chunks[0], a, T // 2) for a in (0, T // 2)]
                v.wait_ge(y_ready, chunks[-1] + 1)
                for c, a, n in pieces:
                    v.tensor_scalar(cv_acc[:, c, a:a + n], cv_y[:, c * ROW + a:c * ROW + a + n],
                                    vec[:, V_DW + c:V_DW + c + 1], vec[:, V_DB + c:V_DB + c + 1],
                                    ALU.mult, ALU.add).then_inc(tap_done, 1)
                with v.Fori(1, TAPS) as k:
                    for q, (c, a, n) in enumerate(pieces):
                        v.wait_ge(tap_done, len(pieces) * k + (done + q + 1 - len(pieces)))
                        v.scalar_tensor_tensor(cv_acc[:, c, a:a + n], cv_y[:, bass.ds(k + (c * ROW + a), n)],
                                               vec[:, bass.ds(DC * k + (V_DW + c), 1)], cv_acc[:, c, a:a + n],
                                               ALU.mult, ALU.add).then_inc(tap_done, 1)
                done += len(pieces) * TAPS
            add_bias(SHIFT[0] + 2 * DC, DC)
            v.wait_ge(mean_done, 1)
            for c in range(DC + 1):
                if c < DC:
                    v.scalar_tensor_tensor(cv_acc[:, c, :], ps_bc[:], -1.0 / D, cv_acc[:, c, :],
                                           ALU.mult, ALU.add).then_inc(centered, 1)
                if c >= 2 and c % 2 == 0:
                    v.wait_ge(sq_ready, SQ0["cv"] + c)
                    if c > 2:
                        v.wait_ge(sq_used, c // 2 - 1)
                    v.tensor_tensor(diag[:], sq[:], ssum[:], ALU.add).then_inc(pair_sum, 1)
            spread(ST["cv"])
            v.wait_ge(bc_done, ST["cv"] + 1)
            for c in range(DC + 2):
                if c < DC:
                    v.tensor_tensor(cv_acc[:, c, :], cv_acc[:, c, :], ps_bc[:], ALU.mult).then_inc(scaled, 1)
                if 1 <= c <= DC:
                    n = c - 1
                    v.wait_ge(ln_silu, n + 1)
                    z_free(Z0["cv"] + n)
                    v.tensor_tensor(z_buf[:, n % 2, :], cv_acc[:, n, :], cv_g[:, n, :], ALU.mult).then_inc(z_ready, 1)
                if c >= 2:
                    n = c - 2
                    lo(f_lo[:, n, :], f_hi[:, n, :].bitcast(F32), Z0["cv"] + n, n % 2)
            v.wait_ge(mod_step, steps["mod"])
            g = G_SUMS
            out("cv_out", 0, "n1", g=g)
            g += 2
            norm(1, ST["n1"])

            v.memset(pl_v[:], 0.0).then_inc(win_step, 1)
            ws = 1
            add_bias(SHIFT[1] + 2 * DC, DC)
            v.wait_ge(cnt_in, 16)
            for j in range(DC):
                if j % SLOTS == 0:
                    sum_mods(g)
                    g += 1
                w = WINDOWS[j // 2]
                wait_left(v, "pl_v", j)
                src, span, length = pl_v[:, j % 2, :], 1, T + 2 * PAD
                while span < w:
                    length -= span
                    dst = pl_s[:, span.bit_length() % 2, :]
                    v.tensor_tensor(dst[:, 0:length], src[:, 0:length], src[:, span:span + length],
                                    ALU.add).then_inc(win_step, 1)
                    ws += 1
                    v.wait_ge(win_step, ws)
                    src, span = dst, 2 * span
                first = PAD - w // 2
                z_free(Z0["pv"] + j)
                v.tensor_tensor(z_buf[:, j % 2, :], src[:, first:first + T], pl_cnt[:, j // 2, :],
                                ALU.mult).then_inc(win_step, 1)
                ws += 1
                v.wait_ge(win_step, ws)
                v.tensor_tensor(z_buf[:, j % 2, :], z_buf[:, j % 2, :], pl_v[:, j % 2, PAD:PAD + T],
                                ALU.subtract).then_inc(z_ready, 1)
                lo(f_lo[:, j, :], f_hi[:, j, :].bitcast(F32), Z0["pv"] + j, j % 2)
            sum_mods(g)
            sum_mods(g + 1)
            g += 2
            for j in range(DC):
                wait_unit(v, "pl_grp", j // 2)
                wait_left(v, "pl_g", j)
                z_free(Z0["pg"] + j)
                v.scalar_tensor_tensor(z_buf[:, j % 2, :], bank[j % SLOTS][:], vec[:, V_POOL + j:V_POOL + j + 1],
                                       pl_g[:, j, :], ALU.mult, ALU.mult).then_inc(left[j % SLOTS], 1)
                lo(h_lo[:, j, :], h_hi[:, j, :].bitcast(F32), Z0["pg"] + j, j % 2)
            v.wait_ge(mod_step, steps["mod"])
            out("pl_out", 1, "n2", g=g)
            g += 2
            v.wait_ge(fr_const, 1)
            v.tensor_tensor(fr_lo[:], fr_raw, fr_hi[:].bitcast(F32), ALU.subtract).then_inc(fr_const_lo, 1)
            norm(2, ST["n2"])

            add_bias(SHIFT[2] + 2 * DC, DC)
            sum_mods(g)
            g += 1
            for n in range(8):
                part = slice((n % 2) * T, (n % 2 + 1) * T)
                v.wait_ge(ab_ready, n + 1)
                v.tensor_tensor(ab_lo[:, n // 2, part], bank[n % SLOTS][:], ab_hi[:, n // 2, part].bitcast(F32),
                                ALU.subtract).then_inc(left[n % SLOTS], 1)
            for k in range(GROUPS):
                v.wait_ge(tile_done, 8 + 3 * k + 2)
                wait_left(v, "fr_2", 3 * k)
                bv, bn = (3 * k + 1) % SLOTS, (3 * k + 2) % SLOTS
                z_free(Z0["fr"] + 2 * k)
                v.scalar_tensor_tensor(z_buf[:, 0, :], bank[bv][:], sign[:, 0:1], s_buf[:, 0, :], ALU.mult,
                                       ALU.add).then_inc(z_ready, 1)
                z_free(Z0["fr"] + 2 * k + 1)
                v.scalar_tensor_tensor(z_buf[:, 1, :], bank[bv][:], sign[:, 1:2], s_buf[:, 0, :], ALU.mult,
                                       ALU.add).then_inc(left[bv], 1)
                wait_left(v, "fr_2", 3 * k + 1)
                if k < GROUPS - 1:
                    v.wait_ge(tile_done, 8 + 3 * k + 3)
                else:
                    wait_unit(v, "fr_2", 3)
                v.tensor_copy(z_buf[0:1, 1, :], bank[bn][0:1, :]).then_inc(left[bn], 1)
                for q in range(2):
                    lo(f_lo[:, 2 * k + q, :], f_hi[:, 2 * k + q, :].bitcast(F32), Z0["fr"] + 2 * k + q, q)
            v.wait_ge(mod_step, steps["mod"])
            out("fr_out", 2, "n3", g=g)
            g += 2
            norm(3, ST["n3"])

            def ffn(layer, n, stat, g=None):
                for p, chunks in enumerate(PARTS):
                    name, z0 = f"in{layer}{p}", Z0[f"f{layer}{p}"]
                    with v.Fori(0, chunks // 2) as i:
                        if g is not None:
                            sum_mods(g, i)
                        for q in range(2):
                            wait_unit(v, name, 2 * q + 1, i)
                            wait_left(v, name, 2 * q, i)
                            z_free(z0 + q, i, 2)
                            v.tensor_tensor(z_buf[:, q, :], bank[2 * q + 1][:], s_buf[:, q, :],
                                            ALU.mult).then_inc(left[2 * q + 1], 1)
                            lo(at(f_lo, 2 * i + q), at(f_hi, 2 * i + q).bitcast(F32), z0 + q, q, i, 2)
                    if g is not None:
                        g += chunks // 2
                    if p == 0:
                        add_bias(SHIFT[n] + 2 * DC, DC)
                        v.wait_ge(mod_step, steps["mod"])
                    out(f"out{layer}{p}", n, stat if p == len(PARTS) - 1 else None, g=g)
                    if g is not None:
                        g += 2

            ffn(0, 3, "n4", g)
            norm(4, ST["n4"])
            add_bias(SHIFT[4] + 2 * DC, DC)

            SSH = SS0["h1"] - SS0["h0"]
            rot_count = {"n": 0}

            def rotary(half, h, n):
                b0, b1 = bank[2 * half], bank[2 * half + 1]
                z0 = Z0["qk0"] + 2 * half if n == 0 else Z0["qk"[half] + "1"]
                zr = ZR0["qk0"] + 2 * half if n == 0 else ZR0["qk"[half] + "1"]
                steps0 = 2 * half + 4 * n
                wait_unit(v, f"qk{n}", 2 * half + 1, h, UH)
                wait_left_own = lambda b: v.wait_ge(left[b], (RH // SLOTS) * h + (R0[f"qk{n}"] // SLOTS + 1))
                if not (n == 0 and half == 0):
                    v.wait_ge(z_ready, ZRH * h + zr_before(n, half))
                v.tensor_tensor(m_buf[:, 0, :], b0[:], rot[:, 0, :], ALU.mult).then_inc(rot_step, 1)
                v.tensor_tensor(m_buf[:, 1, :], b1[:], rot[:, 1, :], ALU.mult).then_inc(rot_step, 1)
                v.wait_ge(rot_step, 4 * h + (steps0 + 2))
                z_free(z0, h, ZH)
                v.tensor_tensor(z_buf[:, 0, :], m_buf[:, 0, :], m_buf[:, 1, :], ALU.subtract).then_inc(z_ready, 1)
                v.wait_ge(z_ready, ZRH * h + (zr + 1))
                v.tensor_tensor(m_buf[:, 0, :], b0[:], rot[:, 1, :], ALU.mult).then_inc(left[2 * half], 1)
                v.tensor_tensor(m_buf[:, 1, :], b1[:], rot[:, 0, :], ALU.mult).then_inc(left[2 * half + 1], 1)
                wait_left_own(2 * half)
                wait_left_own(2 * half + 1)
                z_free(z0 + 1, h, ZH)
                v.tensor_tensor(z_buf[:, 1, :], m_buf[:, 0, :], m_buf[:, 1, :], ALU.add).then_inc(z_ready, 1)
                for q in range(2):
                    lo(qk_lo[:, 2 * half + q, :], qk_hi[:, 2 * half + q, :].bitcast(F32), z0 + q, q, h, ZH)

            def zr_before(n, half):
                if n == 0:
                    return ZR0["qk0"] + 2
                return ZR0["q1"] if half == 0 else ZR0["k1"]

            def head_rest(h, n):
                for j in range(4):
                    v.wait_ge(vh_ready, 4 * h + (4 * n + j + 1))
                    v.tensor_tensor(v_lo[:, j, :], bank[j][:], v_hi[:, j, :].bitcast(F32),
                                    ALU.subtract).then_inc(left[j], 1)
                v.wait_ge(mask_in, 16 * h + 16 * (n + 1))
                for j in range(4):
                    v.wait_ge(tile_done, 8 * h + (TD_HEAD + 8 * n + j + 1))
                    z_free(Z0[f"p{n}"] + j, h, ZH)
                    v.tensor_tensor(z_buf[:, j % 2, :], bank[j][:], mask[:, (3 - j) * P:(3 - j) * P + T],
                                    ALU.mult).then_inc(left[j], 1)
                    lo(f_lo[:, 4 + j, :], f_hi[:, 4 + j, :].bitcast(F32), Z0[f"p{n}"] + j, j % 2, h, ZH)
                if n:
                    for j in range(DC):
                        wait_unit(v, f"ro{n - 1}", j // 2, h, UH)
                        v.scalar_tensor_tensor(x[:, j, :], bank[j % SLOTS][:], gate(4, j), x[:, j, :],
                                               ALU.mult, ALU.add).then_inc(left[j % SLOTS], 1)

            def head_sum(h):
                ss = SS0["h0m"]
                for j in range(4):
                    wait_left(v, "av0", j, h, RH)
                v.wait_ge(sum_step, SSH * h + ss)
                v.tensor_tensor(ssum[:], yh[:, 0, :], yh[:, 1, :], ALU.add).then_inc(sum_step, 1)
                for j in (2, 3):
                    v.wait_ge(sum_step, SSH * h + (ss + j - 1))
                    v.tensor_tensor(ssum[:], ssum[:], yh[:, j, :], ALU.add).then_inc(sum_step, 1)

            def head_center(h):
                v.wait_ge(mean_done, h + 2)
                for j in range(4):
                    v.scalar_tensor_tensor(yh[:, j, :], ps_bc[:], -1.0 / DV, yh[:, j, :],
                                           ALU.mult, ALU.add).then_inc(centered, 1)
                for j in range(3):
                    add_square("h0", j, h, SSH, 4)

            def head_result(h, i, z0):
                v.wait_ge(bc_done, h + (ST["h0"] + 1))
                for j in range(4):
                    v.tensor_tensor(yh[:, j, :], yh[:, j, :], ps_bc[:], ALU.mult).then_inc(scaled, 1)
                for j in range(4):
                    v.wait_ge(scaled, 4 * h + (DC + j + 1))
                    z_free(z0 + j, i, ZH)
                    v.tensor_tensor(z_buf[:, j % 2, :], yh[:, j, :], sg[:, j, :], ALU.mult).then_inc(z_ready, 1)
                    lo(f_lo[:, j, :], f_hi[:, j, :].bitcast(F32), z0 + j, j % 2, i, ZH)

            v.wait_ge(rot_in, 16)
            rotary(0, 0, 0)
            rotary(1, 0, 0)
            v.wait_ge(mod_step, steps["mod"])
            head_rest(0, 0)
            with v.Fori(0, HEADS - 1) as h:
                head_sum(h)
                rotary(0, h, 1)
                head_center(h)
                rotary(1, h, 1)
                spread(h + ST["h0"])
                head_result(h, h, Z0["y0"])
                head_rest(h, 1)
            h = HEADS - 1
            head_sum(h)
            head_center(h)
            spread(h + ST["h0"])
            head_result(h, 0, Z0[f"y{h}"])
            out(f"ro{h}", 4, "n5", per_unit=2)
            norm(5, ST["n5"])
            ffn(1, 5, "n6")
            norm(6, ST["n6"], lo=False)

        @block.tensor
        def _(pe):
            def three(out, w_h, w_l, m_h, m_l, start, stop):
                pe.matmul(out, w_h, m_h, start=start, stop=False)
                pe.matmul(out, w_h, m_l, start=False, stop=False)
                return pe.matmul(out, w_l, m_h, start=False, stop=stop)

            def bank_ready(name, n, i=0, per=SLOTS):
                before = (R0[name] + n) // SLOTS
                if not isinstance(i, int) or before:
                    pe.wait_ge(left[n % SLOTS], (per // SLOTS) * i + before)

            def unit_ready(name, n, i=0, per=SLOTS):
                pe.wait_ge(lo_done, per * i + (U0[name] + n + 1))

            def tile(s, k, a_hi, a_lo, chunks, offset=0):
                w = slice((offset + k) * P, (offset + k + 1) * P)
                return three(bank[s][:], w_hi[:, s, w], w_lo[:, s, w], a_hi[:, k, :], a_lo[:, k, :],
                             k == 0, k == chunks - 1)

            def four_tiles(name, first, a_hi, a_lo, chunks=DC, i=0, ready=None, together=SLOTS):
                done = chunks // 2 if ready else 0
                for s0 in range(0, SLOTS, together):
                    for k in range(done):
                        ready(k)
                        for s in range(s0, s0 + together):
                            if k == 0:
                                unit_ready(name, first + s, i)
                                bank_ready(name, first + s, i)
                            tile(s, k, a_hi, a_lo, chunks)
                for s in range(SLOTS):
                    if not ready:
                        unit_ready(name, first + s, i)
                        bank_ready(name, first + s, i)
                    for k in range(done, chunks):
                        if ready and s == 0:
                            ready(k)
                        last = tile(s, k, a_hi, a_lo, chunks)
                    last.then_inc(unit_used, 1)

            def h_part(n):
                return lambda k: pe.wait_ge(hl_ready, DC * n + k + 1)

            def z_part(name):
                return lambda k: pe.wait_ge(zl_ready, Z0[name] + k + 1)

            def mrow_sums(g, i=0, per=1):
                for s in range(SLOTS):
                    pe.wait_ge(mods_in[g in SECOND][s], 16 * i + (16 * place_count(g) + 16))
                if g:
                    pe.wait_ge(mrow_copied, per * i + g)
                for r in range(2):
                    for q in range(4):
                        k = 4 * r + q
                        last = pe.matmul(ps_mrow[32 * q:32 * q + 32, :], c_pad[:, k, :],
                                         mods_place(g)[:, k // 2, (k % 2) * T:(k % 2 + 1) * T],
                                         start=r == 0, stop=r == 1, tile_position=(0, 32 * q))
                last.then_inc(mrow_done, 1)

            def mcol(g, i=0, per=1):
                if g < G_SUMS:
                    pe.wait_ge(mrow_copied, per * i + (g + 1))
                else:
                    pe.wait_ge(msum_step, DC * per * i + DC * (g + 1 - G_SUMS))
                if g:
                    pe.wait_ge(mcol_copied, per * i + g)
                for j in range(4):
                    last = pe.matmul(ps_mcol[:, j:j + 1], mrow[:, j * P:(j + 1) * P], ones[:, 0:1],
                                     start=True, stop=True)
                last.then_inc(mcol_done, 1)

            def mods(g, i=0, per=1):
                mcol(g - 1, i, per)
                mrow_sums(g, i, per)

            def columns(src, start, stop):
                for j in range(4):
                    last = pe.matmul(ps_stat[:, j:j + 1], src[:, j * P:(j + 1) * P], ones[:, 0:1],
                                     start=start and j == 0, stop=stop and j == 3)
                return last

            def stat(name, i=0, per=0, per_sq=0):
                n = 4 if name[0] == "h" else DC
                pe.wait_ge(sum_step, per * i + (SS0[name] + n - 1))
                columns(ssum, True, False)
                pe.wait_ge(sq_ready, per_sq * i + (SQ0[name] + n))
                columns(sq, False, True).then_inc(stat_done, 1)

            def spread(s):
                for j in range(4):
                    pe.wait_ge(diag_ready, 4 * s + (j + 1))
                    last = pe.matmul(ps_bc[:, j * P:(j + 1) * P], ones[:], diag[:, j * P:(j + 1) * P],
                                     start=True, stop=True)
                last.then_inc(bc_done, 1)

            def mean(n):
                pe.wait_ge(sum_step, n)
                pe.matmul(ps_bc[:], ones[:], ssum[:], start=True, stop=True).then_inc(mean_done, 1)

            def out(name, a_hi, a_lo, ready, g, together=SLOTS):
                four_tiles(name, 0, a_hi, a_lo, ready=ready, together=together)
                mcol(g)
                four_tiles(name, SLOTS, a_hi, a_lo)
                mcol(g + 1)

            pe.wait_ge(c_ready, 1)
            pe.wait_ge(const_ready, 1)
            mrow_sums(0)
            for g in range(1, G_START):
                mods(g)
            mcol(G_START - 1)
            stat("n0")
            spread(0)

            g = G_START
            four_tiles("cv_ab", 0, h_hi, h_lo, ready=h_part(0))
            mrow_sums(g)
            with pe.Fori(1, 4) as i:
                four_tiles("cv_ab", 0, h_hi, h_lo, i=i)
                mods(g + 1, i - 1)
            g += G_AB
            for b in range(2):
                four_tiles("cv_g", SLOTS * b, h_hi, h_lo)
                mods(g)
                g += 1
            assert g + G_WAIT == MOD_1
            mods(g)
            mods(g + 1)
            g += G_WAIT
            mcol(g - 1)
            pe.wait_ge(cv_sum, 3)
            pe.matmul(ps_bc[:], ones[:], ssum[:], start=True, stop=False)
            for c in range(4, DC):
                pe.wait_ge(tap_done, 2 * TAPS * (c // 2 + 1) - 1 + c % 2)
                last = pe.matmul(ps_bc[:], ones[:], cv_acc[:, c, :], start=False, stop=c == DC - 1)
            last.then_inc(mean_done, 1)
            for c in range(DC // 2):
                pe.wait_ge(pair_sum, c + 1)
                columns(diag, c == 0, c == DC // 2 - 1).then_inc(stat_done if c == DC // 2 - 1 else sq_used, 1)
            spread(ST["cv"])
            out("cv_out", f_hi, f_lo, z_part("cv"), g)
            g += 2
            stat("n1")
            spread(ST["n1"])

            for name in ("pl_v", "pl_g"):
                for b in range(2):
                    four_tiles(name, SLOTS * b, h_hi, h_lo, ready=h_part(1) if (name, b) == ("pl_v", 0) else None)
                    mcol(g)
                    g += 1
            for k in range(GROUPS):
                unit_ready("pl_grp", k)
                for d in range(2):
                    bank_ready("pl_grp", 2 * k + d)
                    for c in range(2):
                        w = slice(c * GD + d * P, c * GD + (d + 1) * P)
                        pe.wait_ge(zl_ready, Z0["pv"] + 2 * k + c + 1)
                        last = three(bank[(2 * k + d) % SLOTS][:], w_hi[:, k, w], w_lo[:, k, w],
                                     f_hi[:, 2 * k + c, :], f_lo[:, 2 * k + c, :], c == 0, c == 1)
                last.then_inc(unit_used, 1)
            out("pl_out", h_hi, h_lo, z_part("pg"), g, together=2)
            g += 2
            stat("n2")
            spread(ST["n2"])

            pe.wait_ge(fr_const_lo, 1)
            for n in range(8):
                tok = slice((n // 2) * P, (n // 2 + 1) * P)
                bank_ready("fr_1", n)
                for gg in range(2):
                    for c in range(2):
                        k = 4 * (n % 2) + 2 * gg + c
                        if n < 2:
                            pe.wait_ge(hl_ready, DC * 2 + k + 1)
                        last = three(bank[n % SLOTS][:, gg * GD:(gg + 1) * GD], h_hi[:, k, tok], h_lo[:, k, tok],
                                     fr_hi[:, c, :], fr_lo[:, c, :], c == 0, c == 1)
                last.then_inc(tile_done, 1)
            mcol(g)
            g += 1
            for s in range(SLOTS):
                unit_ready("fr_2", s)
            for b in range(SLOTS):
                wait_left(pe, "fr_1", SLOTS + b)
            for k in range(GROUPS):
                for part in range(3):
                    n = 3 * k + part
                    bank_ready("fr_2", n)
                    rows = bank[n % SLOTS][0:1, :] if part == 2 else bank[n % SLOTS][:]
                    cols = slice(k * GD + P, k * GD + P + 1) if part == 2 else slice(k * GD + part * P, k * GD + (part + 1) * P)
                    for s in range(4):
                        slot, at_ = (2 if part == 1 else 0) + s // 2, slice((s % 2) * T, (s % 2 + 1) * T)
                        last = three(rows, ab_hi[:, s, cols], ab_lo[:, s, cols], w_hi[:, slot, at_],
                                     w_lo[:, slot, at_], s == 0, s == 3)
                    if n == 3 * GROUPS - 1:
                        last.then_inc(unit_used, SLOTS)
                    else:
                        last.then_inc(tile_done, 1)
            out("fr_out", f_hi, f_lo, z_part("fr"), g, together=2)
            g += 2
            stat("n3")
            spread(ST["n3"])

            def ffn(layer, n, g):
                for p, chunks in enumerate(PARTS):
                    name = f"in{layer}{p}"
                    with_mods = layer == 0
                    if p == 0:
                        four_tiles(name, 0, h_hi, h_lo, ready=h_part(n))
                        if with_mods:
                            mcol(g)
                    with pe.Fori(1 if p == 0 else 0, chunks // 2) as i:
                        four_tiles(name, 0, h_hi, h_lo, i=i)
                        if with_mods:
                            mcol(g, i)
                    if with_mods:
                        g += chunks // 2
                    four_tiles(f"out{layer}{p}", 0, f_hi, f_lo, chunks, ready=z_part(f"f{layer}{p}"),
                               together=2)
                    if with_mods:
                        mcol(g)
                    four_tiles(f"out{layer}{p}", SLOTS, f_hi, f_lo, chunks)
                    if with_mods:
                        mcol(g + 1)
                        g += 2
                return g

            ffn(0, 3, g)
            stat("n4")
            spread(ST["n4"])

            SSH = SS0["h1"] - SS0["h0"]

            def two_of_qk(h, half):
                for s in (2 * half, 2 * half + 1):
                    unit_ready("qk1", s, h, UH)
                    bank_ready("qk1", s, h, RH)
                    for k in range(DC):
                        last = tile(s, k, h_hi, h_lo, DC)
                    last.then_inc(unit_used, 1)

            def v_units(h, n, units):
                for u in units:
                    unit_ready(f"v{n}", u, h, UH)
                    for tok in range(4):
                        if u == 0:
                            bank_ready(f"v{n}", tok, h, RH)
                        for kk in range(2):
                            k, cols = 2 * u + kk, slice(tok * P, (tok + 1) * P)
                            last = three(bank[tok][:], h_hi[:, k, cols], h_lo[:, k, cols],
                                         w_hi[:, u, kk * DV:(kk + 1) * DV], w_lo[:, u, kk * DV:(kk + 1) * DV],
                                         k == 0, k == DC - 1)
                        if u == SLOTS - 1 and tok < 3:
                            last.then_inc(v_done, 1)
                    last.then_inc(unit_used, 1)

            def scores(h, n):
                z = Z0["qk0"] + 4 if n == 0 else Z0["k1"] + 2
                pe.wait_ge(zl_ready, ZH * h + z)
                for j in range(4):
                    bank_ready(f"sc{n}", j, h, RH)
                    cols = slice(j * P, (j + 1) * P)
                    for c in range(2):
                        last = three(bank[j][:], qk_hi[:, 2 + c, cols], qk_lo[:, 2 + c, cols],
                                     qk_hi[:, c, :], qk_lo[:, c, :], c == 0, c == 1)
                    last.then_inc(tile_done, 1)

            def project(h, n):
                for u in range(SLOTS):
                    unit_ready(f"ro{n}", u, h, UH)
                    for d in range(2):
                        r = 2 * u + d
                        bank_ready(f"ro{n}", r, h, RH)
                        for k in range(4):
                            w = slice((4 * d + k) * P, (4 * d + k + 1) * P)
                            last = three(bank[r % SLOTS][:], w_hi[:, u, w], w_lo[:, u, w], f_hi[:, k, :],
                                         f_lo[:, k, :], k == 0, k == 3)
                    last.then_inc(unit_used, 1)

            def gate_and_result(h, n):
                for s in range(SLOTS):
                    unit_ready(f"g{n}", s, h, UH)
                    bank_ready(f"g{n}", s, h, RH)
                    for k in range(DC):
                        last = tile(s, k, h_hi, h_lo, DC)
                    last.then_inc(unit_used, 1)
                pe.wait_ge(zl_ready, ZH * h + (Z0[f"p{n}"] + 4))
                for j in range(4):
                    bank_ready(f"av{n}", j, h, RH)
                    cols = slice(j * P, (j + 1) * P)
                    for s in range(4):
                        last = three(bank[j][:], v_hi[:, s, cols], v_lo[:, s, cols], f_hi[:, 4 + s, :],
                                     f_lo[:, 4 + s, :], s == 0, s == 3)
                    last.then_inc(tile_done, 1)

            four_tiles("qk0", 0, h_hi, h_lo, ready=h_part(4))
            v_units(0, 0, range(4))
            scores(0, 0)
            gate_and_result(0, 0)
            with pe.Fori(0, HEADS - 1) as h:
                two_of_qk(h, 0)
                mean(SSH * h + (SS0["h0m"] + 3))
                two_of_qk(h, 1)
                v_units(h, 1, range(0, 1))
                stat("h0", h, SSH, 4)
                v_units(h, 1, range(1, 2))
                spread(h + ST["h0"])
                v_units(h, 1, range(2, 4))
                scores(h, 1)
                pe.wait_ge(zl_ready, ZH * h + (Z0["y0"] + 4))
                project(h, 0)
                gate_and_result(h, 1)
            h = HEADS - 1
            mean(SS0[f"h{h}m"] + 3)
            stat(f"h{h}")
            spread(ST[f"h{h}"])
            pe.wait_ge(zl_ready, Z0[f"y{h}"] + 4)
            project(0, h)
            stat("n5")
            spread(ST["n5"])
            ffn(1, 5, None)
            stat("n6")
            spread(ST["n6"])


TD_HEAD = 8 + 3 * GROUPS - 1


def tiles_of(w):
    k, n = w.shape
    return w.reshape(k // P, P, n // P, P).transpose(2, 1, 0, 3).reshape(n // P, P, k)


def columns(v):
    return v.reshape(-1, P).T


def layout(a):
    out = {}
    out["x_t"] = a["x"][0].T.reshape(DC, P, T).transpose(1, 0, 2)
    gains = [a["norm_g"][0], a["norm_g"][1], a["norm_mix_g_2"][0], a["norm_ffn_g_2"][0],
             a["norm_mix_g_2"][1], a["norm_ffn_g_2"][1], a["final_norm_g_2"]]
    biases = [a["b_mod"].reshape(-1), a["b_ada_2"].reshape(-1), a["b_ada_final_2"]]
    out["vectors"] = np.concatenate(
        [columns(v) for v in [a["c"][0], a["c_2"][0], *biases, *gains, a["cv_dw"][0].reshape(-1), a["cv_db"][0],
                              a["cv_ln_g"][0], a["cv_ln_b"][0], a["pl_scale"][0]]], axis=1)
    mods = [w for w in (*a["w_mod"], *a["w_ada_2"], a["w_ada_final_2"])]
    out["w_mods"] = np.concatenate(
        [w.reshape(4, 2, P, -1, T).transpose(3, 0, 2, 1, 4).reshape(-1, P, 2 * T) for w in mods])
    cv = tiles_of(a["cv_w_in"][0])
    out["cv_ab"] = cv[:2 * DC].reshape(2, DC, P, D).transpose(1, 0, 2, 3).reshape(2 * DC, P, D)
    out["cv_g"] = cv[2 * DC:]
    out["cv_out"] = tiles_of(a["cv_w_out"][0])
    pl = tiles_of(a["pl_w_in"][0])
    out["pl_v"], out["pl_g"] = pl[:DC], pl[DC:]
    out["pl_grp"] = a["pl_w_grp"][0].reshape(GROUPS, 2, P, GD).transpose(0, 2, 1, 3).reshape(GROUPS, P, 2 * GD)
    out["pl_out"] = tiles_of(a["pl_w_out"][0])
    order = np.concatenate([np.r_[g * GD:g * GD + P, g * GD + P, g * GD + GD - 1:g * GD + P:-1]
                            for g in range(GROUPS)])
    out["fr_out"] = tiles_of(a["w_fourier_out_2"][0][order])
    for layer in range(2):
        gate_up = tiles_of(a["w_ffn_in_2"][layer])
        out[f"ff_in{layer}"] = gate_up.reshape(2, FC, P, D).transpose(1, 0, 2, 3).reshape(2 * FC, P, D)
        w = a["w_ffn_out_2"][layer]
        out[f"ff_out{layer}"] = np.concatenate([tiles_of(w[:8 * P]), tiles_of(w[8 * P:16 * P])])
        out[f"ff_tail{layer}"] = tiles_of(w[16 * P:])
    w_in, w_out = a["w_ret_in_2"][0], a["w_ret_out_2"][0]
    ret = []
    for h in range(HEADS):
        q, k = (tiles_of(w_in[:, o + h * DK:o + (h + 1) * DK]) for o in (0, HEADS * DK))
        v = w_in[:, 2 * HEADS * DK + h * DV:2 * HEADS * DK + (h + 1) * DV]
        v = v.reshape(4, 2, P, DV).transpose(0, 2, 1, 3).reshape(4, P, 2 * DV)
        g0 = 2 * HEADS * DK + HEADS * DV + h * DV
        o = tiles_of(w_out[h * DV:(h + 1) * DV])
        ret += [q, k, v, tiles_of(w_in[:, g0:g0 + DV]),
                o.reshape(4, 2, P, DV).transpose(0, 2, 1, 3).reshape(4, P, 2 * DV)]
    out["ret"] = np.concatenate(ret)
    return out


def tables():
    out = {}
    j, k = np.arange(GD)[:, None], np.arange(P)[None, :]
    angle = lambda a, b, n: 2 * np.pi * ((a * b) % n) / n
    ortho = 1.0 / np.sqrt(T * GD)
    feature = np.concatenate([np.cos(angle(j, k, GD)), np.cos(angle(j, P, GD)), np.sin(angle(j, k[:, 1:], GD))], 1)
    out["dft_feature"] = (feature * ortho).reshape(2, P, GD).transpose(1, 0, 2)
    s, tt = np.arange(T)[:, None], np.arange(T)[None, :]
    both = np.concatenate([np.cos(angle(s, tt, T)), np.sin(angle(s, tt, T))])
    out["dft_token"] = both.reshape(4, 2, P, T).transpose(0, 2, 1, 3).reshape(4, P, 2 * T)
    pos = np.arange(T)
    out["pl_cnt"] = np.broadcast_to(
        np.stack([1.0 / (np.clip(pos + w - w // 2, 0, T) - np.clip(pos - w // 2, 0, T)) for w in WINDOWS]),
        (P, len(WINDOWS), T))
    half = DK // 2
    inv_freq = np.float32(10000.0) ** (-np.arange(half, dtype=np.float32) / np.float32(half))
    ang = (pos.astype(np.float32)[None, :] * inv_freq[:, None]).astype(np.float64)
    out["rotary"] = np.stack([np.cos(ang), np.sin(ang)], 1)
    log_f = np.log1p(-np.exp2(-5.0 - np.arange(HEADS)))
    d = np.arange(T + 3 * P)[None, :] - 3 * P - np.arange(P)[:, None]
    out["decay"] = np.stack([np.where(d >= 0, np.exp(np.maximum(d, 0) * log_f[h]),
                                      np.exp(np.maximum(-d, 0) * log_f[HEADS - 1 - h])) for h in range(HEADS)]) * DK ** -0.5
    return {n: np.ascontiguousarray(v, dtype=np.float32) for n, v in out.items()}


def kernel(**inputs):
    import concourse.bacc as bacc
    from concourse.bass_utils import run_bass_kernel_spmd

    arrays = {n: np.ascontiguousarray(v) for n, v in layout({k: np.asarray(v) for k, v in inputs.items()}).items()}
    arrays.update(tables())
    nc = bacc.Bacc("TRN2", target_bir_lowering=False, num_devices=1)
    t = {n: nc.dram_tensor(n + "_in", v.shape, F32, kind="ExternalInput").ap() for n, v in arrays.items()}
    t["y_t"] = nc.dram_tensor("y_t", (P, DC, T), F32, kind="ExternalOutput").ap()
    build_program(nc, t)
    y = run_bass_kernel_spmd(nc, [{n + "_in": v for n, v in arrays.items()}], core_ids=[0]).results[0]["y_t"]
    return np.ascontiguousarray(y.transpose(1, 0, 2).reshape(D, T).T[None])
```

```python
from contextlib import ExitStack

import numpy as np

import concourse.bass as bass
from concourse import mybir

F32 = mybir.dt.float32
F32R = mybir.dt.float32r
ALU = mybir.AluOpType
ACT = mybir.ActivationFunctionType

P = 128
T = 512
D = 1024
DC = D // P
EPS = 1e-6
TAPS = 31
HALO = TAPS // 2
ROW = T + 2 * HALO
WINDOWS = (2, 4, 8, 16)
PAD = WINDOWS[-1] // 2
GROUPS = 4
GD = D // GROUPS
HEADS = 4
DK = D // HEADS
DV = 2 * DK
FF = -(-8 * D // (3 * 256)) * 256
FC = FF // P
PARTS = (8, 8, FC - 16)
SLOTS = 4
UNIT = 1024

MOD_COLS = 20 * DC
MOD_GROUPS = MOD_COLS // 4
MOD_1 = 12
V_C = 0
V_BIAS = V_C + 2 * DC
V_GAIN = V_BIAS + MOD_COLS
V_DW = V_GAIN + 7 * DC
V_DB = V_DW + TAPS * DC
V_LNG = V_DB + DC
V_LNB = V_LNG + DC
V_POOL = V_LNB + DC
V_COLS = V_POOL + DC

DVE_CHUNKS = ((0,), (2, 3), (4, 5), (6, 7))
POOL_TAPS = 6
ACT_TAPS = 13

BUSY = {"std": 1, "norm": 2, "conv": 6, "squares": 3, "layer norm": 4, "first norm": 4}

SHIFT = [3 * DC * n for n in range(7)]

G_START, G_AB, G_GATE, G_WAIT = 4, 4, 2, 2
W_FIRST = G_START + G_AB + G_GATE
G_SUMS = W_FIRST + G_WAIT


SECOND = [g for g in range(G_START) if g % 2] + [W_FIRST]


def product_of(c, m):
    return m - 1 if c == 1 else TAPS - 1 + (c - 6) * (POOL_TAPS - 1) + m - 1


def sums_before(c, m):
    n = product_of(c, m) - 2
    if n < TAPS - 1:
        return n + 2
    return TAPS + (n - (TAPS - 1)) // (POOL_TAPS - 1) + 1 + (n - (TAPS - 1)) + 1


def place_count(g):
    return sum((n in SECOND) == (g in SECOND) for n in range(g))


def place_before(g):
    return max((n + 1 for n in range(g) if (n in SECOND) == (g in SECOND)), default=None)


def starts(parts):
    at, found = 0, {}
    for name, n in parts:
        found[name] = at
        at += n
    return found, at


def head_order(of):
    out = []
    for h in range(HEADS):
        out += [of("qk", h), of("v", h), of("sc", h)]
        if h:
            out.append(of("ro", h - 1))
        out += [of("g", h), of("av", h)] if h < HEADS - 1 else [of("av", h), of("g", h)]
    return out + [of("ro", HEADS - 1)]


def both_ffn(layer, n_in, n_out):
    return [x for p, n in enumerate(PARTS)
            for x in ((f"in{layer}{p}", n_in(n)), (f"out{layer}{p}", n_out))]


U0, N_UNITS = starts(
    [("cv_ab", 16), ("cv_g", 8), ("cv_out", 8), ("pl_v", 8), ("pl_g", 8), ("pl_grp", 4), ("pl_out", 8),
     ("fr_2", 4), ("fr_out", 8)] + both_ffn(0, lambda n: 2 * n, 8)
    + head_order(lambda kind, h: (f"{kind}{h}", 0 if kind in ("sc", "av") else 4))
    + both_ffn(1, lambda n: 2 * n, 8))
R0, _ = starts(
    [("cv_ab", 16), ("cv_g", 8), ("cv_out", 8), ("pl_v", 8), ("pl_g", 8), ("pl_grp", 8), ("pl_out", 8),
     ("fr_1", 8), ("fr_2", 12), ("fr_out", 8)] + both_ffn(0, lambda n: 2 * n, 8)
    + head_order(lambda kind, h: (f"{kind}{h}", 8 if kind == "ro" else 4))
    + both_ffn(1, lambda n: 2 * n, 8))
assert all(v % SLOTS == 0 for v in (*U0.values(), *R0.values()))
UH, RH = U0["qk2"] - U0["qk1"], R0["qk2"] - R0["qk1"]

ffn_z = lambda layer: [(f"f{layer}{p}", n) for p, n in enumerate(PARTS)]
Z0, _ = starts(
    [("cv", 8), ("pv", 8), ("pg", 8), ("fr", 8)] + ffn_z(0) + [("qk0", 4), ("p0", 4)]
    + [x for h in range(1, HEADS) for x in ((f"q{h}", 2), (f"k{h}", 2), (f"y{h - 1}", 4), (f"p{h}", 4))]
    + [(f"y{HEADS - 1}", 4)] + ffn_z(1))
ZH = Z0["q2"] - Z0["q1"]
ZR0, _ = starts(
    [("cv", 8), ("pv", 8), ("fr", 4), ("qk0", 4)]
    + [x for h in range(1, HEADS) for x in ((f"q{h}", 2), (f"k{h}", 2), (f"y{h - 1}", 4))]
    + [(f"y{HEADS - 1}", 4)])
ZRH = ZR0["q2"] - ZR0["q1"]

STATS = ["n0", "cv", "n1", "n2", "n3", "n4"] + [f"h{h}" for h in range(HEADS)] + ["n5", "n6"]
ST = {name: i for i, name in enumerate(STATS)}
SS0, _ = starts([x for s in STATS if s != "cv" for x in (
    [(s + "m", 3), (s, 3)] if s[0] == "h" else [(s, DC - 1)])])
SQ0, _ = starts([(s, 4 if s[0] == "h" else DC) for s in STATS])


def build_program(nc, t):
    with ExitStack() as ctx:
        sem = lambda name: ctx.enter_context(nc.semaphore(name))
        sb = lambda name, shape, dt=F32: ctx.enter_context(nc.sbuf_tensor(name, shape, dt))

        w_raw = sb("w_raw", [P, SLOTS, UNIT])
        w_hi = sb("w_hi", [P, SLOTS, UNIT], F32R)
        w_lo = sb("w_lo", [P, SLOTS, UNIT], F32R)
        x = sb("x", [P, DC, T])
        h_hi = sb("h_hi", [P, DC, T], F32R)
        h_lo = sb("h_lo", [P, DC, T], F32R)
        f_hi = sb("f_hi", [P, 8, T], F32R)
        f_lo = sb("f_lo", [P, 8, T], F32R)
        sq = sb("sq", [P, T])
        ssum = sb("ssum", [P, T])
        diag = sb("diag", [P, T])
        mrow = sb("mrow", [P, T])
        ident = sb("ident", [P, P])
        ones = sb("ones", [P, P])
        vec = sb("vec", [P, V_COLS])
        c_pad = sb("c_pad", [P, DC, 32])
        c_2 = sb("c_2", [P, DC])
        mraw = sb("mraw", [P, MOD_COLS])
        mod = sb("mod", [P, MOD_COLS])
        aff = sb("aff", [P, DC])
        stdev = sb("stdev", [P, 4])
        rstd = sb("rstd", [P, 4])
        eps = sb("eps", [P, 1])
        spare = sb("spare", [P, 1])
        sign = sb("sign", [P, 2])

        def phase(*parts):
            with ExitStack() as s:
                return [s.enter_context(nc.sbuf_tensor(n, shape, dt)) for n, shape, dt in parts]

        mods_ring, = phase(("mods_ring", [P, SLOTS, UNIT], F32))
        _, cv_y, cv_acc, cv_g = phase(
            ("under_cv", [P, SLOTS * UNIT], F32), ("cv_y", [P, DC * ROW], F32),
            ("cv_acc", [P, DC, T], F32), ("cv_g", [P, DC, T], F32))
        _, m_buf, z_buf, s_buf, pl_v, pl_s, pl_cnt, pl_g = phase(
            ("under_pl", [P, SLOTS * UNIT], F32),
            ("m_buf", [P, 2, T], F32), ("z_buf", [P, 2, T], F32), ("s_buf", [P, 2, T], F32),
            ("pl_v", [P, 2, T + 2 * PAD], F32), ("pl_s", [P, 2, T + 2 * PAD], F32),
            ("pl_cnt", [P, len(WINDOWS), T], F32), ("pl_g", [P, DC, T], F32))
        mods_place = lambda g: (mods_ring if g not in SECOND else w_raw if g >= G_START else
                                cv_acc[:].rearrange("p (s c) n -> p s (c n)", s=SLOTS))
        fr_raw = s_buf[:, 1, :].rearrange("p (k n) -> p k n", k=2)
        _, _, fr_hi, fr_lo, ab_hi, ab_lo = phase(
            ("under_fr", [P, SLOTS * UNIT], F32), ("beside_fr", [P, 6 * T], F32),
            ("fr_hi", [P, 2, GD], F32R), ("fr_lo", [P, 2, GD], F32R),
            ("ab_hi", [P, 4, D], F32R), ("ab_lo", [P, 4, D], F32R))
        yh, sg, _, rot, mask, qk_hi, qk_lo, v_hi, v_lo = phase(
            ("yh", [P, 4, T], F32), ("sg", [P, 4, T], F32), ("beside_ret", [P, 4 * T], F32),
            ("rot", [P, 2, T], F32), ("mask", [P, T + 3 * P], F32),
            ("qk_hi", [P, 4, T], F32R), ("qk_lo", [P, 4, T], F32R),
            ("v_hi", [P, 4, DV], F32R), ("v_lo", [P, 4, DV], F32R))

        ps = lambda name: ctx.enter_context(nc.psum_tensor(name, [P, T], F32))
        bank = [ps(f"bank{b}") for b in range(SLOTS)]
        ps_stat, ps_bc, ps_mcol, ps_mrow = ps("ps_stat"), ps("ps_bc"), ps("ps_mcol"), ps("ps_mrow")

        raw_in = [sem(f"raw_in{s}") for s in range(SLOTS)]
        mods_in = [[sem(f"mods_in{s}") for s in range(SLOTS)], [sem(f"mods_odd_in{s}") for s in range(SLOTS)]]
        vec_in, x_in, cnt_in, fr_in, rot_in, mask_in, y_out = (
            sem(n) for n in ("vec_in", "x_in", "cnt_in", "fr_in", "rot_in", "mask_in", "y_out"))
        hi_done = sem("hi_done")
        lo_done = sem("lo_done")
        unit_used = sem("unit_used")
        tile_done = sem("tile_done")
        left = [sem(f"left_bank{b}") for b in range(SLOTS)]
        zeroed, const_ready, c_ready = sem("zeroed"), sem("const_ready"), sem("c_ready")
        mrow_done, mrow_copied = sem("mrow_done"), sem("mrow_copied")
        mcol_done, mcol_copied = sem("mcol_done"), sem("mcol_copied")
        msum_step = sem("msum_step")
        mod_step = sem("mod_step")
        sq_ready, sum_step, sq_used = sem("sq_ready"), sem("sum_step"), sem("sq_used")
        pair_sum = sem("pair_sum")
        pool_tap = sem("pool_tap")
        product_ready = sem("product_ready")
        v_done = sem("v_done")
        stat_done, std_ready, rstd_ready, diag_ready, bc_done, mean_done, centered, scaled = (
            sem(n) for n in ("stat_done", "std_ready", "rstd_ready", "diag_ready", "bc_done", "mean_done",
                             "centered", "scaled"))
        m_ready, hh_ready, hl_ready = sem("m_ready"), sem("hh_ready"), sem("hl_ready")
        z_ready, zh_ready, zl_ready = sem("z_ready"), sem("zh_ready"), sem("zl_ready")
        halo_ready, y_ready, tap_done, ln_silu = sem("halo_ready"), sem("y_ready"), sem("tap_done"), sem("ln_silu")
        win_step, fr_const, fr_const_lo, ab_ready, vh_ready, rot_step = (
            sem(n) for n in ("win_step", "fr_const", "fr_const_lo", "ab_ready", "vh_ready", "rot_step"))
        out_ready = sem("out_ready")

        def wait_unit(eng, name, n, i=0, per=SLOTS):
            eng.wait_ge(unit_used, per * i + (U0[name] + n + 1))

        def wait_left(eng, name, n, i=0, per=SLOTS):
            eng.wait_ge(left[n % SLOTS], (per // SLOTS) * i + ((R0[name] + n) // SLOTS + 1))

        def at(buf, i):
            return buf[:, i, :] if isinstance(i, int) else buf[:, bass.ds(i, 1), :].rearrange("p a n -> p (a n)")

        block = ctx.enter_context(nc.Block())

        @block.sync
        def _(sp):
            def four(name, a, first, width=UNIT, i=0, per_u=SLOTS, per_a=SLOTS, fresh=False):
                for s in range(SLOTS):
                    if not fresh:
                        sp.wait_ge(lo_done, per_u * i + (U0[name] + s + 1 - SLOTS))
                    src = a[bass.ds(per_a * i + (first + s), 1)].rearrange("a p n -> p (a n)")
                    sp.dma_start(w_raw[:, s, 0:width], src).then_inc(raw_in[s], 16)

            def later(name, n):
                U0[f"{name}+{n}"] = U0[name] + SLOTS * n
                return f"{name}+{n}"

            def mods(g, i=0, per=1):
                if g > G_SUMS:
                    sp.wait_ge(msum_step, DC * per * i + DC * (g - G_SUMS))
                elif place_before(g):
                    sp.wait_ge(mrow_done, per * i + place_before(g))
                for s in range(SLOTS):
                    src = t["w_mods"][bass.ds(SLOTS * per * i + (SLOTS * g + s), 1)].rearrange("a p n -> p (a n)")
                    sp.dma_start(mods_place(g)[:, s, :], src).then_inc(mods_in[g in SECOND][s], 16)

            sp.dma_start(vec[:], t["vectors"]).then_inc(vec_in, 16)
            mods(0)
            mods(1)
            sp.dma_start(x[:], t["x_t"]).then_inc(x_in, 16)
            for g in range(2, G_START):
                mods(g)
            g = G_START
            four("cv_ab", t["cv_ab"], 0, fresh=True)
            mods(g)
            with sp.Fori(1, 4) as i:
                four("cv_ab", t["cv_ab"], 0, i=i)
                mods(g + 1, i - 1)
            g += G_AB
            for b in range(2):
                four(later("cv_g", b), t["cv_g"], SLOTS * b)
                mods(g + b)
            g += G_GATE
            sp.wait_ge(lo_done, U0["cv_out"])
            mods(g)
            mods(g + 1)
            sp.wait_ge(mrow_done, W_FIRST + 1)
            g += G_WAIT
            for b in range(2):
                four(later("cv_out", b), t["cv_out"], SLOTS * b, fresh=b == 0)
                mods(g + b)
            g += 2
            for name in ("pl_v", "pl_g"):
                for b in range(2):
                    four(later(name, b), t[name], SLOTS * b)
                    if (name, b) == ("pl_v", 0):
                        sp.wait_ge(zl_ready, Z0["cv"] + DC)
                        sp.dma_start(pl_cnt[:], t["pl_cnt"]).then_inc(cnt_in, 16)
                        sp.dma_start(fr_raw, t["dft_feature"]).then_inc(fr_in, 16)
                    mods(g + b)
                g += 2
            four("pl_grp", t["pl_grp"], 0, width=2 * GD)
            for b in range(2):
                four(later("pl_out", b), t["pl_out"], SLOTS * b)
                mods(g + b)
            g += 2
            four("fr_2", t["dft_token"], 0)
            mods(g)
            g += 1
            for b in range(2):
                four(later("fr_out", b), t["fr_out"], SLOTS * b)
                mods(g + b)
            g += 2

            def ffn(layer, g):
                first_in = 0
                for p, n in enumerate(PARTS):
                    with sp.Fori(0, n // 2) as i:
                        four(f"in{layer}{p}", t[f"ff_in{layer}"], first_in, i=i)
                        if layer == 0:
                            mods(g, i)
                    if layer == 0:
                        g += n // 2
                    first_in += 2 * n
                    src, first_out = (t[f"ff_out{layer}"], 8 * p) if n == 8 else (t[f"ff_tail{layer}"], 0)
                    with sp.Fori(0, 2) as i:
                        four(f"out{layer}{p}", src, first_out, width=n * P, i=i)
                        if layer == 0:
                            mods(g, i)
                    if layer == 0:
                        g += 2
                return g

            g = ffn(0, g)
            assert g == MOD_GROUPS, g

            def mask_load(h):
                sp.dma_start(mask[:], t["decay"][bass.ds(h, 1)].rearrange("a p n -> p (a n)")).then_inc(mask_in, 16)

            sp.wait_ge(zl_ready, Z0["f02"] + PARTS[2])
            sp.dma_start(rot[:], t["rotary"]).then_inc(rot_in, 16)
            mask_load(0)
            four("qk0", t["ret"], 0)
            four("v0", t["ret"], 4)
            four("g0", t["ret"], 8)
            with sp.Fori(0, HEADS - 1) as h:
                four("qk1", t["ret"], 16, i=h, per_u=UH, per_a=16)
                sp.wait_ge(zl_ready, ZH * h + (Z0["p0"] + 4))
                mask_load(h + 1)
                four("v1", t["ret"], 20, i=h, per_u=UH, per_a=16)
                four("ro0", t["ret"], 12, i=h, per_u=UH, per_a=16)
                four("g1", t["ret"], 24, i=h, per_u=UH, per_a=16)
            four(f"ro{HEADS - 1}", t["ret"], 16 * (HEADS - 1) + 12)
            ffn(1, g)
            for c in range(DC):
                sp.wait_ge(out_ready, c + 1)
                sp.dma_start(t["y_t"][:, c, :], x[:, c, :]).then_inc(y_out, 16)
            sp.wait_ge(y_out, 16 * DC)

        @block.gpsimd
        def _(pool):
            pool.memset(ident[:], 0.0)
            pool.memset(ones[:], 1.0)
            pool.memset(eps[:], EPS)
            pool.memset(sign[:, 0:1], -1.0)
            pool.memset(sign[:, 1:2], 1.0)
            pool.memset(c_pad[:], 0.0).then_inc(zeroed, 1)
            pool.wait_ge(zeroed, 1)
            pool.memset(sign[0:1, :], 0.0)
            pool.affine_select(out=ident[:], in_=ident[:], compare_op=ALU.not_equal, fill=1.0, base=0,
                               pattern=[[-1, P]], channel_multiplier=1).then_inc(const_ready, 1)

            def lo_part(u, s):
                pool.wait_ge(hi_done, u + 1)
                pool.tensor_tensor(w_lo[:, s, :], w_raw[:, s, :], w_hi[:, s, :].bitcast(F32),
                                   ALU.subtract).then_inc(lo_done, 1)

            for u in range(SLOTS):
                lo_part(u, u)
            pool.wait_ge(hl_ready, DC)
            rows = cv_y[:].rearrange("p (c n) -> p c n", c=DC)
            pool.memset(rows[:, :, 0:HALO], 0.0)
            pool.memset(rows[:, :, HALO + T:ROW], 0.0).then_inc(halo_ready, 1)

            def y_and_lo_parts(i, k):
                for q in range(2):
                    if q:
                        lo_part(SLOTS * i + 5, 1)
                    lo_part(SLOTS * i + (4 + 2 * q), 2 * q)
                    wait_left(pool, "cv_ab", 2 * q, i)
                    wait_left(pool, "cv_ab", 2 * q + 1, i)
                    at_y = (2 * i + q) * ROW + HALO
                    pool.tensor_tensor(cv_y[:, at_y:at_y + T], cv_g[:, 2 * q, :], cv_g[:, 2 * q + 1, :],
                                       ALU.mult).then_inc(y_ready, 1)
                    if i:
                        for m in range(2):
                            tap(k + 2 * q + m)
                lo_part(SLOTS * i + 7, 3)

            def tap(k):
                product = (sq, diag)[(k - 1) % 2]
                if k < ACT_TAPS:
                    pool.wait_ge(pool_tap, k)
                    pool.tensor_scalar(product[:], cv_y[:, ROW + k:ROW + k + T],
                                       vec[:, V_DW + DC * k + 1:V_DW + DC * k + 2], None,
                                       ALU.mult).then_inc(product_ready, 1)
                pool.wait_ge(product_ready, k)
                if k >= ACT_TAPS:
                    pool.wait_ge(pool_tap, k)
                pool.tensor_tensor(cv_acc[:, 1, :], cv_acc[:, 1, :], product[:], ALU.add).then_inc(pool_tap, 1)

            y_and_lo_parts(0, 0)
            pool.wait_ge(y_ready, 2)
            pool.tensor_scalar(cv_acc[:, 1, :], cv_y[:, ROW:ROW + T], vec[:, V_DW + 1:V_DW + 2],
                               vec[:, V_DB + 1:V_DB + 2], ALU.mult, ALU.add).then_inc(pool_tap, 1)
            for i in range(1, 4):
                y_and_lo_parts(i, 4 * i - 3)
            first = U0["cv_g"]
            for q in range(2):
                lo_part(first + SLOTS + 2 * q, 2 * q)
                lo_part(first + SLOTS + 2 * q + 1, 2 * q + 1)
                for m in range(4):
                    tap(ACT_TAPS + 4 * q + m)
            for k in range(ACT_TAPS + 8, TAPS):
                tap(k)
            pool.wait_ge(tap_done, 2 * TAPS)
            steps = TAPS
            for c in (6, 7):
                part = cv_y[:, (c - 6) * ROW:(c - 6) * ROW + T]
                pool.wait_ge(pool_tap, TAPS)
                pool.wait_ge(y_ready, c + 1)
                pool.tensor_scalar(part, cv_y[:, c * ROW:c * ROW + T], vec[:, V_DW + c:V_DW + c + 1], None,
                                   ALU.mult).then_inc(pool_tap, 1)
                for m in range(1, POOL_TAPS):
                    steps += 1
                    n = product_of(c, m)
                    pool.wait_ge(product_ready, n + 1)
                    pool.wait_ge(pool_tap, steps)
                    pool.tensor_tensor(part, part, (sq, diag)[n % 2][:], ALU.add).then_inc(pool_tap, 1)
                steps += 1
            first = U0["cv_out"]
            with pool.Fori(0, (N_UNITS - first) // SLOTS) as i:
                for s in range(SLOTS):
                    lo_part(SLOTS * i + (first + s), s)

        @block.scalar
        def _(act):
            def refill(name, s, i=0, per=SLOTS):
                u = U0[name] + s + SLOTS
                if u >= N_UNITS:
                    return
                act.wait_ge(raw_in[u % SLOTS], 16 * (per // SLOTS) * i + 16 * (u // SLOTS + 1))
                act.wait_ge(unit_used, per * i + (u + 1 - SLOTS))
                act.activation(w_hi[:, u % SLOTS, :], w_raw[:, u % SLOTS, :], ACT.Copy).then_inc(hi_done, 1)

            def mods(g):
                mcol(g - 1)
                act.wait_ge(mrow_done, g + 1)
                act.activation(mrow[:], ps_mrow[:], ACT.Copy).then_inc(mrow_copied, 1)

            def mcol(g):
                act.wait_ge(mcol_done, g + 1)
                if isinstance(g, int):
                    dst = mraw[:, 4 * g:4 * g + 4]
                else:
                    act.wait_ge(const_ready, 1)
                    dst = mraw[:, bass.ds(4 * g, 4)]
                act.activation(dst, ps_mcol[:, 0:4], ACT.Copy).then_inc(mcol_copied, 1)

            def square(stat, c, src, i=0, per=0):
                if SS0[stat] + c:
                    act.wait_ge(sum_step, per * i + (SS0[stat] + c))
                if c == 0 and ST[stat]:
                    act.wait_ge(stat_done, i + ST[stat])
                act.activation(sq[:], src, ACT.Square).then_inc(sq_ready, 1)

            def load_table(function):
                act.activation(spare[:], eps[:], function)

            def std(stat, n):
                act.wait_ge(stat_done, stat + 1)
                act.wait_ge(const_ready, 1)
                act.activation(stdev[:], ps_stat[:, 0:4], ACT.Sqrt, bias=eps[:], scale=1.0 / n).then_inc(std_ready, 1)

            def norm(n):
                for c in range(DC):
                    act.wait_ge(m_ready, DC * n + c + 1)
                    act.activation(h_hi[:, c, :], m_buf[:, c % 2, :], ACT.Identity,
                                   bias=mod[:, SHIFT[n] + c:SHIFT[n] + c + 1]).then_inc(hh_ready, 1)

            def hi(dst, q):
                act.activation(dst, z_buf[:, q, :], ACT.Copy).then_inc(zh_ready, 1)

            def out(name, stat, g=None):
                for j in range(DC):
                    if stat is not None:
                        if j == 0:
                            load_table(ACT.Sqrt)
                        wait_left(act, name, j)
                        square(stat, j, x[:, j, :])
                    refill(name, j)
                    if g is not None and j % SLOTS == SLOTS - 1:
                        mcol(g)
                        g += 1
                return g

            act.wait_ge(const_ready, 1)
            act.wait_ge(vec_in, 16)
            act.activation(c_2[:], vec[:, V_C + DC:V_C + 2 * DC], ACT.Silu)
            act.activation(c_pad[:, :, 0], vec[:, V_C:V_C + DC], ACT.Silu).then_inc(c_ready, 1)
            act.wait_ge(mrow_done, 1)
            act.activation(mrow[:], ps_mrow[:], ACT.Copy).then_inc(mrow_copied, 1)
            mods(1)
            load_table(ACT.Sqrt)
            act.wait_ge(x_in, 16)
            for c in range(DC):
                square("n0", c, x[:, c, :])
            for g in range(2, G_START):
                mods(g)
                if g == 2:
                    std(ST["n0"], D)
            mcol(G_START - 1)
            for u in range(SLOTS):
                act.wait_ge(raw_in[u], 16)
                act.activation(w_hi[:, u, :], w_raw[:, u, :], ACT.Copy).then_inc(hi_done, 1)
            norm(0)

            def ab(i):
                for q in range(2):
                    wait_unit(act, "cv_ab", 2 * q, i)
                    if not isinstance(i, int):
                        act.wait_ge(y_ready, 2 * i + (q - 1))
                    act.activation(cv_g[:, 2 * q, :], bank[2 * q][:], ACT.Copy).then_inc(left[2 * q], 1)
                    refill("cv_ab", 2 * q, i)
                    wait_unit(act, "cv_ab", 2 * q + 1, i)
                    act.activation(cv_g[:, 2 * q + 1, :], bank[2 * q + 1][:], ACT.Sigmoid).then_inc(left[2 * q + 1], 1)
                    refill("cv_ab", 2 * q + 1, i)

            g = G_START
            ab(0)
            act.wait_ge(mrow_done, g + 1)
            act.activation(mrow[:], ps_mrow[:], ACT.Copy).then_inc(mrow_copied, 1)
            with act.Fori(1, 4) as i:
                ab(i)
                mods(i + g)
            g += G_AB
            act.wait_ge(y_ready, DC)

            def products(k, n, c=1):
                for m in range(k, k + n):
                    act.wait_ge(pool_tap, sums_before(c, m))
                    if (c, m) == (1, ACT_TAPS):
                        act.wait_ge(product_ready, ACT_TAPS - 1)
                    act.activation((sq, diag)[product_of(c, m) % 2][:], cv_y[:, c * ROW + m:c * ROW + m + T], ACT.Copy,
                                   scale=vec[:, V_DW + DC * m + c:V_DW + DC * m + c + 1]).then_inc(product_ready, 1)

            for j in range(DC):
                wait_unit(act, "cv_g", j)
                act.activation(cv_g[:, j, :], bank[j % SLOTS][:], ACT.Silu).then_inc(left[j % SLOTS], 1)
                if j < SLOTS:
                    refill("cv_g", j)
                else:
                    products(ACT_TAPS + 2 * j, 2)
                if j == 1:
                    products(ACT_TAPS, 4)
                if j == 3:
                    products(ACT_TAPS + 4, 4)
                if j % SLOTS == SLOTS - 1:
                    mods(g)
                    g += 1
            products(TAPS - 2, 2)
            mods(g)
            products(1, POOL_TAPS - 1, 6)
            mods(g + 1)
            products(1, POOL_TAPS - 1, 7)
            g += G_WAIT
            mcol(g - 1)
            for j in range(SLOTS, DC):
                refill("cv_g", j)
            load_table(ACT.Sqrt)
            act.wait_ge(mean_done, 1)
            for c in range(DC):
                act.wait_ge(centered, c + 1)
                if c >= 2:
                    act.wait_ge(pair_sum, c // 2)
                act.activation((sq, ssum)[c % 2][:], cv_acc[:, c, :], ACT.Square).then_inc(sq_ready, 1)
            std(ST["cv"], D)
            load_table(ACT.Silu)
            for c in range(DC + 1):
                if c < DC:
                    act.wait_ge(scaled, c + 1)
                    act.activation(cv_acc[:, c, :], cv_acc[:, c, :], ACT.Silu, bias=vec[:, V_LNB + c:V_LNB + c + 1],
                                   scale=vec[:, V_LNG + c:V_LNG + c + 1]).then_inc(ln_silu, 1)
                if c:
                    act.wait_ge(z_ready, ZR0["cv"] + c)
                    hi(f_hi[:, c - 1, :], (c - 1) % 2)
            g = out("cv_out", "n1", g)
            std(ST["n1"], D)
            norm(1)

            for j in range(DC):
                wait_unit(act, "pl_v", j)
                if j < 2:
                    act.wait_ge(win_step, 1)
                else:
                    act.wait_ge(z_ready, ZR0["pv"] + j - 1)
                act.activation(pl_v[:, j % 2, PAD:PAD + T], bank[j % SLOTS][:], ACT.Copy).then_inc(left[j % SLOTS], 1)
                refill("pl_v", j)
                act.wait_ge(z_ready, ZR0["pv"] + j + 1)
                hi(f_hi[:, j, :], j % 2)
                if j % SLOTS == SLOTS - 1:
                    mcol(g)
                    g += 1
            for j in range(DC):
                wait_unit(act, "pl_g", j)
                act.activation(pl_g[:, j, :], bank[j % SLOTS][:], ACT.Silu).then_inc(left[j % SLOTS], 1)
                refill("pl_g", j)
                if j % SLOTS == SLOTS - 1:
                    mcol(g)
                    g += 1
            for j in range(DC):
                wait_left(act, "pl_grp", j)
                hi(h_hi[:, j, :], j % 2)
                if j % 2:
                    refill("pl_grp", j // 2)
            g = out("pl_out", "n2", g)
            act.wait_ge(fr_in, 16)
            act.activation(fr_hi[:], fr_raw, ACT.Copy).then_inc(fr_const, 1)
            std(ST["n2"], D)
            norm(2)

            for n in range(8):
                act.wait_ge(tile_done, n + 1)
                act.activation(ab_hi[:, n % 4, (n // 4) * T:(n // 4 + 1) * T], bank[n % SLOTS][:],
                               ACT.Copy).then_inc(ab_ready, 1)
            for k in range(GROUPS):
                act.wait_ge(tile_done, 8 + 3 * k + 1)
                if k:
                    wait_left(act, "fr_2", 3 * k - 1)
                else:
                    act.wait_ge(fr_const_lo, 1)
                act.activation(s_buf[:, 0, :], bank[3 * k % SLOTS][:], ACT.Copy).then_inc(left[3 * k % SLOTS], 1)
                if k == GROUPS - 1:
                    mcol(g)
                    g += 1
                    refill("fr_2", 0)
                    refill("fr_2", 1)
                act.wait_ge(z_ready, ZR0["fr"] + k + 1)
                hi(f_hi[:, 2 * k, :], 0)
                wait_left(act, "fr_2", 3 * k + 1)
                hi(f_hi[:, 2 * k + 1, :], 1)
            refill("fr_2", 2)
            refill("fr_2", 3)
            g = out("fr_out", "n3", g)
            std(ST["n3"], D)
            norm(3)

            def ffn(layer, g, stat):
                for p, n in enumerate(PARTS):
                    name = f"in{layer}{p}"
                    with_mods = layer == 0
                    with act.Fori(0, n // 2) as i:
                        for q in range(2):
                            wait_unit(act, name, 2 * q, i)
                            act.wait_ge(left[2 * q + 1], i + R0[name] // SLOTS)
                            act.activation(s_buf[:, q, :], bank[2 * q][:], ACT.Silu).then_inc(left[2 * q], 1)
                            refill(name, 2 * q, i)
                            wait_left(act, name, 2 * q + 1, i)
                            act.wait_ge(const_ready, 1)
                            hi(at(f_hi, 2 * i + q), q)
                            refill(name, 2 * q + 1, i)
                        if with_mods:
                            mcol(i + g)
                    if with_mods:
                        g += n // 2
                    g = out(f"out{layer}{p}", stat if p == len(PARTS) - 1 else None, g if with_mods else None)
                return g

            ffn(0, g, "n4")
            std(ST["n4"], D)
            norm(4)

            def v_and_scores(h, n, first_refill):
                for s in range(first_refill, 3):
                    refill(f"v{n}", s, h, UH)
                for j in range(4):
                    if j < 3:
                        act.wait_ge(v_done, 3 * h + (3 * n + j + 1))
                    else:
                        wait_unit(act, f"v{n}", 3, h, UH)
                    act.activation(v_hi[:, j, :], bank[j][:], ACT.Copy).then_inc(vh_ready, 1)
                refill(f"v{n}", 3, h, UH)
                for j in range(4):
                    wait_left(act, f"sc{n}", j, h, RH)
                    hi(f_hi[:, 4 + j, :], j % 2)

            def gate_silu(name, s, h=0):
                wait_unit(act, name, s, h, UH)
                act.activation(sg[:, s, :], bank[s][:], ACT.Silu).then_inc(left[s], 1)
                refill(name, s, h, UH)

            def copy_result(h):
                for j in range(4):
                    act.wait_ge(tile_done, 8 * h + (TD_HEAD + 4 + j + 1))
                    act.activation(yh[:, j, :], bank[j][:], ACT.Copy).then_inc(left[j], 1)

            def head_squares(h):
                for j in range(4):
                    act.wait_ge(centered, 4 * h + (DC + j + 1))
                    square("h0", j, yh[:, j, :], h, SS0["h1"] - SS0["h0"])

            for s in range(SLOTS):
                refill("qk0", s)
            for j in range(4):
                act.wait_ge(z_ready, ZR0["qk0"] + j + 1)
                hi(qk_hi[:, j, :], j % 2)
            v_and_scores(0, 0, 0)
            with act.Fori(0, HEADS - 1) as h:
                for s in range(SLOTS):
                    gate_silu("g0", s, h)
                copy_result(h)
                refill("qk1", 0, h, UH)
                head_squares(h)
                refill("qk1", 1, h, UH)
                for half in range(2):
                    for j in range(2):
                        act.wait_ge(z_ready, ZRH * h + (ZR0["qk"[half] + "1"] + j + 1))
                        hi(qk_hi[:, 2 * half + j, :], j)
                    if half == 0:
                        refill("qk1", 2, h, UH)
                        std(h + ST["h0"], DV)
                        refill("qk1", 3, h, UH)
                refill("v1", 0, h, UH)
                refill("v1", 1, h, UH)
                for j in range(4):
                    act.wait_ge(z_ready, ZRH * h + (ZR0["y0"] + j + 1))
                    hi(f_hi[:, j, :], j % 2)
                v_and_scores(h, 1, 2)
                for s in range(SLOTS):
                    refill("ro0", s, h, UH)
            h = HEADS - 1
            copy_result(h)
            gate_silu(f"g{h}", 0)
            head_squares(h)
            gate_silu(f"g{h}", 1)
            gate_silu(f"g{h}", 2)
            std(ST[f"h{h}"], DV)
            gate_silu(f"g{h}", 3)
            for j in range(4):
                act.wait_ge(z_ready, ZR0[f"y{h}"] + j + 1)
                hi(f_hi[:, j, :], j % 2)
            name = f"ro{HEADS - 1}"
            load_table(ACT.Sqrt)
            for j in range(DC):
                wait_left(act, name, j)
                square("n5", j, x[:, j, :])
                if j % 2:
                    refill(name, j // 2)
            std(ST["n5"], D)
            norm(5)
            ffn(1, None, "n6")
            std(ST["n6"], D)
            for c in range(DC):
                act.wait_ge(m_ready, DC * 6 + c + 1)
                act.activation(x[:, c, :], m_buf[:, c % 2, :], ACT.Identity,
                               bias=mod[:, SHIFT[6] + c:SHIFT[6] + c + 1]).then_inc(out_ready, 1)

        @block.vector
        def _(v):
            steps = {"mod": 0}

            def add_bias(a, n):
                v.wait_ge(mcol_copied, -(-(a + n) // 4))
                v.tensor_tensor(mod[:, a:a + n], mraw[:, a:a + n], vec[:, V_BIAS + a:V_BIAS + a + n],
                                ALU.add).then_inc(mod_step, 1)
                steps["mod"] += 1

            def prepare(n):
                add_bias(SHIFT[n], 2 * DC)
                v.wait_ge(mod_step, steps["mod"])
                v.scalar_tensor_tensor(aff[:], mod[:, SHIFT[n] + DC:SHIFT[n] + 2 * DC], 1.0,
                                       vec[:, V_GAIN + n * DC:V_GAIN + (n + 1) * DC], ALU.add,
                                       ALU.mult).then_inc(mod_step, 1)
                steps["mod"] += 1

            def gate(n, j):
                c = SHIFT[n] + 2 * DC + j
                return mod[:, c:c + 1]

            def add_square(stat, c, i=0, per=0, per_sq=0):
                v.wait_ge(sq_ready, per_sq * i + (SQ0[stat] + c + 1))
                if SS0[stat] + c:
                    v.wait_ge(sum_step, per * i + (SS0[stat] + c))
                if c == 0:
                    v.tensor_copy(ssum[:], sq[:]).then_inc(sum_step, 1)
                else:
                    v.tensor_tensor(ssum[:], ssum[:], sq[:], ALU.add).then_inc(sum_step, 1)

            def spread(stat):
                v.wait_ge(std_ready, stat + 1)
                v.reciprocal(rstd[:], stdev[:]).then_inc(rstd_ready, 1)
                v.wait_ge(rstd_ready, stat + 1)
                for j in range(4):
                    v.tensor_scalar(diag[:, j * P:(j + 1) * P], ident[:], rstd[:, j:j + 1], None,
                                    ALU.mult).then_inc(diag_ready, 1)

            def norm(n, stat, lo=True):
                if n == 0:
                    spread(stat)
                    prepare(n)
                else:
                    prepare(n)
                    spread(stat)
                v.wait_ge(mod_step, steps["mod"])
                v.wait_ge(bc_done, stat + 1)
                for c in range(DC + 1):
                    if c < DC:
                        if c >= 2:
                            v.wait_ge(hl_ready if lo else out_ready, (DC * n if lo else 0) + c - 1)
                        v.scalar_tensor_tensor(m_buf[:, c % 2, :], x[:, c, :], aff[:, c:c + 1], ps_bc[:],
                                               ALU.mult, ALU.mult).then_inc(m_ready, 1)
                    if c and lo:
                        v.wait_ge(hh_ready, DC * n + c)
                        v.scalar_tensor_tensor(h_lo[:, c - 1, :], m_buf[:, (c - 1) % 2, :],
                                               mod[:, SHIFT[n] + c - 1:SHIFT[n] + c],
                                               h_hi[:, c - 1, :].bitcast(F32), ALU.add,
                                               ALU.subtract).then_inc(hl_ready, 1)

            def sum_mods(g, i=0):
                steps0 = DC * (g - G_SUMS)
                v.wait_ge(mcol_done, i + g)
                for k in range(DC):
                    part = mods_ring[:, k // 2, (k % 2) * T:(k % 2 + 1) * T]
                    if k % 2 == 0:
                        v.wait_ge(mods_in[0][k // 2], 16 * i + (16 * place_count(g) + 16))
                    if k == 0:
                        v.tensor_scalar(mrow[:], part, c_2[:, 0:1], None, ALU.mult).then_inc(msum_step, 1)
                    else:
                        v.wait_ge(msum_step, DC * i + (steps0 + k))
                        v.scalar_tensor_tensor(mrow[:], part, c_2[:, k:k + 1], mrow[:], ALU.mult,
                                               ALU.add).then_inc(msum_step, 1)

            def z_free(z, i=0, per=0):
                if not isinstance(i, int) or per * i + z >= 2:
                    v.wait_ge(zl_ready, per * i + (z - 1))

            def lo(dst, hi, z, q, i=0, per=0):
                v.wait_ge(zh_ready, per * i + (z + 1))
                v.tensor_tensor(dst, z_buf[:, q, :], hi, ALU.subtract).then_inc(zl_ready, 1)

            def out(name, n, stat, per_unit=1, g=None):
                for j in range(DC):
                    if g is not None and j % SLOTS == 0:
                        sum_mods(g + j // SLOTS)
                    wait_unit(v, name, j // per_unit)
                    v.scalar_tensor_tensor(x[:, j, :], bank[j % SLOTS][:], gate(n, j), x[:, j, :],
                                           ALU.mult, ALU.add).then_inc(left[j % SLOTS], 1)
                    if stat is not None and j < DC - 1:
                        add_square(stat, j)

            for c in range(DC - 1):
                add_square("n0", c)
            norm(0, 0)
            done = 0
            for chunks in DVE_CHUNKS:
                first = POOL_TAPS if chunks == (6, 7) else 0
                pieces = [(c, 0, T) for c in chunks] if len(chunks) > 1 else [(chunks[0], a, T // 2) for a in (0, T // 2)]
                v.wait_ge(y_ready, chunks[-1] + 1)
                for c, a, n in pieces:
                    at_y, weight = c * ROW + a + first, V_DW + DC * first + c
                    v.tensor_scalar(cv_acc[:, c, a:a + n], cv_y[:, at_y:at_y + n], vec[:, weight:weight + 1],
                                    vec[:, V_DB + c:V_DB + c + 1],
                                    ALU.mult, ALU.add).then_inc(tap_done, 1)
                with v.Fori(first + 1, TAPS) as k:
                    for q, (c, a, n) in enumerate(pieces):
                        v.wait_ge(tap_done, len(pieces) * k + (done + q + 1 - len(pieces) * (first + 1)))
                        v.scalar_tensor_tensor(cv_acc[:, c, a:a + n], cv_y[:, bass.ds(k + (c * ROW + a), n)],
                                               vec[:, bass.ds(DC * k + (V_DW + c), 1)], cv_acc[:, c, a:a + n],
                                               ALU.mult, ALU.add).then_inc(tap_done, 1)
                done += len(pieces) * (TAPS - first)
            for q, c in enumerate(DVE_CHUNKS[-1]):
                v.wait_ge(tap_done, done + q - 1)
                v.wait_ge(pool_tap, TAPS + (q + 1) * POOL_TAPS)
                v.tensor_tensor(cv_acc[:, c, :], cv_acc[:, c, :], cv_y[:, q * ROW:q * ROW + T], ALU.add).then_inc(tap_done, 1)
            add_bias(SHIFT[0] + 2 * DC, DC)
            v.wait_ge(mean_done, 1)
            for c in range(DC + 1):
                if c < DC:
                    v.scalar_tensor_tensor(cv_acc[:, c, :], ps_bc[:], -1.0 / D, cv_acc[:, c, :],
                                           ALU.mult, ALU.add).then_inc(centered, 1)
                if c >= 2 and c % 2 == 0:
                    v.wait_ge(sq_ready, SQ0["cv"] + c)
                    if c > 2:
                        v.wait_ge(sq_used, c // 2 - 1)
                    v.tensor_tensor(diag[:], sq[:], ssum[:], ALU.add).then_inc(pair_sum, 1)
            spread(ST["cv"])
            v.wait_ge(bc_done, ST["cv"] + 1)
            for c in range(DC + 2):
                if c < DC:
                    v.tensor_tensor(cv_acc[:, c, :], cv_acc[:, c, :], ps_bc[:], ALU.mult).then_inc(scaled, 1)
                if 1 <= c <= DC:
                    n = c - 1
                    v.wait_ge(ln_silu, n + 1)
                    z_free(Z0["cv"] + n)
                    v.tensor_tensor(z_buf[:, n % 2, :], cv_acc[:, n, :], cv_g[:, n, :], ALU.mult).then_inc(z_ready, 1)
                if c >= 2:
                    n = c - 2
                    lo(f_lo[:, n, :], f_hi[:, n, :].bitcast(F32), Z0["cv"] + n, n % 2)
            v.wait_ge(mod_step, steps["mod"])
            g = G_SUMS
            out("cv_out", 0, "n1", g=g)
            g += 2
            norm(1, ST["n1"])

            v.memset(pl_v[:], 0.0).then_inc(win_step, 1)
            ws = 1
            add_bias(SHIFT[1] + 2 * DC, DC)
            v.wait_ge(cnt_in, 16)
            for j in range(DC):
                if j % SLOTS == 0:
                    sum_mods(g)
                    g += 1
                w = WINDOWS[j // 2]
                wait_left(v, "pl_v", j)
                src, span, length = pl_v[:, j % 2, :], 1, T + 2 * PAD
                while span < w:
                    length -= span
                    dst = pl_s[:, span.bit_length() % 2, :]
                    v.tensor_tensor(dst[:, 0:length], src[:, 0:length], src[:, span:span + length],
                                    ALU.add).then_inc(win_step, 1)
                    ws += 1
                    v.wait_ge(win_step, ws)
                    src, span = dst, 2 * span
                first = PAD - w // 2
                z_free(Z0["pv"] + j)
                v.tensor_tensor(z_buf[:, j % 2, :], src[:, first:first + T], pl_cnt[:, j // 2, :],
                                ALU.mult).then_inc(win_step, 1)
                ws += 1
                v.wait_ge(win_step, ws)
                v.tensor_tensor(z_buf[:, j % 2, :], z_buf[:, j % 2, :], pl_v[:, j % 2, PAD:PAD + T],
                                ALU.subtract).then_inc(z_ready, 1)
                lo(f_lo[:, j, :], f_hi[:, j, :].bitcast(F32), Z0["pv"] + j, j % 2)
            sum_mods(g)
            sum_mods(g + 1)
            g += 2
            for j in range(DC + 1):
                if j < DC:
                    wait_unit(v, "pl_grp", j // 2)
                    wait_left(v, "pl_g", j)
                    z_free(Z0["pg"] + j)
                    v.scalar_tensor_tensor(z_buf[:, j % 2, :], bank[j % SLOTS][:], vec[:, V_POOL + j:V_POOL + j + 1],
                                           pl_g[:, j, :], ALU.mult, ALU.mult).then_inc(left[j % SLOTS], 1)
                if j:
                    n = j - 1
                    lo(h_lo[:, n, :], h_hi[:, n, :].bitcast(F32), Z0["pg"] + n, n % 2)
            v.wait_ge(mod_step, steps["mod"])
            out("pl_out", 1, "n2", g=g)
            g += 2
            v.wait_ge(fr_const, 1)
            v.tensor_tensor(fr_lo[:], fr_raw, fr_hi[:].bitcast(F32), ALU.subtract).then_inc(fr_const_lo, 1)
            norm(2, ST["n2"])

            add_bias(SHIFT[2] + 2 * DC, DC)
            for n in range(8):
                part = slice((n // 4) * T, (n // 4 + 1) * T)
                v.wait_ge(ab_ready, n + 1)
                v.tensor_tensor(ab_lo[:, n % 4, part], bank[n % SLOTS][:], ab_hi[:, n % 4, part].bitcast(F32),
                                ALU.subtract).then_inc(left[n % SLOTS], 1)
            for k in range(GROUPS):
                if k < GROUPS - 1:
                    v.wait_ge(tile_done, 8 + 3 * k + 3)
                else:
                    wait_unit(v, "fr_2", 3)
                wait_left(v, "fr_2", 3 * k)
                bn, bv = (3 * k + 1) % SLOTS, (3 * k + 2) % SLOTS
                z_free(Z0["fr"] + 2 * k)
                v.scalar_tensor_tensor(z_buf[:, 0, :], bank[bv][:], sign[:, 0:1], s_buf[:, 0, :], ALU.mult,
                                       ALU.add).then_inc(z_ready, 1)
                z_free(Z0["fr"] + 2 * k + 1)
                v.scalar_tensor_tensor(z_buf[:, 1, :], bank[bv][:], sign[:, 1:2], s_buf[:, 0, :], ALU.mult,
                                       ALU.add).then_inc(left[bv], 1)
                wait_left(v, "fr_2", 3 * k + 2)
                v.tensor_copy(z_buf[0:1, 1, :], bank[bn][0:1, :]).then_inc(left[bn], 1)
                for q in range(2):
                    lo(f_lo[:, 2 * k + q, :], f_hi[:, 2 * k + q, :].bitcast(F32), Z0["fr"] + 2 * k + q, q)
                if k == 0:
                    sum_mods(g)
                    g += 1
            v.wait_ge(mod_step, steps["mod"])
            out("fr_out", 2, "n3", g=g)
            g += 2
            norm(3, ST["n3"])

            def ffn(layer, n, stat, g=None):
                for p, chunks in enumerate(PARTS):
                    name, z0 = f"in{layer}{p}", Z0[f"f{layer}{p}"]
                    with v.Fori(0, chunks // 2) as i:
                        if g is not None:
                            sum_mods(g, i)
                        for q in range(2):
                            wait_unit(v, name, 2 * q + 1, i)
                            wait_left(v, name, 2 * q, i)
                            z_free(z0 + q, i, 2)
                            v.tensor_tensor(z_buf[:, q, :], bank[2 * q + 1][:], s_buf[:, q, :],
                                            ALU.mult).then_inc(left[2 * q + 1], 1)
                            lo(at(f_lo, 2 * i + q), at(f_hi, 2 * i + q).bitcast(F32), z0 + q, q, i, 2)
                    if g is not None:
                        g += chunks // 2
                    if p == 0:
                        add_bias(SHIFT[n] + 2 * DC, DC)
                        v.wait_ge(mod_step, steps["mod"])
                    out(f"out{layer}{p}", n, stat if p == len(PARTS) - 1 else None, g=g)
                    if g is not None:
                        g += 2

            ffn(0, 3, "n4", g)
            norm(4, ST["n4"])
            add_bias(SHIFT[4] + 2 * DC, DC)

            SSH = SS0["h1"] - SS0["h0"]
            def rotary(half, h, n):
                b0, b1 = bank[2 * half], bank[2 * half + 1]
                z0 = Z0["qk0"] + 2 * half if n == 0 else Z0["qk"[half] + "1"]
                zr = ZR0["qk0"] + 2 * half if n == 0 else ZR0["qk"[half] + "1"]
                steps0 = 2 * half + 4 * n
                wait_unit(v, f"qk{n}", 2 * half + 1, h, UH)
                wait_left_own = lambda b: v.wait_ge(left[b], (RH // SLOTS) * h + (R0[f"qk{n}"] // SLOTS + 1))
                if not (n == 0 and half == 0):
                    v.wait_ge(z_ready, ZRH * h + zr_before(n, half))
                v.tensor_tensor(m_buf[:, 0, :], b0[:], rot[:, 0, :], ALU.mult).then_inc(rot_step, 1)
                v.tensor_tensor(m_buf[:, 1, :], b1[:], rot[:, 1, :], ALU.mult).then_inc(rot_step, 1)
                v.wait_ge(rot_step, 4 * h + (steps0 + 2))
                z_free(z0, h, ZH)
                v.tensor_tensor(z_buf[:, 0, :], m_buf[:, 0, :], m_buf[:, 1, :], ALU.subtract).then_inc(z_ready, 1)
                v.wait_ge(z_ready, ZRH * h + (zr + 1))
                v.tensor_tensor(m_buf[:, 0, :], b0[:], rot[:, 1, :], ALU.mult).then_inc(left[2 * half], 1)
                v.tensor_tensor(m_buf[:, 1, :], b1[:], rot[:, 0, :], ALU.mult).then_inc(left[2 * half + 1], 1)
                wait_left_own(2 * half)
                wait_left_own(2 * half + 1)
                z_free(z0 + 1, h, ZH)
                v.tensor_tensor(z_buf[:, 1, :], m_buf[:, 0, :], m_buf[:, 1, :], ALU.add).then_inc(z_ready, 1)
                for q in range(2):
                    lo(qk_lo[:, 2 * half + q, :], qk_hi[:, 2 * half + q, :].bitcast(F32), z0 + q, q, h, ZH)

            def zr_before(n, half):
                if n == 0:
                    return ZR0["qk0"] + 2
                return ZR0["q1"] if half == 0 else ZR0["k1"]

            def head_rest(h, n):
                for j in range(4):
                    v.wait_ge(vh_ready, 4 * h + (4 * n + j + 1))
                    v.tensor_tensor(v_lo[:, j, :], bank[j][:], v_hi[:, j, :].bitcast(F32),
                                    ALU.subtract).then_inc(left[j], 1)
                v.wait_ge(mask_in, 16 * h + 16 * (n + 1))
                for j in range(5):
                    if j < 4:
                        v.wait_ge(tile_done, 8 * h + (TD_HEAD + 8 * n + j + 1))
                        z_free(Z0[f"p{n}"] + j, h, ZH)
                        v.tensor_tensor(z_buf[:, j % 2, :], bank[j][:], mask[:, (3 - j) * P:(3 - j) * P + T],
                                        ALU.mult).then_inc(left[j], 1)
                    if j:
                        m = j - 1
                        lo(f_lo[:, 4 + m, :], f_hi[:, 4 + m, :].bitcast(F32), Z0[f"p{n}"] + m, m % 2, h, ZH)
                if n:
                    for j in range(DC):
                        wait_unit(v, f"ro{n - 1}", j // 2, h, UH)
                        v.scalar_tensor_tensor(x[:, j, :], bank[j % SLOTS][:], gate(4, j), x[:, j, :],
                                               ALU.mult, ALU.add).then_inc(left[j % SLOTS], 1)

            def head_sum(h):
                ss = SS0["h0m"]
                for j in range(4):
                    wait_left(v, f"av{h}", j) if isinstance(h, int) else wait_left(v, "av0", j, h, RH)
                v.wait_ge(sum_step, SSH * h + ss)
                v.tensor_tensor(ssum[:], yh[:, 0, :], yh[:, 1, :], ALU.add).then_inc(sum_step, 1)
                for j in (2, 3):
                    v.wait_ge(sum_step, SSH * h + (ss + j - 1))
                    v.tensor_tensor(ssum[:], ssum[:], yh[:, j, :], ALU.add).then_inc(sum_step, 1)

            def head_center(h):
                v.wait_ge(mean_done, h + 2)
                for j in range(4):
                    v.scalar_tensor_tensor(yh[:, j, :], ps_bc[:], -1.0 / DV, yh[:, j, :],
                                           ALU.mult, ALU.add).then_inc(centered, 1)
                for j in range(3):
                    add_square("h0", j, h, SSH, 4)

            def head_result(h, i, z0):
                for j in range(4):
                    if isinstance(h, int):
                        wait_left(v, f"g{h}", j)
                    v.tensor_tensor(yh[:, j, :], yh[:, j, :], sg[:, j, :], ALU.mult).then_inc(scaled, 1)
                v.wait_ge(bc_done, h + (ST["h0"] + 1))
                for j in range(5):
                    if j < 4:
                        v.wait_ge(scaled, 4 * h + (DC + j + 1))
                        z_free(z0 + j, i, ZH)
                        v.tensor_tensor(z_buf[:, j % 2, :], yh[:, j, :], ps_bc[:], ALU.mult).then_inc(z_ready, 1)
                    if j:
                        m = j - 1
                        lo(f_lo[:, m, :], f_hi[:, m, :].bitcast(F32), z0 + m, m % 2, i, ZH)

            v.wait_ge(rot_in, 16)
            rotary(0, 0, 0)
            rotary(1, 0, 0)
            v.wait_ge(mod_step, steps["mod"])
            head_rest(0, 0)
            with v.Fori(0, HEADS - 1) as h:
                head_sum(h)
                head_center(h)
                rotary(0, h, 1)
                spread(h + ST["h0"])
                rotary(1, h, 1)
                head_result(h, h, Z0["y0"])
                head_rest(h, 1)
            h = HEADS - 1
            head_sum(h)
            head_center(h)
            spread(h + ST["h0"])
            head_result(h, 0, Z0[f"y{h}"])
            out(f"ro{h}", 4, "n5", per_unit=2)
            norm(5, ST["n5"])
            ffn(1, 5, "n6")
            norm(6, ST["n6"], lo=False)

        @block.tensor
        def _(pe):
            def three(out, w_h, w_l, m_h, m_l, start, stop):
                pe.matmul(out, w_h, m_h, start=start, stop=False)
                pe.matmul(out, w_h, m_l, start=False, stop=False)
                return pe.matmul(out, w_l, m_h, start=False, stop=stop)

            def bank_ready(name, n, i=0, per=SLOTS):
                before = (R0[name] + n) // SLOTS
                if not isinstance(i, int) or before:
                    pe.wait_ge(left[n % SLOTS], (per // SLOTS) * i + before)

            def unit_ready(name, n, i=0, per=SLOTS):
                pe.wait_ge(lo_done, per * i + (U0[name] + n + 1))

            def tile(s, k, a_hi, a_lo, chunks, offset=0):
                w = slice((offset + k) * P, (offset + k + 1) * P)
                return three(bank[s][:], w_hi[:, s, w], w_lo[:, s, w], a_hi[:, k, :], a_lo[:, k, :],
                             k == 0, k == chunks - 1)

            def four_tiles(name, first, a_hi, a_lo, chunks=DC, i=0, ready=None, together=SLOTS):
                done = chunks // 2 if ready else 0
                for s0 in range(0, SLOTS, together):
                    for k in range(done):
                        ready(k)
                        for s in range(s0, s0 + together):
                            if k == 0:
                                unit_ready(name, first + s, i)
                                bank_ready(name, first + s, i)
                            tile(s, k, a_hi, a_lo, chunks)
                for s in range(SLOTS):
                    if not ready:
                        unit_ready(name, first + s, i)
                        bank_ready(name, first + s, i)
                    for k in range(done, chunks):
                        if ready and s == 0:
                            ready(k)
                        last = tile(s, k, a_hi, a_lo, chunks)
                    last.then_inc(unit_used, 1)

            def h_part(n):
                return lambda k: pe.wait_ge(hl_ready, DC * n + k + 1)

            def z_part(name):
                return lambda k: pe.wait_ge(zl_ready, Z0[name] + k + 1)

            def mrow_sums(g, i=0, per=1):
                for s in range(SLOTS):
                    pe.wait_ge(mods_in[g in SECOND][s], 16 * i + (16 * place_count(g) + 16))
                if g:
                    pe.wait_ge(mrow_copied, per * i + g)
                for r in range(2):
                    for q in range(4):
                        k = 4 * r + q
                        last = pe.matmul(ps_mrow[32 * q:32 * q + 32, :], c_pad[:, k, :],
                                         mods_place(g)[:, k // 2, (k % 2) * T:(k % 2 + 1) * T],
                                         start=r == 0, stop=r == 1, tile_position=(0, 32 * q))
                last.then_inc(mrow_done, 1)

            def mcol(g, i=0, per=1):
                if g < G_SUMS:
                    pe.wait_ge(mrow_copied, per * i + (g + 1))
                else:
                    pe.wait_ge(msum_step, DC * per * i + DC * (g + 1 - G_SUMS))
                if g:
                    pe.wait_ge(mcol_copied, per * i + g)
                for j in range(4):
                    last = pe.matmul(ps_mcol[:, j:j + 1], mrow[:, j * P:(j + 1) * P], ones[:, 0:1],
                                     start=True, stop=True)
                last.then_inc(mcol_done, 1)

            def mods(g, i=0, per=1):
                mcol(g - 1, i, per)
                mrow_sums(g, i, per)

            def keep_busy(n):
                for _ in range(n):
                    pe.matmul(ps_mrow[:], ones[:], vec[:, 0:T], start=True, stop=True)

            def columns(src, start, stop):
                for j in range(4):
                    last = pe.matmul(ps_stat[:, j:j + 1], src[:, j * P:(j + 1) * P], ones[:, 0:1],
                                     start=start and j == 0, stop=stop and j == 3)
                return last

            def stat(name, i=0, per=0, per_sq=0):
                n = 4 if name[0] == "h" else DC
                pe.wait_ge(sum_step, per * i + (SS0[name] + n - 1))
                columns(ssum, True, False)
                pe.wait_ge(sq_ready, per_sq * i + (SQ0[name] + n))
                columns(sq, False, True).then_inc(stat_done, 1)
                if name[0] == "n" and name != "n0":
                    keep_busy(BUSY["std"])

            def spread(s):
                for j in range(4):
                    pe.wait_ge(diag_ready, 4 * s + (j + 1))
                    last = pe.matmul(ps_bc[:, j * P:(j + 1) * P], ones[:], diag[:, j * P:(j + 1) * P],
                                     start=True, stop=True)
                last.then_inc(bc_done, 1)

            def mean(n):
                pe.wait_ge(sum_step, n)
                pe.matmul(ps_bc[:], ones[:], ssum[:], start=True, stop=True).then_inc(mean_done, 1)

            def out(name, a_hi, a_lo, ready, g, together=SLOTS):
                four_tiles(name, 0, a_hi, a_lo, ready=ready, together=together)
                mcol(g)
                four_tiles(name, SLOTS, a_hi, a_lo)
                mcol(g + 1)

            pe.wait_ge(c_ready, 1)
            pe.wait_ge(const_ready, 1)
            mrow_sums(0)
            for g in range(1, G_START):
                mods(g)
                if g == 2:
                    stat("n0")
            spread(ST["n0"])
            mcol(G_START - 1)
            keep_busy(BUSY["first norm"])

            g = G_START
            four_tiles("cv_ab", 0, h_hi, h_lo, ready=h_part(0), together=2)
            mrow_sums(g)
            with pe.Fori(1, 4) as i:
                four_tiles("cv_ab", 0, h_hi, h_lo, i=i)
                mods(g + 1, i - 1)
            g += G_AB
            for b in range(2):
                four_tiles("cv_g", SLOTS * b, h_hi, h_lo)
                mods(g)
                g += 1
            assert g + G_WAIT == MOD_1
            mods(g)
            mods(g + 1)
            g += G_WAIT
            mcol(g - 1)
            pe.wait_ge(tap_done, 6 * TAPS)
            for c in (0, 2, 3, 4, 5, 1, 6, 7):
                if c == 1:
                    pe.wait_ge(pool_tap, TAPS)
                if c == 6:
                    keep_busy(BUSY["conv"])
                if c >= 6:
                    pe.wait_ge(tap_done, 6 * TAPS + 2 * (TAPS - POOL_TAPS) + c - 5)
                last = pe.matmul(ps_bc[:], ones[:], cv_acc[:, c, :], start=c == 0, stop=c == DC - 1)
            last.then_inc(mean_done, 1)
            keep_busy(BUSY["squares"])
            for c in range(DC // 2):
                pe.wait_ge(pair_sum, c + 1)
                columns(diag, c == 0, c == DC // 2 - 1).then_inc(stat_done if c == DC // 2 - 1 else sq_used, 1)
                keep_busy(1)
            spread(ST["cv"])
            keep_busy(BUSY["layer norm"])
            out("cv_out", f_hi, f_lo, z_part("cv"), g)
            g += 2
            stat("n1")
            spread(ST["n1"])
            keep_busy(BUSY["norm"])

            for name in ("pl_v", "pl_g"):
                for b in range(2):
                    four_tiles(name, SLOTS * b, h_hi, h_lo, ready=h_part(1) if (name, b) == ("pl_v", 0) else None)
                    mcol(g)
                    g += 1
            for k in range(GROUPS):
                unit_ready("pl_grp", k)
                for d in range(2):
                    bank_ready("pl_grp", 2 * k + d)
                    for c in range(2):
                        w = slice(c * GD + d * P, c * GD + (d + 1) * P)
                        pe.wait_ge(zl_ready, Z0["pv"] + 2 * k + c + 1)
                        last = three(bank[(2 * k + d) % SLOTS][:], w_hi[:, k, w], w_lo[:, k, w],
                                     f_hi[:, 2 * k + c, :], f_lo[:, 2 * k + c, :], c == 0, c == 1)
                last.then_inc(unit_used, 1)
            out("pl_out", h_hi, h_lo, z_part("pg"), g, together=2)
            g += 2
            stat("n2")
            spread(ST["n2"])
            keep_busy(BUSY["norm"])

            pe.wait_ge(fr_const_lo, 1)
            for k in range(DC):
                pe.wait_ge(hl_ready, DC * 2 + k + 1)
                gg, c = k % 4 // 2, k % 2
                for tok in range(4):
                    if k % 4 == 0:
                        bank_ready("fr_1", k + tok)
                    cols = slice(tok * P, (tok + 1) * P)
                    last = three(bank[tok][:, gg * GD:(gg + 1) * GD], h_hi[:, k, cols], h_lo[:, k, cols],
                                 fr_hi[:, c, :], fr_lo[:, c, :], c == 0, c == 1)
                    if k % 4 == 3:
                        last.then_inc(tile_done, 1)
            for s in range(SLOTS):
                unit_ready("fr_2", s)
            for b in range(SLOTS):
                wait_left(pe, "fr_1", SLOTS + b)
            for k in range(GROUPS):
                if k == GROUPS - 1:
                    mcol(g)
                    g += 1
                for part in range(3):
                    n = 3 * k + part
                    bank_ready("fr_2", n)
                    rows = bank[n % SLOTS][0:1, :] if part == 1 else bank[n % SLOTS][:]
                    c = k * GD + (0, P, P)[part]
                    cols = slice(c, c + 1) if part == 1 else slice(c, c + P)
                    for s in range(4):
                        slot, at_ = (2 if part == 2 else 0) + s // 2, slice((s % 2) * T, (s % 2 + 1) * T)
                        last = three(rows, ab_hi[:, s, cols], ab_lo[:, s, cols], w_hi[:, slot, at_],
                                     w_lo[:, slot, at_], s == 0, s == 3)
                    if k == GROUPS - 1 and part:
                        last.then_inc(unit_used, 2)
                    else:
                        last.then_inc(tile_done, 1)
            out("fr_out", f_hi, f_lo, z_part("fr"), g, together=2)
            g += 2
            stat("n3")
            spread(ST["n3"])
            keep_busy(BUSY["norm"])

            def ffn(layer, n, g):
                for p, chunks in enumerate(PARTS):
                    name = f"in{layer}{p}"
                    with_mods = layer == 0
                    if p == 0:
                        four_tiles(name, 0, h_hi, h_lo, ready=h_part(n))
                        if with_mods:
                            mcol(g)
                    with pe.Fori(1 if p == 0 else 0, chunks // 2) as i:
                        four_tiles(name, 0, h_hi, h_lo, i=i)
                        if with_mods:
                            mcol(g, i)
                    if with_mods:
                        g += chunks // 2
                    four_tiles(f"out{layer}{p}", 0, f_hi, f_lo, chunks, ready=z_part(f"f{layer}{p}"),
                               together=2)
                    if with_mods:
                        mcol(g)
                    four_tiles(f"out{layer}{p}", SLOTS, f_hi, f_lo, chunks)
                    if with_mods:
                        mcol(g + 1)
                        g += 2
                return g

            ffn(0, 3, g)
            stat("n4")
            spread(ST["n4"])
            keep_busy(BUSY["norm"])

            SSH = SS0["h1"] - SS0["h0"]

            def qk_units(h, units):
                for s in units:
                    unit_ready("qk1", s, h, UH)
                    bank_ready("qk1", s, h, RH)
                    for k in range(DC):
                        last = tile(s, k, h_hi, h_lo, DC)
                    last.then_inc(unit_used, 1)

            def v_units(h, n, units):
                for u in units:
                    unit_ready(f"v{n}", u, h, UH)
                    for tok in range(4):
                        if u == 0:
                            bank_ready(f"v{n}", tok, h, RH)
                        for kk in range(2):
                            k, cols = 2 * u + kk, slice(tok * P, (tok + 1) * P)
                            last = three(bank[tok][:], h_hi[:, k, cols], h_lo[:, k, cols],
                                         w_hi[:, u, kk * DV:(kk + 1) * DV], w_lo[:, u, kk * DV:(kk + 1) * DV],
                                         k == 0, k == DC - 1)
                        if u == SLOTS - 1 and tok < 3:
                            last.then_inc(v_done, 1)
                    last.then_inc(unit_used, 1)

            def scores(h, n):
                z = Z0["qk0"] + 4 if n == 0 else Z0["k1"] + 2
                pe.wait_ge(zl_ready, ZH * h + z)
                for j in range(4):
                    bank_ready(f"sc{n}", j, h, RH)
                    cols = slice(j * P, (j + 1) * P)
                    for c in range(2):
                        last = three(bank[j][:], qk_hi[:, 2 + c, cols], qk_lo[:, 2 + c, cols],
                                     qk_hi[:, c, :], qk_lo[:, c, :], c == 0, c == 1)
                    last.then_inc(tile_done, 1)

            def project(h, n):
                def share(u, d, k):
                    w = slice((4 * d + k) * P, (4 * d + k + 1) * P)
                    return three(bank[(2 * u + d) % SLOTS][:], w_hi[:, u, w], w_lo[:, u, w], f_hi[:, k, :],
                                 f_lo[:, k, :], k == 0, k == 3)

                z = Z0["y0"] if n == 0 else Z0[f"y{n}"]
                for k in range(4):
                    pe.wait_ge(zl_ready, ZH * h + (z + k + 1))
                    for u in range(2):
                        if k == 0:
                            unit_ready(f"ro{n}", u, h, UH)
                        for d in range(2):
                            if k == 0:
                                bank_ready(f"ro{n}", 2 * u + d, h, RH)
                            last = share(u, d, k)
                        if k == 3:
                            last.then_inc(unit_used, 1)
                for u in range(2, SLOTS):
                    unit_ready(f"ro{n}", u, h, UH)
                    for d in range(2):
                        bank_ready(f"ro{n}", 2 * u + d, h, RH)
                        for k in range(4):
                            last = share(u, d, k)
                    last.then_inc(unit_used, 1)

            def gate(h, n, units=range(SLOTS)):
                for s in units:
                    unit_ready(f"g{n}", s, h, UH)
                    bank_ready(f"g{n}", s, h, RH)
                    for k in range(DC):
                        last = tile(s, k, h_hi, h_lo, DC)
                    last.then_inc(unit_used, 1)

            def result(h, n):
                pe.wait_ge(zl_ready, ZH * h + (Z0[f"p{n}"] + 4))
                for j in range(4):
                    bank_ready(f"av{n}", j, h, RH)
                    cols = slice(j * P, (j + 1) * P)
                    for s in range(4):
                        last = three(bank[j][:], v_hi[:, s, cols], v_lo[:, s, cols], f_hi[:, 4 + s, :],
                                     f_lo[:, 4 + s, :], s == 0, s == 3)
                    last.then_inc(tile_done, 1)

            four_tiles("qk0", 0, h_hi, h_lo, ready=h_part(4))
            v_units(0, 0, range(4))
            scores(0, 0)
            with pe.Fori(0, HEADS - 1) as h:
                gate(h, 0)
                result(h, 0)
                qk_units(h, (0,))
                mean(SSH * h + (SS0["h0m"] + 3))
                qk_units(h, (1, 2))
                stat("h0", h, SSH, 4)
                qk_units(h, (3,))
                spread(h + ST["h0"])
                v_units(h, 1, range(SLOTS))
                scores(h, 1)
                project(h, 0)
            h = HEADS - 1
            result(0, h)
            gate(0, h, (0,))
            mean(SS0[f"h{h}m"] + 3)
            gate(0, h, (1, 2))
            stat(f"h{h}")
            gate(0, h, (3,))
            spread(ST[f"h{h}"])
            project(0, h)
            stat("n5")
            spread(ST["n5"])
            keep_busy(BUSY["norm"])
            ffn(1, 5, None)
            stat("n6")
            spread(ST["n6"])


TD_HEAD = 8 + 3 * GROUPS - 2


def tiles_of(w):
    k, n = w.shape
    return w.reshape(k // P, P, n // P, P).transpose(2, 1, 0, 3).reshape(n // P, P, k)


def columns(v):
    return v.reshape(-1, P).T


def layout(a):
    out = {}
    out["x_t"] = a["x"][0].T.reshape(DC, P, T).transpose(1, 0, 2)
    gains = [a["norm_g"][0], a["norm_g"][1], a["norm_mix_g_2"][0], a["norm_ffn_g_2"][0],
             a["norm_mix_g_2"][1], a["norm_ffn_g_2"][1], a["final_norm_g_2"]]
    biases = [a["b_mod"].reshape(-1), a["b_ada_2"].reshape(-1), a["b_ada_final_2"]]
    out["vectors"] = np.concatenate(
        [columns(v) for v in [a["c"][0], a["c_2"][0], *biases, *gains, a["cv_dw"][0].reshape(-1), a["cv_db"][0],
                              a["cv_ln_g"][0], a["cv_ln_b"][0], a["pl_scale"][0]]], axis=1)
    mods = [w for w in (*a["w_mod"], *a["w_ada_2"], a["w_ada_final_2"])]
    out["w_mods"] = np.concatenate(
        [w.reshape(4, 2, P, -1, T).transpose(3, 0, 2, 1, 4).reshape(-1, P, 2 * T) for w in mods])
    cv = tiles_of(a["cv_w_in"][0])
    out["cv_ab"] = cv[:2 * DC].reshape(2, DC, P, D).transpose(1, 0, 2, 3).reshape(2 * DC, P, D)
    out["cv_g"] = cv[2 * DC:]
    out["cv_out"] = tiles_of(a["cv_w_out"][0])
    pl = tiles_of(a["pl_w_in"][0])
    out["pl_v"], out["pl_g"] = pl[:DC], pl[DC:]
    out["pl_grp"] = a["pl_w_grp"][0].reshape(GROUPS, 2, P, GD).transpose(0, 2, 1, 3).reshape(GROUPS, P, 2 * GD)
    out["pl_out"] = tiles_of(a["pl_w_out"][0])
    order = np.concatenate([np.r_[g * GD:g * GD + P, g * GD + P, g * GD + GD - 1:g * GD + P:-1]
                            for g in range(GROUPS)])
    out["fr_out"] = tiles_of(a["w_fourier_out_2"][0][order])
    for layer in range(2):
        gate_up = tiles_of(a["w_ffn_in_2"][layer])
        out[f"ff_in{layer}"] = gate_up.reshape(2, FC, P, D).transpose(1, 0, 2, 3).reshape(2 * FC, P, D)
        w = a["w_ffn_out_2"][layer]
        out[f"ff_out{layer}"] = np.concatenate([tiles_of(w[:8 * P]), tiles_of(w[8 * P:16 * P])])
        out[f"ff_tail{layer}"] = tiles_of(w[16 * P:])
    w_in, w_out = a["w_ret_in_2"][0], a["w_ret_out_2"][0]
    ret = []
    for h in range(HEADS):
        q, k = (tiles_of(w_in[:, o + h * DK:o + (h + 1) * DK]) for o in (0, HEADS * DK))
        v = w_in[:, 2 * HEADS * DK + h * DV:2 * HEADS * DK + (h + 1) * DV]
        v = v.reshape(4, 2, P, DV).transpose(0, 2, 1, 3).reshape(4, P, 2 * DV)
        g0 = 2 * HEADS * DK + HEADS * DV + h * DV
        o = tiles_of(w_out[h * DV:(h + 1) * DV])
        ret += [q, k, v, tiles_of(w_in[:, g0:g0 + DV]),
                o.reshape(4, 2, P, DV).transpose(0, 2, 1, 3).reshape(4, P, 2 * DV)]
    out["ret"] = np.concatenate(ret)
    return out


def tables():
    out = {}
    j, k = np.arange(GD)[:, None], np.arange(P)[None, :]
    angle = lambda a, b, n: 2 * np.pi * ((a * b) % n) / n
    ortho = 1.0 / np.sqrt(T * GD)
    feature = np.concatenate([np.cos(angle(j, k, GD)), np.cos(angle(j, P, GD)), np.sin(angle(j, k[:, 1:], GD))], 1)
    out["dft_feature"] = (feature * ortho).reshape(2, P, GD).transpose(1, 0, 2)
    s, tt = np.arange(T)[:, None], np.arange(T)[None, :]
    both = np.concatenate([np.cos(angle(s, tt, T)), np.sin(angle(s, tt, T))])
    out["dft_token"] = both.reshape(4, 2, P, T).transpose(0, 2, 1, 3).reshape(4, P, 2 * T)
    pos = np.arange(T)
    out["pl_cnt"] = np.broadcast_to(
        np.stack([1.0 / (np.clip(pos + w - w // 2, 0, T) - np.clip(pos - w // 2, 0, T)) for w in WINDOWS]),
        (P, len(WINDOWS), T))
    half = DK // 2
    inv_freq = np.float32(10000.0) ** (-np.arange(half, dtype=np.float32) / np.float32(half))
    ang = (pos.astype(np.float32)[None, :] * inv_freq[:, None]).astype(np.float64)
    out["rotary"] = np.stack([np.cos(ang), np.sin(ang)], 1)
    log_f = np.log1p(-np.exp2(-5.0 - np.arange(HEADS)))
    d = np.arange(T + 3 * P)[None, :] - 3 * P - np.arange(P)[:, None]
    out["decay"] = np.stack([np.where(d >= 0, np.exp(np.maximum(d, 0) * log_f[h]),
                                      np.exp(np.maximum(-d, 0) * log_f[HEADS - 1 - h])) for h in range(HEADS)]) * DK ** -0.5
    return {n: np.ascontiguousarray(v, dtype=np.float32) for n, v in out.items()}


def kernel(**inputs):
    import concourse.bacc as bacc
    from concourse.bass_utils import run_bass_kernel_spmd

    arrays = {n: np.ascontiguousarray(v) for n, v in layout({k: np.asarray(v) for k, v in inputs.items()}).items()}
    arrays.update(tables())
    nc = bacc.Bacc("TRN2", target_bir_lowering=False, num_devices=1)
    t = {n: nc.dram_tensor(n + "_in", v.shape, F32, kind="ExternalInput").ap() for n, v in arrays.items()}
    t["y_t"] = nc.dram_tensor("y_t", (P, DC, T), F32, kind="ExternalOutput").ap()
    build_program(nc, t)
    y = run_bass_kernel_spmd(nc, [{n + "_in": v for n, v in arrays.items()}], core_ids=[0]).results[0]["y_t"]
    return np.ascontiguousarray(y.transpose(1, 0, 2).reshape(D, T).T[None])
```
